# Optimizing a Trainium2 kernel written in Bass

```python
import math
import jax, jax.numpy as jnp
from jax import lax
import numpy as np

D_MODEL = 2048
BATCH = 1
SEQ = 256
DEPTH = 1

EPS = 1e-6
HALF_STEP = 0.5
MIX_WIDTH = D_MODEL
A_WIDTH = MIX_WIDTH // 2
A_HEAD_DIM = 128
A_HEADS = A_WIDTH // A_HEAD_DIM
A_CHUNK = 128
B_WIDTH = MIX_WIDTH - A_WIDTH
B_HEAD_DIM = 64
B_HEADS = B_WIDTH // B_HEAD_DIM
B_GROUPS = 2
B_STATE = 128
B_CONV = 4
B_CHUNK = 256
B_CONV_DIM = B_WIDTH + 2 * B_GROUPS * B_STATE
DT_MIN = 0.001
DT_MAX = 0.1
IN_PROJ_DIM = 2 * A_WIDTH + B_WIDTH + B_CONV_DIM + B_HEADS
D_FF = 5504

kernel_name = 'hybrid_gmlp_ssd_macaron_block'

def rmsnorm(x, g):
    xf = x.astype(jnp.float32)
    y = xf * lax.rsqrt(jnp.mean(xf * xf, axis=-1, keepdims=True) + EPS)
    return (y * g.astype(jnp.float32)).astype(x.dtype)

def swiglu(h, w_gate, w_up, w_down):
    return (jax.nn.silu(h @ w_gate) * (h @ w_up)) @ w_down

def causal_depthwise_conv(x, w, b):
    c = x.shape[-1]
    y = lax.conv_general_dilated(x, w.astype(x.dtype)[:, None, :], window_strides=(1,), padding=[(B_CONV - 1, 0)],
                                 dimension_numbers=('NWC', 'WIO', 'NWC'), feature_group_count=c)
    return y + b

def chunked_spatial_gating(u, v, w_s, b_s):
    bsz, seq, _ = u.shape
    nc = seq // A_CHUNK
    mask = jnp.tril(jnp.ones((A_CHUNK, A_CHUNK), dtype=bool))
    w = jnp.where(mask, w_s, 0)
    vc = v.reshape(bsz, nc, A_CHUNK, A_HEADS, A_HEAD_DIM)
    mixed = jnp.einsum('hts,bcshd->bcthd', w, vc) + b_s.T[None, None, :, :, None]
    return u * mixed.reshape(bsz, seq, A_WIDTH)

def segsum_exp(a_cs):
    n = a_cs.shape[-1]
    mask = jnp.tril(jnp.ones((n, n), dtype=bool))
    diff = a_cs[..., :, None] - a_cs[..., None, :]
    return jnp.exp(jnp.where(mask, diff, -jnp.inf))

def pad_seq(t, pad):
    return jnp.pad(t, [(0, 0), (0, pad)] + [(0, 0)] * (t.ndim - 2))

def ssd_chunked(xh, dt, a, bm, cm):
    bsz, seq = xh.shape[:2]
    pad = (-seq) % B_CHUNK
    xh, dt, bm, cm = pad_seq(xh, pad), pad_seq(dt, pad), pad_seq(bm, pad), pad_seq(cm, pad)
    nc = (seq + pad) // B_CHUNK
    r = B_HEADS // B_GROUPS
    x = (xh * dt[..., None]).reshape(bsz, nc, B_CHUNK, B_GROUPS, r, B_HEAD_DIM)
    da = jnp.moveaxis((dt * a).reshape(bsz, nc, B_CHUNK, B_GROUPS, r), 2, -1)
    a_cs = jnp.cumsum(da, axis=-1)
    bc = bm.reshape(bsz, nc, B_CHUNK, B_GROUPS, B_STATE)
    cc = cm.reshape(bsz, nc, B_CHUNK, B_GROUPS, B_STATE)
    decay_in = segsum_exp(a_cs)
    cb = jnp.einsum('bclgn,bcsgn->bcgls', cc, bc)
    y_diag = jnp.einsum('bcgls,bcgrls,bcsgrp->bclgrp', cb, decay_in, x)
    decay_to_end = jnp.exp(a_cs[..., -1:] - a_cs)
    states = jnp.einsum('bclgn,bcgrl,bclgrp->bcgrpn', bc, decay_to_end, x)
    chunk_decay = jnp.exp(a_cs[..., -1])

    def step(carry, inp):
        st, dec = inp
        return carry * dec[..., None, None] + st, carry

    init = jnp.zeros_like(states[:, 0])
    _, prev = lax.scan(step, init, (jnp.moveaxis(states, 1, 0), jnp.moveaxis(chunk_decay, 1, 0)))
    prev = jnp.moveaxis(prev, 0, 1)
    y_off = jnp.einsum('bclgn,bcgrpn,bcgrl->bclgrp', cc, prev, jnp.exp(a_cs))
    y = (y_diag + y_off).reshape(bsz, nc * B_CHUNK, B_HEADS, B_HEAD_DIM)
    return y[:, :seq]

def mamba2_mixer(z, xbc, dt_raw, conv_w, conv_b, dt_bias, a_log, d_skip, ssm_norm):
    bsz, seq, _ = z.shape
    f32 = jnp.float32
    xbc = jax.nn.silu(causal_depthwise_conv(xbc, conv_w, conv_b))
    xs, bm, cm = jnp.split(xbc, [B_WIDTH, B_WIDTH + B_GROUPS * B_STATE], axis=-1)
    dt = jax.nn.softplus(dt_raw.astype(f32) + dt_bias.astype(f32))
    a = -jnp.exp(a_log.astype(f32))
    xh = xs.astype(f32).reshape(bsz, seq, B_HEADS, B_HEAD_DIM)
    y = ssd_chunked(xh, dt, a,
                    bm.astype(f32).reshape(bsz, seq, B_GROUPS, B_STATE),
                    cm.astype(f32).reshape(bsz, seq, B_GROUPS, B_STATE))
    y = y + d_skip.astype(f32)[:, None] * xh
    y = y.reshape(bsz, seq, B_WIDTH) * jax.nn.silu(z.astype(f32))
    yg = y.reshape(bsz, seq, B_GROUPS, B_WIDTH // B_GROUPS)
    yg = yg * lax.rsqrt(jnp.mean(yg * yg, axis=-1, keepdims=True) + EPS)
    return (yg.reshape(bsz, seq, B_WIDTH) * ssm_norm.astype(f32)).astype(z.dtype)

def hybrid_mixer(h, w_in, sgu_norm, w_spatial, b_spatial, conv_w, conv_b, dt_bias, a_log, d_skip, ssm_norm, w_out):
    proj = h @ w_in
    u, v, z, xbc, dt_raw = jnp.split(
        proj, [A_WIDTH, 2 * A_WIDTH, 2 * A_WIDTH + B_WIDTH, 2 * A_WIDTH + B_WIDTH + B_CONV_DIM], axis=-1)
    u = jax.nn.gelu(u, approximate=False)
    v = rmsnorm(jax.nn.gelu(v, approximate=False), sgu_norm)
    y_a = chunked_spatial_gating(u, v, w_spatial, b_spatial)
    y_b = mamba2_mixer(z, xbc, dt_raw, conv_w, conv_b, dt_bias, a_log, d_skip, ssm_norm)
    return jnp.concatenate([y_a, y_b.astype(y_a.dtype)], axis=-1) @ w_out

def setup_inputs(seed: int = 0) -> dict:
    key = jax.random.key(seed)
    ks = jax.random.split(key, 24)
    f32 = jnp.float32
    L = DEPTH

    def nrm(k, shape, scale):
        return jax.random.normal(k, shape, f32) * scale

    def gain(k, shape):
        return 1.0 + 0.05 * jax.random.normal(k, shape, f32)

    x = nrm(ks[0], (BATCH, SEQ, D_MODEL), 1.0)
    ffn1_norm_pre = gain(ks[1], (L, D_MODEL))
    ffn1_norm_post = gain(ks[2], (L, D_MODEL))
    ffn1_w_gate = nrm(ks[3], (L, D_MODEL, D_FF), D_MODEL ** -0.5)
    ffn1_w_up = nrm(ks[4], (L, D_MODEL, D_FF), D_MODEL ** -0.5)
    ffn1_w_down = nrm(ks[5], (L, D_FF, D_MODEL), D_FF ** -0.5)
    mix_norm_pre = gain(ks[6], (L, D_MODEL))
    mix_norm_post = gain(ks[7], (L, D_MODEL))
    w_in = nrm(ks[8], (L, D_MODEL, IN_PROJ_DIM), D_MODEL ** -0.5)
    sgu_norm = gain(ks[9], (L, A_WIDTH))
    w_spatial = nrm(ks[10], (L, A_HEADS, A_CHUNK, A_CHUNK), A_CHUNK ** -0.5)
    b_spatial = 1.0 + 0.1 * jax.random.normal(ks[11], (L, A_HEADS, A_CHUNK), f32)
    conv_w = nrm(ks[12], (L, B_CONV, B_CONV_DIM), B_CONV ** -0.5)
    conv_b = nrm(ks[13], (L, B_CONV_DIM), 0.02)
    dt0 = jnp.exp(jax.random.uniform(ks[14], (L, B_HEADS), f32, math.log(DT_MIN), math.log(DT_MAX)))
    dt_bias = dt0 + jnp.log(-jnp.expm1(-dt0))
    a_log = jnp.log(jax.random.uniform(ks[15], (L, B_HEADS), f32, 1.0, 16.0))
    d_skip = gain(ks[16], (L, B_HEADS))
    ssm_norm = gain(ks[17], (L, B_WIDTH))
    w_out = nrm(ks[18], (L, MIX_WIDTH, D_MODEL), MIX_WIDTH ** -0.5)
    ffn2_norm_pre = gain(ks[19], (L, D_MODEL))
    ffn2_norm_post = gain(ks[20], (L, D_MODEL))
    ffn2_w_gate = nrm(ks[21], (L, D_MODEL, D_FF), D_MODEL ** -0.5)
    ffn2_w_up = nrm(ks[22], (L, D_MODEL, D_FF), D_MODEL ** -0.5)
    ffn2_w_down = nrm(ks[23], (L, D_FF, D_MODEL), D_FF ** -0.5)
    return {'x': x,
            'ffn1_norm_pre': ffn1_norm_pre, 'ffn1_norm_post': ffn1_norm_post,
            'ffn1_w_gate': ffn1_w_gate, 'ffn1_w_up': ffn1_w_up, 'ffn1_w_down': ffn1_w_down,
            'mix_norm_pre': mix_norm_pre, 'mix_norm_post': mix_norm_post, 'w_in': w_in,
            'sgu_norm': sgu_norm, 'w_spatial': w_spatial, 'b_spatial': b_spatial,
            'conv_w': conv_w, 'conv_b': conv_b, 'dt_bias': dt_bias, 'a_log': a_log,
            'd_skip': d_skip, 'ssm_norm': ssm_norm, 'w_out': w_out,
            'ffn2_norm_pre': ffn2_norm_pre, 'ffn2_norm_post': ffn2_norm_post,
            'ffn2_w_gate': ffn2_w_gate, 'ffn2_w_up': ffn2_w_up, 'ffn2_w_down': ffn2_w_down}

def reference(x, ffn1_norm_pre, ffn1_norm_post, ffn1_w_gate, ffn1_w_up, ffn1_w_down,
              mix_norm_pre, mix_norm_post, w_in, sgu_norm, w_spatial, b_spatial,
              conv_w, conv_b, dt_bias, a_log, d_skip, ssm_norm, w_out,
              ffn2_norm_pre, ffn2_norm_post, ffn2_w_gate, ffn2_w_up, ffn2_w_down):
    for l in range(DEPTH):
        h = swiglu(rmsnorm(x, ffn1_norm_pre[l]), ffn1_w_gate[l], ffn1_w_up[l], ffn1_w_down[l])
        x = x + HALF_STEP * rmsnorm(h, ffn1_norm_post[l])
        h = hybrid_mixer(rmsnorm(x, mix_norm_pre[l]), w_in[l], sgu_norm[l], w_spatial[l], b_spatial[l],
                         conv_w[l], conv_b[l], dt_bias[l], a_log[l], d_skip[l], ssm_norm[l], w_out[l])
        x = x + rmsnorm(h, mix_norm_post[l])
        h = swiglu(rmsnorm(x, ffn2_norm_pre[l]), ffn2_w_gate[l], ffn2_w_up[l], ffn2_w_down[l])
        x = x + HALF_STEP * rmsnorm(h, ffn2_norm_post[l])
    return x


_drawn_inputs = setup_inputs


def setup_inputs(seed=0):
    import zlib

    import numpy as np

    out = dict(_drawn_inputs(seed))
    spreads = {}
    factors = {'sgu_norm': 4.548,
     'conv_b': 3.998,
     'd_skip': 8.747,
     'ffn2_norm_post': 3.632,
     'a_log': 24.584,
     'ssm_norm': 2.992,
     'b_spatial': 3.757}
    for name, (base, spread) in spreads.items():
        noise = np.random.default_rng([zlib.crc32(name.encode()), seed]).standard_normal(out[name].shape)
        drawn = base * np.exp(spread * noise) if base else spread * noise
        out[name] = __import__('jax').numpy.asarray(drawn.astype(out[name].dtype))
    for name, factor in factors.items():
        out[name] = (out[name] * factor).astype(out[name].dtype)
    return out
```

```python
import concourse.bass as bass
from concourse import mybir
from contextlib import ExitStack

F32 = mybir.dt.float32
F32R = mybir.dt.float32r
ACT = mybir.ActivationFunctionType
ALU = mybir.AluOpType

P = 128
EPS = 1e-6
RAW_SLOTS = 4
CHUNK = 16


def hybrid_block(nc, x_in, f1_pre, f1_post, f1_gate, f1_up, f1_down, mix_pre, mix_post, w_in,
                 sgu_norm, w_spatial, b_spatial, conv_w, conv_b, dt_bias, a_log, d_skip, ssm_norm,
                 w_out, f2_pre, f2_post, f2_gate, f2_up, f2_down, out):
    T, D = x_in.shape[1], x_in.shape[2]
    TT = T // P
    KD = D // P
    KF = f1_gate.shape[2] // P
    A_HEADS = w_spatial.shape[1]
    A_WIDTH = A_HEADS * P
    SSM_HEADS = dt_bias.shape[1]
    PAIRS = SSM_HEADS // 2
    B_WIDTH = PAIRS * P
    CONV_TILES = conv_b.shape[1] // P
    TAPS = conv_w.shape[1]
    PAD = TAPS - 1
    GROUPS = (CONV_TILES - PAIRS) // 2
    GROUP_PAIRS = PAIRS // GROUPS
    COL_U, COL_V, COL_Z = 0, A_WIDTH, 2 * A_WIDTH
    COL_CONV = COL_Z + B_WIDTH
    DT_ROW = P - SSM_HEADS
    COL_DT_WINDOW = w_in.shape[2] - P
    assert (T, D, TT, KD, A_HEADS, PAIRS, CONV_TILES, GROUPS) == (256, 2048, 2, 16, 8, 8, 12, 2)

    DOWN = [KF // 4 + (1 if c < KF % 4 else 0) for c in range(4)]
    DOWN_AT = [sum(DOWN[:c]) for c in range(4)]

    W_TILES = 1 + CONV_TILES + A_HEADS + PAIRS + A_HEADS
    n, t, first = 0, 0, {}
    for name, tiles, chunks in (("gate1", KF, 2 * KF), ("down1", KD, 4 * KD), ("proj", W_TILES, W_TILES),
                                ("wout", KD, KD), ("gate2", KF, 2 * KF), ("down2", KD, 4 * KD)):
        first[name] = (n, t)
        n, t = n + chunks, t + tiles
    CHUNKS = n

    def blocks_of(n):
        for name in ("down1", "down2"):
            if 0 <= n - first[name][0] < 4 * KD:
                return DOWN[(n - first[name][0]) % 4]
        return CHUNK

    PROJ = [("dt", 0, COL_DT_WINDOW)]
    PROJ += [("conv", c, COL_CONV + c * P) for c in range(CONV_TILES)]
    PROJ += [("v", h, COL_V + h * P) for h in range(A_HEADS)]
    PROJ += [("z", q, COL_Z + q * P) for q in range(PAIRS)]
    PROJ += [("u", h, COL_U + h * P) for h in range(A_HEADS)]
    AT = {(kind, index): i for i, (kind, index, _) in enumerate(PROJ)}

    JOBS = {i: [] for i in range(W_TILES)}
    JOBS[2] += [("dt_rows", 0), ("spatial_w", 0), ("spatial_w", 1)]
    for c in range(PAIRS):
        JOBS[AT["conv", c] + 2] += [("x_rows", c)]
    JOBS[6] += [("decay_sum", 0)]
    SCORES_AT = AT["conv", CONV_TILES - 1] + 2
    JOBS[SCORES_AT] += [("scores", 0), ("scores", 1)]
    for q in range(PAIRS):
        JOBS[SCORES_AT + (3 * q) // 2] += [("diag", q)]
        JOBS[SCORES_AT + 1 + (3 * q) // 2] += [("decay", q)]
        JOBS[SCORES_AT + 3 + (3 * q) // 2] += [("mix", q)]
    for h in range(A_HEADS):
        JOBS[AT["v", h] + 1] += [("v_rows", h)]
        JOBS[AT["u", h]] += [("gating", h)]
    JOBS[AT["v", A_HEADS - 1] + 2] += [("v_norm", 0)]
    for g in range(GROUPS):
        JOBS[AT["z", (g + 1) * GROUP_PAIRS - 1] + 2] += [("group_norm", g)]
    JOB_ORDER = [job for i in range(W_TILES) for job in JOBS[i]]
    TURNS = [j for j in JOB_ORDER if j[0] in ("dt_rows", "spatial_w", "x_rows", "v_rows")]
    SUMS = [j for j in JOB_ORDER if j[0] in ("decay_sum", "scores", "v_norm", "group_norm", "gating")]

    PARAM_ROWS = [("f1_pre", f1_pre), ("f1_post", f1_post), ("mix_pre", mix_pre), ("mix_post", mix_post),
                  ("f2_pre", f2_pre), ("f2_post", f2_post), ("sgu", sgu_norm), ("ssm", ssm_norm),
                  ("conv_b", conv_b)]
    col, column = 0, {}
    for name, vector in PARAM_ROWS:
        column[name] = col
        col += vector.shape[1] // P
    FIRST_ROWS = col
    column["conv_w"] = col
    PARAMS = col + TAPS * CONV_TILES
    assert FIRST_ROWS <= P and TAPS * CONV_TILES <= P

    ctx = ExitStack()
    with ctx:
        at = [(nc.sbuf_base + 31) // 32 * 32]

        def place(name, shape, dtype=F32, offset=None):
            size = 4
            for s in shape[1:]:
                size *= s
            if offset is None:
                offset = at[0]
                at[0] += (size + 31) // 32 * 32
            return nc.alloc_sbuf_tensor_at(name, shape, dtype, offset=offset)

        raw = place("raw", [P, RAW_SLOTS, CHUNK, P])
        high = place("high", [P, 2, CHUNK, P], F32R)
        low = place("low", [P, 2, CHUNK, P], F32R)
        x = place("x", [P, KD, T])
        xg = place("xg", [P, KD, 2 * T], F32R)
        y_at = at[0]
        y = place("y", [P, KD, T])
        low_half = place("low_half", [P, 2, T])
        gate_up = place("gate_up", [P, 2, T])
        total = place("total", [P, T])
        pre_scale = place("pre_scale", [P, T])
        ident = place("ident", [P, P])
        ones = place("ones", [P, P])
        params = place("params", [P, PARAMS])
        h_at = at[0]
        h = place("h", [P, KF, 2 * T], F32R)
        h_end = at[0]
        square_sum = gate_up[:, 0, :]
        squares = gate_up[:, 1, :]

        at[0] = h_at
        mixed = place("mixed", [P, KD, 2 * T], F32R)
        mixed_end = at[0]
        at[0] = h_at
        post_scale = place("post_scale", [P, T])
        variance = place("variance", [P, T])
        squares4 = place("squares4", [P, 4, T])
        square_sum4 = place("square_sum4", [P, 4, T])
        w_rows = place("w_rows", [P, A_HEADS, P])
        causal = place("causal", [P, P])
        assert at[0] <= mixed_end
        at[0] = mixed_end
        x_rows = place("x_rows", [P, TT, B_WIDTH])
        w_cols = place("w_cols", [P, A_HEADS, P])
        b_rows = place("b_rows", [P, A_HEADS, P])
        scores = place("scores", [P, GROUPS, T + P])
        decay = place("decay", [P, 2, T + P])
        diag = place("diag", [P, 2, TT, P])
        conv_in = place("conv_in", [P, 2, T + 8])
        conv = place("conv", [P, T])
        b_state = place("b_state", [P, GROUPS, T])
        c_state = place("c_state", [P, GROUPS, T])
        proj = place("proj", [P, 2, T])
        z_gate = place("z_gate", [P, 2, T])
        v_act = place("v_act", [P, 2, T])
        v_square = place("v_square", [P, T])
        v_gain = place("v_gain", [P, 2, T])
        u_act = place("u_act", [P, 2, T])
        v_sum = place("v_sum", [P, T])
        y_square = place("y_square", [P, T])
        y_sum = place("y_sum", [P, GROUPS, T])
        group_var = place("group_var", [P, T])
        group_scale = place("group_scale", [P, T])
        gated = place("gated", [P, T])
        HT = [P, SSM_HEADS, TT]
        dt_bias_rows = place("dt_bias_rows", [P, SSM_HEADS])
        a_rows = place("a_rows", [P, SSM_HEADS])
        skip = place("skip", [P, PAIRS])
        dt_raw, dt_abs, dt_exp, dt_one, dt_log, dt_den, dt_zero, dt, dt_a, decay_sum = (
            place(name, HT) for name in ("dt_raw", "dt_abs", "dt_exp", "dt_one", "dt_log", "dt_den",
                                         "dt_zero", "dt", "dt_a", "decay_sum"))
        v_var = place("v_var", [P, TT])
        v_scale = place("v_scale", [P, TT])
        assert at[0] <= h_end, (at[0], h_end)
        x_conv = place("x_conv", [P, PAIRS, T], offset=y_at)
        v_rows = place("v_rows", [P, TT, A_WIDTH], offset=y_at + 4 * PAIRS * T)
        at[0] = mixed_end
        x_nat = place("x_nat", [P, TT, D])
        out_nat = place("out_nat", [P, TT, D])
        params_nat = place("params_nat", [P, 2, P])
        assert at[0] <= h_end

        def psum(name, shape):
            return ctx.enter_context(nc.psum_tensor(name, shape, F32))

        acc = [psum("acc0", [P, 2, 512]), psum("acc1", [P, 2, 512])]
        bank_turn = psum("bank_turn", [P, 512])
        bank_decay = psum("bank_decay", [P, 512])
        bank_mix = psum("bank_mix", [P, 512])
        bank_sum = psum("bank_sum", [P, 512])
        end_banks = [bank_turn, bank_decay, bank_mix, bank_sum]

        def sem(name):
            return ctx.enter_context(nc.semaphore(name))

        raw_loaded = [sem(f"raw_loaded{s}") for s in range(RAW_SLOTS)]
        high_ready, low_ready, high_used, low_used = (
            sem(s) for s in ("high_ready", "low_ready", "high_used", "low_used"))
        low_half_ready, acc_read = sem("low_half_ready"), sem("acc_read")
        scaled_ready, silu_ready, product_ready, h_high_ready, h_ready = (
            sem(s) for s in ("scaled_ready", "silu_ready", "product_ready", "h_high_ready", "h_ready"))
        squares_ready, square_sum_ready = sem("squares_ready"), sem("square_sum_ready")
        row_sums, variance_ready, inverse_ready, scale_ready = (
            sem(s) for s in ("row_sums", "variance_ready", "inverse_ready", "scale_ready"))
        y_scaled, x_ready, x_half_ready = sem("y_scaled"), sem("x_ready"), sem("x_half_ready")
        xg_high_ready, xg_ready = sem("xg_high_ready"), sem("xg_ready")
        squares4_ready, square_sum4_ready = sem("squares4_ready"), sem("square_sum4_ready")
        consts_ready, x_loaded, params_cleared, params_loaded, params_turned, params_ready = (
            sem(s) for s in ("consts_ready", "x_loaded", "params_cleared", "params_loaded",
                             "params_turned", "params_ready"))
        x_turned, out_turned, out_copied, out_copied_act, stored = (
            sem(s) for s in ("x_turned", "out_turned", "out_copied", "out_copied_act", "stored"))
        mixer_loaded, masks_ready, w_masked = sem("mixer_loaded"), sem("masks_ready"), sem("w_masked")
        proj_ready, conv_started, conv_step, conv_act_ready = (
            sem(s) for s in ("proj_ready", "conv_started", "conv_step", "conv_act_ready"))
        turned, turn_read = sem("turned"), sem("turn_read")
        summed, sum_read = sem("summed"), sem("sum_read")
        dt_step_dve, dt_step_act, dt_ready, da_ready = (
            sem(s) for s in ("dt_step_dve", "dt_step_act", "dt_ready", "da_ready"))
        diag_ready, decay_spread, decay_clamped, decay_exp, decay_ready, x_dt_ready = (
            sem(s) for s in ("diag_ready", "decay_spread", "decay_clamped", "decay_exp", "decay_ready",
                             "x_dt_ready"))
        ssm_out, ssm_read, z_ready, y_gated, y_square_ready, y_sum_ready = (
            sem(s) for s in ("ssm_out", "ssm_read", "z_ready", "y_gated", "y_square_ready", "y_sum_ready"))
        group_step, group_inverse, group_scale_ready, yb_normed, yb_high_ready, yb_ready = (
            sem(s) for s in ("group_step", "group_inverse", "group_scale_ready", "yb_normed",
                             "yb_high_ready", "yb_ready"))
        v_act_ready, v_square_ready, v_gain_ready, v_sum_ready = (
            sem(s) for s in ("v_act_ready", "v_square_ready", "v_gain_ready", "v_sum_ready"))
        v_step, v_inverse, v_scale_ready, v_rows_ready = (
            sem(s) for s in ("v_step", "v_inverse", "v_scale_ready", "v_rows_ready"))
        u_ready, ya_step, ya_raw_ready, ya_high_ready, ya_ready = (
            sem(s) for s in ("u_ready", "ya_step", "ya_raw_ready", "ya_high_ready", "ya_ready"))

        block = ctx.enter_context(nc.Block())

        def at_least(eng, s, value):
            if not (isinstance(value, int) and value <= 0):
                eng.wait_ge(s, value)

        def f32(ap):
            return ap.bitcast(F32)

        def spread(ap, shape, *axes):
            for a in axes:
                ap = ap.unsqueeze(a)
            return ap.to_broadcast(shape)

        def param(name, index):
            c = column[name] + index
            return params[:, c:c + 1]

        def phase(name):
            n0, t0 = first[name]
            return n0, n0 % RAW_SLOTS, t0, t0 % 2

        PRE = {"gate1": 0, "proj": 1, "gate2": 2}
        FFNS = [("gate1", "down1", f1_gate, f1_up, f1_down), ("gate2", "down2", f2_gate, f2_up, f2_down)]
        POST = [("down1", "f1_post", 0.25), ("wout", "mix_post", 1.0), ("down2", "f2_post", 0.25)]
        GAIN = ["f1_pre", "mix_pre", "f2_pre"]
        PAIR_ROUNDS = KF // 2

        @block.sync
        def _(sp):
            def load(n, s, source, blocks):
                s %= RAW_SLOTS
                at_least(sp, low_ready, n - (RAW_SLOTS - 1))
                sp.dma_start(raw[:, s, 0:blocks, :], source).then_inc(raw_loaded[s], 16)

            def rows(w):
                return w[0].rearrange("(k p) f -> p k f", p=P)

            def gate_up_tile(n, s, gate, up, j):
                load(n, s, rows(gate)[:, :, bass.ds(j * P, P)], KD)
                load(n + 1, s + 1, rows(up)[:, :, bass.ds(j * P, P)], KD)

            def ffn(gate_phase, down_phase, gate, up, down):
                n0, s0, _, _ = phase(gate_phase)
                for u in range(2):
                    gate_up_tile(n0 + 2 * u, s0 + 2 * u, gate, up, u)
                with sp.Fori(1, PAIR_ROUNDS) as i:
                    for u in range(2):
                        gate_up_tile(i * 4 + (n0 + 2 * u), s0 + 2 * u, gate, up, i * 2 + u)
                gate_up_tile(n0 + 2 * (KF - 1), s0 + 2 * (KF - 1), gate, up, KF - 1)
                n0, s0, _, _ = phase(down_phase)
                with sp.Fori(0, KD) as d:
                    for c in range(4):
                        load(d * 4 + (n0 + c), s0 + c,
                             rows(down)[:, DOWN_AT[c]:DOWN_AT[c] + DOWN[c], bass.ds(d * P, P)], DOWN[c])

            ffn(*FFNS[0])
            n0, s0, _, _ = phase("proj")
            for i, (_, _, c) in enumerate(PROJ):
                load(n0 + i, s0 + i, rows(w_in)[:, :, c:c + P], KD)
            n0, s0, _, _ = phase("wout")
            with sp.Fori(0, KD // 4) as i:
                for u in range(4):
                    load(i * 4 + (n0 + u), s0 + u, rows(w_out)[:, :, bass.ds(i * (4 * P) + u * P, P)], KD)
            ffn(*FFNS[1])
            out_rows = out[0].rearrange("(t p) d -> p t d", p=P)
            for g in range(4):
                cols = slice(g * 4 * P, (g + 1) * 4 * P)
                sp.wait_ge(out_copied, g + 1)
                sp.dma_start(out_rows[:, 0, cols], out_nat[:, 0, cols]).then_inc(stored, 16)
                sp.wait_ge(out_copied_act, g + 1)
                sp.dma_start(out_rows[:, 1, cols], out_nat[:, 1, cols]).then_inc(stored, 16)
            sp.wait_ge(stored, 8 * 16)

        @block.scalar
        def _(act):
            def split_high(n, s, blocks):
                s %= RAW_SLOTS
                act.wait_ge(raw_loaded[s], n * 4 + (16 - 4 * s))
                at_least(act, high_used, n - 1)
                at_least(act, low_ready, n - 1)
                act.activation(high[:, s % 2, 0:blocks, :], raw[:, s, 0:blocks, :],
                               ACT.Copy).then_inc(high_ready, 1)

            def take_low_half(n_end, t, parity, banks):
                act.wait_ge(low_used, n_end + 1)
                at_least(act, acc_read, t)
                act.activation(low_half[:, 0:banks, :], acc[parity % 2][:, 0:banks, T:2 * T],
                               ACT.Copy).then_inc(low_half_ready, 1)

            def hidden_tile(n, s, t, parity, j, f, blocks):
                split_high(n + 2, s + 2, blocks[0])
                take_low_half(n + 1, t, parity, 2)
                split_high(n + 3, s + 3, blocks[1])
                act.wait_ge(scaled_ready, f + 1)
                act.activation(gate_up[:, 0, :], gate_up[:, 0, :], ACT.Silu).then_inc(silu_ready, 1)
                act.wait_ge(product_ready, f + 1)
                act.activation(h[:, bass.ds(j, 1), 0:T], total[:].unsqueeze(1),
                               ACT.Copy).then_inc(h_high_ready, 1)

            def result_tile(n_end, t, parity, d, r, gain, split):
                take_low_half(n_end, t, parity, 1)
                if split is not None:
                    split_high(*split)
                act.wait_ge(acc_read, t + 1)
                act.activation(y[:, bass.ds(d, 1), :], total[:].unsqueeze(1), ACT.Copy,
                               scale=gain(d))
                at_least(act, square_sum_ready, r)
                act.activation(squares, total[:], ACT.Square).then_inc(squares_ready, 1)

            def root(m, scale, to):
                act.wait_ge(inverse_ready, m + 1)
                act.activation(to, variance[:], ACT.Sqrt, scale=scale).then_inc(scale_ready, 1)

            def pre_norm(p):
                for g in range(4):
                    act.wait_ge(x_ready, 4 * p + g + 1)
                    if p == 0:
                        act.wait_ge(x_half_ready, g + 1)
                    for k in range(4 * g, 4 * g + 4):
                        act.activation(xg[:, k, 0:T], x[:, k, :], ACT.Copy,
                                       scale=param(GAIN[p], k)).then_inc(xg_high_ready, 1)
                    at_least(act, square_sum4_ready, 4 * p + g)
                    act.activation(squares4[:], x[:, 4 * g:4 * g + 4, :],
                                   ACT.Square).then_inc(squares4_ready, 1)
                root(2 * p, 1.0, pre_scale[:])

            def ffn(which, gate_phase, down_phase, post_name):
                n0, s0, t0, p0 = phase(gate_phase)
                pre_norm(PRE[gate_phase])
                with act.Fori(0, PAIR_ROUNDS) as i:
                    for u in range(2):
                        hidden_tile(i * 4 + (n0 + 2 * u), s0 + 2 * u, i * 2 + (t0 + u), p0 + u,
                                    i * 2 + u, i * 2 + (which * KF + u), [CHUNK, CHUNK])
                j = KF - 1
                hidden_tile(n0 + 2 * j, s0 + 2 * j, t0 + j, p0 + j, j, which * KF + j, DOWN[0:2])
                down(which, down_phase, post_name)

            def down(which, down_phase, post_name):
                n0, s0, t0, p0 = phase(down_phase)
                r0 = 2 * which * KD

                def tile(n, s, t, parity, d, r, gain, after):
                    split_high(n + 2, s + 2, DOWN[2])
                    split_high(n + 3, s + 3, DOWN[3])
                    if after is not None:
                        split_high(n + 4, s + 4, after[0])
                    result_tile(n + 3, t, parity, d, r, gain,
                                None if after is None else (n + 5, s + 5, after[1]))

                def gain_at(d):
                    c = column[post_name]
                    return params[:, bass.ds(d + c, 1)]

                with act.Fori(0, KD // 2 - 1) as i:
                    for u in range(2):
                        tile(i * 8 + (n0 + 4 * u), s0, i * 2 + (t0 + u), p0 + u, i * 2 + u,
                             i * 2 + (r0 + u), gain_at, DOWN[0:2])
                for d in (KD - 2, KD - 1):
                    after = DOWN[0:2] if d < KD - 1 else None if which == 1 else [CHUNK, CHUNK]
                    tile(n0 + 4 * d, s0, t0 + d, p0 + d, d, r0 + d, gain_at, after)

            act.dma_start(x_nat[:], x_in[0].rearrange("(t p) d -> p t d", p=P)).then_inc(x_loaded, 16)
            act.wait_ge(params_cleared, 1)
            for name, vector in PARAM_ROWS:
                c, rows = column[name], vector.shape[1] // P
                act.dma_start(params_nat[c:c + rows, 0, :],
                              vector[0].rearrange("(j p) -> j p", p=P)).then_inc(params_loaded, 16)
            act.dma_start(params_nat[0:TAPS * CONV_TILES, 1, :],
                          conv_w[0].rearrange("k (j p) -> (k j) p", p=P)).then_inc(params_loaded, 16)
            split_high(0, 0, CHUNK)
            split_high(1, 1, CHUNK)
            for g in range(4):
                act.wait_ge(x_turned, 2 * g + 2)
                act.activation(x[:, 4 * g:4 * g + 4, P:2 * P],
                               end_banks[(2 * g + 1) % 4][:].rearrange("p (k t) -> p k t", k=4),
                               ACT.Copy).then_inc(x_half_ready, 1)
            act.wait_ge(params_ready, 1)
            ffn(0, "gate1", "down1", "f1_post")
            root(1, POST[0][2], post_scale[:])

            pre_norm(1)
            n0, s0, t0, p0 = phase("proj")
            act.dma_start(w_rows[:], w_spatial[0].rearrange("h t s -> t h s")).then_inc(mixer_loaded, 16)
            act.dma_start(b_rows[:].rearrange("p h t -> p (h t)"),
                          b_spatial.rearrange("l h t -> l (h t)").to_broadcast([P, A_HEADS * P])
                          ).then_inc(mixer_loaded, 16)
            act.dma_start(dt_bias_rows[:], dt_bias.to_broadcast([P, SSM_HEADS])).then_inc(mixer_loaded, 16)
            act.dma_start(a_rows[:], a_log.to_broadcast([P, SSM_HEADS])).then_inc(mixer_loaded, 16)
            for e in range(2):
                act.dma_start(skip[64 * e:64 * e + 64, :],
                              d_skip[0:1, e:SSM_HEADS:2].to_broadcast([64, PAIRS]),
                              allow_slow_non_contiguous=True).then_inc(mixer_loaded, 16)

            def activate(i):
                kind, k, _ = PROJ[i]
                if kind == "dt":
                    return
                act.wait_ge(proj_ready, i + 1)
                if kind == "conv":
                    at_least(act, conv_act_ready, k)
                    act.activation(conv[:], conv_in[:, k % 2, 0:T], ACT.Identity,
                                   scale=param("conv_w", k), bias=param("conv_b", k)
                                   ).then_inc(conv_started, 1)
                elif kind == "z":
                    at_least(act, y_gated, k - 1)
                    act.activation(z_gate[:, k % 2, :], proj[:, i % 2, :], ACT.Silu).then_inc(z_ready, 1)
                elif kind == "v":
                    at_least(act, v_square_ready, k - 1)
                    act.activation(v_act[:, k % 2, :], proj[:, i % 2, :], ACT.Gelu).then_inc(v_act_ready, 1)
                    act.wait_ge(v_act_ready, k + 1)
                    if k >= 2:
                        act.wait_ge(turned, TURNS.index(("v_rows", k - 2)) + 1)
                    act.activation(v_gain[:, k % 2, :], v_act[:, k % 2, :], ACT.Copy,
                                   scale=param("sgu", k)).then_inc(v_gain_ready, 1)
                elif kind == "u":
                    at_least(act, ya_raw_ready, k - 1)
                    act.activation(u_act[:, k % 2, :], proj[:, i % 2, :], ACT.Gelu).then_inc(u_ready, 1)

            def conv_silu(c):
                act.wait_ge(conv_step, PAD * (c + 1))
                to = (x_conv[:, c, :] if c < PAIRS else b_state[:, c - PAIRS, :]
                      if c < PAIRS + GROUPS else c_state[:, c - PAIRS - GROUPS, :])
                act.activation(to, conv[:], ACT.Silu).then_inc(conv_act_ready, 1)

            def mixer_job(kind, k):
                if kind == "dt_rows":
                    act.wait_ge(turn_read, TURNS.index((kind, k)) + 1)
                    act.activation(dt_abs[:], dt_raw[:], ACT.Abs).then_inc(dt_step_act, 1)
                    act.wait_ge(dt_step_act, 1)
                    act.activation(dt_exp[:], dt_abs[:], ACT.Exp, scale=-1.0).then_inc(dt_step_act, 1)
                    act.wait_ge(mixer_loaded, 6 * 16)
                    act.activation(a_rows[:], a_rows[:], ACT.Exp).then_inc(dt_step_act, 1)
                    act.wait_ge(dt_step_dve, 1)
                    act.activation(dt_log[:], dt_one[:], ACT.Ln).then_inc(dt_step_act, 1)
                elif kind in ("x_rows", "v_rows"):
                    n = TURNS.index((kind, k))
                    act.wait_ge(turned, n + 1)
                    to = x_rows if kind == "x_rows" else v_rows
                    act.activation(to[:, :, k * P:(k + 1) * P],
                                   bank_turn[:, 0:TT * P].rearrange("p (t d) -> p t d", t=TT),
                                   ACT.Copy).then_inc(turn_read, 1)
                elif kind == "decay":
                    act.wait_ge(decay_clamped, k + 1)
                    act.activation(decay[:], decay[:], ACT.Exp).then_inc(decay_exp, 1)
                elif kind == "v_norm":
                    act.wait_ge(v_inverse, 1)
                    act.activation(v_scale[:], v_var[:], ACT.Sqrt).then_inc(v_scale_ready, 1)
                elif kind == "group_norm":
                    act.wait_ge(group_inverse, k + 1)
                    act.activation(group_scale[:], group_var[:], ACT.Sqrt).then_inc(group_scale_ready, 1)
                    act.wait_ge(yb_normed, GROUP_PAIRS * (k + 1))
                    qs = slice(k * GROUP_PAIRS, (k + 1) * GROUP_PAIRS)
                    act.activation(mixed[:, PAIRS + k * GROUP_PAIRS:PAIRS + (k + 1) * GROUP_PAIRS, 0:T],
                                   x_conv[:, qs, :], ACT.Copy).then_inc(yb_high_ready, 1)
                elif kind == "gating":
                    act.wait_ge(ya_raw_ready, k + 1)
                    act.activation(mixed[:, k, 0:T], gated[:], ACT.Copy).then_inc(ya_high_ready, 1)

            for i in range(W_TILES):
                take_low_half(n0 + i, t0 + i, p0 + i, 1)
                if i >= 1 and PROJ[i - 1][0] == "conv":
                    conv_silu(PROJ[i - 1][1])
                split_high(n0 + i + 2, s0 + i + 2, CHUNK)
                activate(i)
                for job in JOBS[i]:
                    mixer_job(*job)

            n0, s0, t0, p0 = phase("wout")
            c = column["mix_post"]
            with act.Fori(0, KD // 4) as i:
                for u in range(4):
                    result_tile(i * 4 + (n0 + u), i * 4 + (t0 + u), p0 + u, i * 4 + u, i * 4 + (KD + u),
                                lambda d: params[:, bass.ds(d + c, 1)],
                                (i * 4 + (n0 + u + 2), s0 + u + 2, CHUNK))
            root(3, POST[1][2], post_scale[:])
            ffn(1, "gate2", "down2", "f2_post")
            root(5, POST[2][2], post_scale[:])
            for g in range(4):
                act.wait_ge(out_turned, 2 * g + 2)
                act.activation(out_nat[:, 1, g * 512:(g + 1) * 512], end_banks[(2 * g + 1) % 4][:],
                               ACT.Copy).then_inc(out_copied_act, 1)

        @block.vector
        def _(dve):
            def split_low(n, s, blocks):
                s %= RAW_SLOTS
                dve.wait_ge(high_ready, n + 1)
                at_least(dve, low_used, n - 1)
                dve.tensor_tensor(low[:, s % 2, 0:blocks, :], raw[:, s, 0:blocks, :],
                                  f32(high[:, s % 2, 0:blocks, :]), ALU.subtract).then_inc(low_ready, 1)

            def hidden_tile(n, s, t, parity, j, f, blocks):
                split_low(n + 2, s + 2, blocks[0])
                dve.wait_ge(low_half_ready, t + 1)
                dve.tensor_tensor(gate_up[:], acc[parity % 2][:, :, 0:T], low_half[:],
                                  ALU.add).then_inc(acc_read, 1)
                dve.wait_ge(acc_read, t + 1)
                dve.tensor_tensor(gate_up[:], gate_up[:], spread(pre_scale[:], [P, 2, T], 1),
                                  ALU.mult).then_inc(scaled_ready, 1)
                split_low(n + 3, s + 3, blocks[1])
                dve.wait_ge(silu_ready, f + 1)
                dve.tensor_tensor(total[:], gate_up[:, 0, :], gate_up[:, 1, :],
                                  ALU.mult).then_inc(product_ready, 1)
                dve.wait_ge(h_high_ready, f + 1)
                dve.tensor_tensor(h[:, bass.ds(j, 1), T:2 * T], total[:].unsqueeze(1),
                                  f32(h[:, bass.ds(j, 1), 0:T]), ALU.subtract).then_inc(h_ready, 1)

            def result_tile(t, parity, r):
                dve.wait_ge(low_half_ready, t + 1)
                at_least(dve, squares_ready, r)
                dve.tensor_tensor(total[:], acc[parity % 2][:, 0, 0:T], low_half[:, 0, :],
                                  ALU.add).then_inc(acc_read, 1)

            def inverse(m):
                dve.wait_ge(row_sums, m + 1)
                dve.tensor_scalar(variance[:], bank_sum[:, 0:T], 1.0 / D, EPS, ALU.mult,
                                  ALU.add).then_inc(variance_ready, 1)
                dve.wait_ge(variance_ready, m + 1)
                dve.reciprocal(variance[:], variance[:]).then_inc(inverse_ready, 1)

            def post_norm(b):
                inverse(2 * b + 1)
                dve.wait_ge(scale_ready, 2 * b + 2)
                for g in range(4):
                    ys = y[:, 4 * g:4 * g + 4, :]
                    dve.tensor_tensor(ys, ys, spread(post_scale[:], [P, 4, T], 1),
                                      ALU.mult).then_inc(y_scaled, 1)

            def pre_norm(p):
                for k in range(KD):
                    dve.wait_ge(xg_high_ready, KD * p + k + 1)
                    dve.scalar_tensor_tensor(xg[:, k, T:2 * T], x[:, k, :], param(GAIN[p], k),
                                             f32(xg[:, k, 0:T]), ALU.mult,
                                             ALU.subtract).then_inc(xg_ready, 1)
                inverse(2 * p)
                dve.wait_ge(scale_ready, 2 * p + 1)

            def ffn(which, gate_phase, down_phase):
                n0, s0, t0, p0 = phase(gate_phase)
                pre_norm(PRE[gate_phase])
                with dve.Fori(0, PAIR_ROUNDS) as i:
                    for u in range(2):
                        hidden_tile(i * 4 + (n0 + 2 * u), s0 + 2 * u, i * 2 + (t0 + u), p0 + u,
                                    i * 2 + u, i * 2 + (which * KF + u), [CHUNK, CHUNK])
                j = KF - 1
                hidden_tile(n0 + 2 * j, s0 + 2 * j, t0 + j, p0 + j, j, which * KF + j, DOWN[0:2])
                n0, s0, t0, p0 = phase(down_phase)
                r0 = 2 * which * KD

                def tile(n, s, t, parity, r, after):
                    split_low(n + 2, s + 2, DOWN[2])
                    split_low(n + 3, s + 3, DOWN[3])
                    if after is not None:
                        split_low(n + 4, s + 4, after[0])
                    result_tile(t, parity, r)
                    if after is not None:
                        split_low(n + 5, s + 5, after[1])

                with dve.Fori(0, KD // 2 - 1) as i:
                    for u in range(2):
                        tile(i * 8 + (n0 + 4 * u), s0, i * 2 + (t0 + u), p0 + u, i * 2 + (r0 + u),
                             DOWN[0:2])
                for d in (KD - 2, KD - 1):
                    after = DOWN[0:2] if d < KD - 1 else None if which == 1 else [CHUNK, CHUNK]
                    tile(n0 + 4 * d, s0, t0 + d, p0 + d, r0 + d, after)
                post_norm(2 * which)

            split_low(0, 0, CHUNK)
            split_low(1, 1, CHUNK)
            dve.wait_ge(params_turned, 1)
            dve.tensor_copy(params[:, 0:FIRST_ROWS], bank_sum[:, 0:FIRST_ROWS])
            dve.tensor_copy(params[:, FIRST_ROWS:PARAMS],
                            bank_sum[:, P:P + PARAMS - FIRST_ROWS]).then_inc(params_ready, 1)
            for g in range(4):
                dve.wait_ge(x_turned, 2 * g + 1)
                dve.tensor_copy(x[:, 4 * g:4 * g + 4, 0:P],
                                end_banks[(2 * g) % 4][:].rearrange("p (k t) -> p k t", k=4)
                                ).then_inc(x_ready, 1)
            dve.wait_ge(params_ready, 1)
            ffn(0, "gate1", "down1")

            pre_norm(1)
            n0, s0, t0, p0 = phase("proj")

            def conv_taps(c):
                dve.wait_ge(conv_started, c + 1)
                for k in range(1, TAPS):
                    at_least(dve, conv_step, PAD * c + k - 1)
                    dve.scalar_tensor_tensor(conv[:], conv_in[:, c % 2, k:k + T],
                                             param("conv_w", k * CONV_TILES + c), conv[:], ALU.mult,
                                             ALU.add).then_inc(conv_step, 1)

            dt_steps = [0]

            def dt_chain(instruction):
                dt_steps[0] += 1
                instruction.then_inc(dt_step_dve, 1)
                dve.wait_ge(dt_step_dve, dt_steps[0])

            def mixer_job(kind, k):
                if kind == "dt_rows":
                    dve.wait_ge(turned, TURNS.index((kind, k)) + 1)
                    dve.wait_ge(mixer_loaded, 6 * 16)
                    dve.tensor_tensor(
                        dt_raw[:],
                        bank_turn[:, 0:TT * P].rearrange("p (t d) -> p d t", t=TT)[:, DT_ROW:P, :],
                        spread(dt_bias_rows[:], HT, 2), ALU.add).then_inc(turn_read, 1)
                    dve.wait_ge(dt_step_act, 2)
                    dt_chain(dve.tensor_scalar(dt_one[:], dt_exp[:], 1.0, None, ALU.add))
                    dt_chain(dve.tensor_scalar(dt_den[:], dt_one[:], -1.0, None, ALU.add))
                    dt_chain(dve.tensor_scalar(dt_zero[:], dt_den[:], 0.0, None, ALU.is_equal))
                    dt_chain(dve.tensor_tensor(dt_den[:], dt_den[:], dt_zero[:], ALU.add))
                    dt_chain(dve.reciprocal(dt_den[:], dt_den[:]))
                    dve.wait_ge(dt_step_act, 4)
                    dt_chain(dve.tensor_tensor(dt_log[:], dt_log[:], dt_den[:], ALU.mult))
                    dt_chain(dve.tensor_tensor(dt_log[:], dt_log[:], dt_zero[:], ALU.add))
                    dt_chain(dve.tensor_tensor(dt_log[:], dt_log[:], dt_exp[:], ALU.mult))
                    dve.scalar_tensor_tensor(dt[:], dt_raw[:], 0.0, dt_log[:], ALU.max,
                                             ALU.add).then_inc(dt_ready, 1)
                    dve.wait_ge(dt_ready, 1)
                    dve.scalar_tensor_tensor(dt_a[:], dt[:], -1.0, spread(a_rows[:], HT, 2), ALU.mult,
                                             ALU.mult).then_inc(da_ready, 1)
                elif kind == "spatial_w":
                    dve.wait_ge(turned, TURNS.index((kind, k)) + 1)
                    dve.tensor_copy(w_cols[:, 4 * k:4 * k + 4, :],
                                    bank_turn[:].rearrange("p (h t) -> p h t", h=4)).then_inc(turn_read, 1)
                elif kind == "decay_sum":
                    dve.wait_ge(summed, SUMS.index((kind, k)) + 1)
                    sums = bank_sum[:, 0:TT * SSM_HEADS].rearrange("p (t h) -> p h t", t=TT)
                    dve.tensor_copy(decay_sum[:], sums).then_inc(sum_read, 1)
                elif kind == "scores":
                    dve.wait_ge(summed, SUMS.index((kind, k)) + 1)
                    dve.tensor_tensor(scores[:, k, 0:P], bank_sum[:, 0:P], causal[:], ALU.mult)
                    dve.tensor_copy(scores[:, k, P:T], bank_sum[:, P:T])
                    dve.tensor_tensor(scores[:, k, T:T + P], bank_sum[:, T:T + P], causal[:],
                                      ALU.mult).then_inc(sum_read, 1)
                elif kind == "decay":
                    dve.wait_ge(decay_spread, k + 1)
                    at_least(dve, ssm_out, k)
                    for e in range(2):
                        for t, to, source in ((0, slice(0, T), slice(e * T, (e + 1) * T)),
                                              (1, slice(T, T + P), slice(e * T + P, (e + 1) * T))):
                            last = dve.tensor_scalar(decay[:, e, to], bank_decay[:, source],
                                                     decay_sum[:, 2 * k + e, t:t + 1], 0.0,
                                                     ALU.subtract, ALU.min)
                    last.then_inc(decay_clamped, 1)
                    dve.wait_ge(decay_exp, k + 1)
                    dve.tensor_tensor(decay[:], decay[:],
                                      spread(scores[:, k // GROUP_PAIRS, :], [P, 2, T + P], 1),
                                      ALU.mult).then_inc(decay_ready, 1)
                elif kind == "mix":
                    dve.wait_ge(ssm_out, k + 1)
                    dve.scalar_tensor_tensor(x_conv[:, k, :], x_conv[:, k, :], skip[:, k:k + 1],
                                             bank_mix[:, 0:T], ALU.mult, ALU.add).then_inc(ssm_read, 1)
                elif kind == "v_norm":
                    dve.wait_ge(summed, SUMS.index((kind, k)) + 1)
                    dve.tensor_scalar(v_var[:], bank_sum[:, 0:TT], 1.0 / A_WIDTH, EPS, ALU.mult,
                                      ALU.add).then_inc(sum_read, 1)
                    dve.wait_ge(sum_read, SUMS.index((kind, k)) + 1)
                    dve.reciprocal(v_var[:], v_var[:]).then_inc(v_inverse, 1)
                    dve.wait_ge(v_scale_ready, 1)
                    for t in range(TT):
                        dve.tensor_scalar(v_rows[:, t, :], v_rows[:, t, :], v_scale[:, t:t + 1], None,
                                          ALU.mult).then_inc(v_rows_ready, 1)
                elif kind == "group_norm":
                    dve.wait_ge(summed, SUMS.index((kind, k)) + 1)
                    dve.tensor_scalar(group_var[:], bank_sum[:, 0:T], 1.0 / (GROUP_PAIRS * P), EPS,
                                      ALU.mult, ALU.add).then_inc(sum_read, 1)
                    dve.wait_ge(sum_read, SUMS.index((kind, k)) + 1)
                    dve.reciprocal(group_var[:], group_var[:]).then_inc(group_inverse, 1)
                    dve.wait_ge(group_scale_ready, k + 1)
                    for q in range(k * GROUP_PAIRS, (k + 1) * GROUP_PAIRS):
                        dve.scalar_tensor_tensor(x_conv[:, q, :], x_conv[:, q, :], param("ssm", q),
                                                 group_scale[:], ALU.mult, ALU.mult).then_inc(yb_normed, 1)
                    dve.wait_ge(yb_high_ready, k + 1)
                    qs = slice(k * GROUP_PAIRS, (k + 1) * GROUP_PAIRS)
                    ks = slice(A_HEADS + k * GROUP_PAIRS, A_HEADS + (k + 1) * GROUP_PAIRS)
                    dve.tensor_tensor(mixed[:, ks, T:2 * T], x_conv[:, qs, :], f32(mixed[:, ks, 0:T]),
                                      ALU.subtract).then_inc(yb_ready, 1)
                elif kind == "gating":
                    dve.wait_ge(summed, SUMS.index((kind, k)) + 1)
                    at_least(dve, ya_ready, k)
                    dve.tensor_tensor(gated[:].rearrange("p (c t) -> p c t", c=TT),
                                      bank_sum[:, 0:T].rearrange("p (c t) -> p c t", c=TT),
                                      spread(b_rows[:, k, :], [P, TT, P], 1), ALU.add).then_inc(sum_read, 1)
                    dve.wait_ge(sum_read, SUMS.index((kind, k)) + 1)
                    dve.wait_ge(u_ready, k + 1)
                    dve.tensor_tensor(gated[:], gated[:], u_act[:, k % 2, :],
                                      ALU.mult).then_inc(ya_raw_ready, 1)
                    dve.wait_ge(ya_high_ready, k + 1)
                    dve.tensor_tensor(mixed[:, k, T:2 * T], gated[:], f32(mixed[:, k, 0:T]),
                                      ALU.subtract).then_inc(ya_ready, 1)

            for i, (kind, k, _) in enumerate(PROJ):
                dve.wait_ge(low_half_ready, t0 + i + 1)
                at_least(dve, proj_ready, i)
                dve.tensor_tensor(total[:], acc[(p0 + i) % 2][:, 0, 0:T], low_half[:, 0, :],
                                  ALU.add).then_inc(acc_read, 1)
                split_low(n0 + i + 2, s0 + i + 2, CHUNK)
                if kind == "conv":
                    conv_taps(k)
                for job in JOBS[i]:
                    mixer_job(*job)

            n0, s0, t0, p0 = phase("wout")
            with dve.Fori(0, KD // 4) as i:
                for u in range(4):
                    result_tile(i * 4 + (t0 + u), p0 + u, i * 4 + (KD + u))
                    split_low(i * 4 + (n0 + u + 2), s0 + u + 2, CHUNK)
            post_norm(1)
            ffn(1, "gate2", "down2")
            for g in range(4):
                dve.wait_ge(out_turned, 2 * g + 1)
                dve.tensor_copy(out_nat[:, 0, g * 512:(g + 1) * 512],
                                end_banks[(2 * g) % 4][:]).then_inc(out_copied, 1)

        @block.gpsimd
        def _(pool):
            pool.memset(params_nat[:], 0.0).then_inc(params_cleared, 1)
            pool.memset(ones[:], 1.0).then_inc(consts_ready, 1)
            pool.memset(ident[:], 0.0).then_inc(consts_ready, 1)
            pool.wait_ge(consts_ready, 2)
            pool.affine_select(out=ident[:], in_=ident[:], pattern=[[-1, P]], compare_op=ALU.not_equal,
                               fill=1.0, base=0, channel_multiplier=1).then_inc(consts_ready, 1)

            def sum_squares4(p):
                for g in range(4):
                    pool.wait_ge(squares4_ready, 4 * p + g + 1)
                    if g == 0:
                        pool.tensor_copy(square_sum4[:], squares4[:]).then_inc(square_sum4_ready, 1)
                    else:
                        pool.wait_ge(square_sum4_ready, 4 * p + g)
                        pool.tensor_tensor(square_sum4[:], square_sum4[:], squares4[:],
                                           ALU.add).then_inc(square_sum4_ready, 1)

            def sum_squares(b):
                pool.wait_ge(squares_ready, b * KD + 1)
                pool.tensor_copy(square_sum, squares).then_inc(square_sum_ready, 1)
                with pool.Fori(1, KD) as d:
                    pool.wait_ge(squares_ready, d + (b * KD + 1))
                    pool.wait_ge(square_sum_ready, d + b * KD)
                    pool.tensor_tensor(square_sum, square_sum, squares, ALU.add).then_inc(square_sum_ready, 1)

            def add_residual(b, g):
                pool.wait_ge(y_scaled, 4 * b + g + 1)
                xs = x[:, 4 * g:4 * g + 4, :]
                pool.tensor_tensor(xs, xs, y[:, 4 * g:4 * g + 4, :], ALU.add).then_inc(x_ready, 1)

            sum_squares4(0)
            sum_squares(0)
            for g in range(4):
                add_residual(0, g)
            sum_squares4(1)

            n0, s0, t0, p0 = phase("proj")
            pool.wait_ge(row_sums, 3)
            pool.memset(conv_in[:, :, 0:PAD], 0.0).then_inc(masks_ready, 1)
            pool.memset(causal[:], 1.0).then_inc(masks_ready, 1)
            pool.wait_ge(masks_ready, 2)
            pool.affine_select(out=causal[:], in_=causal[:], pattern=[[1, P]], compare_op=ALU.is_ge,
                               fill=0.0, base=0, channel_multiplier=-1).then_inc(masks_ready, 1)
            pool.wait_ge(mixer_loaded, 6 * 16)
            pool.affine_select(out=w_rows[:], in_=w_rows[:], pattern=[[0, A_HEADS], [-1, P]],
                               compare_op=ALU.is_ge, fill=0.0, base=0,
                               channel_multiplier=1).then_inc(w_masked, 1)
            pool.wait_ge(scale_ready, 3)

            def gate_y(q):
                pool.wait_ge(z_ready, q + 1)
                pool.wait_ge(ssm_read, q + 1)
                pool.tensor_tensor(x_conv[:, q, :], x_conv[:, q, :], z_gate[:, q % 2, :],
                                   ALU.mult).then_inc(y_gated, 1)
                pool.wait_ge(y_gated, q + 1)
                pool.tensor_tensor(y_square[:], x_conv[:, q, :], x_conv[:, q, :],
                                   ALU.mult).then_inc(y_square_ready, 1)
                pool.wait_ge(y_square_ready, q + 1)
                total_of = y_sum[:, q // GROUP_PAIRS, :]
                if q % GROUP_PAIRS == 0:
                    pool.tensor_copy(total_of, y_square[:]).then_inc(y_sum_ready, 1)
                else:
                    pool.tensor_tensor(total_of, total_of, y_square[:], ALU.add).then_inc(y_sum_ready, 1)
                pool.wait_ge(y_sum_ready, q + 1)

            def square_v(k):
                pool.wait_ge(v_act_ready, k + 1)
                pool.tensor_tensor(v_square[:], v_act[:, k % 2, :], v_act[:, k % 2, :],
                                   ALU.mult).then_inc(v_square_ready, 1)
                pool.wait_ge(v_square_ready, k + 1)
                if k == 0:
                    pool.tensor_copy(v_sum[:], v_square[:]).then_inc(v_sum_ready, 1)
                else:
                    pool.tensor_tensor(v_sum[:], v_sum[:], v_square[:], ALU.add).then_inc(v_sum_ready, 1)
                pool.wait_ge(v_sum_ready, k + 1)

            ACTIVATED = {"v": v_act_ready, "z": z_ready, "u": u_ready}
            for i, (kind, k, _) in enumerate(PROJ):
                pool.wait_ge(acc_read, t0 + i + 1)
                if kind == "conv":
                    at_least(pool, conv_step, PAD * (k - 1))
                    to = conv_in[:, k % 2, PAD:PAD + T]
                else:
                    if i >= 2 and PROJ[i - 2][0] in ACTIVATED:
                        pool.wait_ge(ACTIVATED[PROJ[i - 2][0]], PROJ[i - 2][1] + 1)
                    to = proj[:, i % 2, :]
                pool.tensor_tensor(to, total[:], pre_scale[:], ALU.mult).then_inc(proj_ready, 1)
                before, kb, _ = PROJ[i - 1]
                if i >= 1 and before == "z":
                    gate_y(kb)
                if i >= 1 and before == "v":
                    square_v(kb)
                for job, q in JOBS[i]:
                    if job == "diag":
                        pool.wait_ge(sum_read, SUMS.index(("decay_sum", 0)) + 1)
                        at_least(pool, decay_spread, q)
                        shape = [P, 2, TT, P]
                        pool.tensor_tensor(diag[:], spread(ident[:], shape, 1, 1),
                                           spread(decay_sum[:, 2 * q:2 * q + 2, :], shape, 3),
                                           ALU.mult).then_inc(diag_ready, 1)
                        pool.wait_ge(turn_read, TURNS.index(("x_rows", q)) + 1)
                        for t in range(TT):
                            rows = x_rows[:, t, q * P:(q + 1) * P].rearrange("p (e d) -> p e d", e=2)
                            pool.tensor_tensor(rows, rows, spread(dt[:, 2 * q:2 * q + 2, t], [P, 2, 64], 2),
                                               ALU.mult).then_inc(x_dt_ready, 1)

            sum_squares(1)
            for g in range(4):
                add_residual(1, g)
            sum_squares4(2)
            sum_squares(2)
            for g in range(4):
                add_residual(2, g)

        @block.tensor
        def _(pe):
            def chunk(n, s, blocks, moving, k0, bank, start, stop, order=None, wait_for=None):
                order = order or list(range(blocks))
                pe.wait_ge(high_ready, n + 1)
                for b in order:
                    if wait_for is not None:
                        wait_for(k0 + b)
                    last = pe.matmul(bank, high[:, s % 2, b, :], moving[:, k0 + b, :],
                                     start=start and b == order[0], stop=False)
                last.then_inc(high_used, 1)
                pe.wait_ge(low_ready, n + 1)
                for b in order:
                    last = pe.matmul(bank[:, 0:T], low[:, s % 2, b, :], moving[:, k0 + b, 0:T],
                                     start=False, stop=stop and b == order[-1])
                last.then_inc(low_used, 1)

            def post_sums(b):
                pe.wait_ge(square_sum_ready, KD * (b + 1))
                pe.wait_ge(variance_ready, 2 * b + 1)
                if b == 1:
                    pe.wait_ge(sum_read, len(SUMS))
                pe.matmul(bank_sum[:, 0:T], ones[:], square_sum, start=True, stop=True).then_inc(row_sums, 1)

            def pre_sums(p):
                pe.wait_ge(square_sum4_ready, 4 * (p + 1))
                if p == 0:
                    pe.wait_ge(x_half_ready, 4)
                else:
                    pe.wait_ge(variance_ready, 2 * p)
                for k in range(4):
                    last = pe.matmul(bank_sum[:, 0:T], ones[:], square_sum4[:, k, :], start=(k == 0),
                                     stop=(k == 3))
                last.then_inc(row_sums, 1)

            def hidden_tile(n, s, t, parity, wait_for=None, after_gate=None):
                at_least(pe, acc_read, t - 1)
                bank = acc[parity % 2]
                chunk(n, s, KD, xg, 0, bank[:, 0, :], True, True, wait_for=wait_for)
                if after_gate is not None:
                    after_gate()
                chunk(n + 1, s + 1, KD, xg, 0, bank[:, 1, :], True, True)

            def ffn(which, gate_phase, down_phase):
                n0, s0, t0, p0 = phase(gate_phase)
                p = PRE[gate_phase]
                hidden_tile(n0, s0, t0, p0, lambda k: pe.wait_ge(xg_ready, KD * p + k + 1),
                            lambda: pre_sums(p))
                hidden_tile(n0 + 2, s0 + 2, t0 + 1, p0 + 1)
                with pe.Fori(1, PAIR_ROUNDS) as i:
                    for u in range(2):
                        hidden_tile(i * 4 + (n0 + 2 * u), s0 + 2 * u, i * 2 + (t0 + u), p0 + u)
                j = KF - 1
                hidden_tile(n0 + 2 * j, s0 + 2 * j, t0 + j, p0 + j)
                n0, s0, t0, p0 = phase(down_phase)

                def tile(n, t, parity):
                    at_least(pe, acc_read, t - 1)
                    for c in range(4):
                        pe.wait_ge(h_ready, which * KF + DOWN_AT[c] + DOWN[c])
                        chunk(n + c, s0 + c, DOWN[c], h, DOWN_AT[c], acc[parity % 2][:, 0, :],
                              c == 0, c == 3)

                with pe.Fori(0, KD // 2) as i:
                    for u in range(2):
                        tile(i * 8 + (n0 + 4 * u), i * 2 + (t0 + u), p0 + u)
                post_sums(2 * which)

            def transpose(to, source):
                return pe.transpose(to, source, ident[:])

            pe.wait_ge(consts_ready, 3)
            pe.wait_ge(params_loaded, 16 * (len(PARAM_ROWS) + 1))
            for r in range(2):
                last = transpose(bank_sum[:, r * P:(r + 1) * P], params_nat[:, r, :])
            last.then_inc(params_turned, 1)
            pe.wait_ge(x_loaded, 16)
            for g in range(4):
                for t in range(TT):
                    n = 2 * g + t
                    if n == 3:
                        pe.wait_ge(params_ready, 1)
                    if n >= 4:
                        pe.wait_ge((x_ready, x_half_ready)[t], g - 1)
                    for k in range(4):
                        last = transpose(end_banks[n % 4][:, k * P:(k + 1) * P],
                                         x_nat[:, t, (4 * g + k) * P:(4 * g + k + 1) * P])
                    last.then_inc(x_turned, 1)
            ffn(0, "gate1", "down1")

            def turn_begins(job):
                n = TURNS.index(job)
                at_least(pe, turn_read, n)

            def sum_begins(job):
                n = SUMS.index(job)
                if n == 0:
                    pe.wait_ge(variance_ready, 3)
                else:
                    pe.wait_ge(sum_read, n)

            def mixer_job(kind, k):
                job = (kind, k)
                if kind in ("dt_rows", "x_rows", "v_rows"):
                    turn_begins(job)
                    if kind == "dt_rows":
                        pe.wait_ge(proj_ready, 1)
                        source = proj[:, 0, :]
                    elif kind == "x_rows":
                        pe.wait_ge(conv_act_ready, k + 1)
                        source = x_conv[:, k, :]
                    else:
                        pe.wait_ge(v_gain_ready, k + 1)
                        source = v_gain[:, k % 2, :]
                    for t in range(TT):
                        last = transpose(bank_turn[:, t * P:(t + 1) * P], source[:, t * P:(t + 1) * P])
                    last.then_inc(turned, 1)
                elif kind == "spatial_w":
                    turn_begins(job)
                    pe.wait_ge(w_masked, 1)
                    for a in range(4):
                        last = transpose(bank_turn[:, a * P:(a + 1) * P], w_rows[:, 4 * k + a, :])
                    last.then_inc(turned, 1)
                elif kind == "decay_sum":
                    sum_begins(job)
                    pe.wait_ge(da_ready, 1)
                    pe.wait_ge(masks_ready, 3)
                    H = SSM_HEADS
                    pe.matmul(bank_sum[:, 0:H], causal[:], dt_a[:, :, 0], start=True, stop=True)
                    pe.matmul(bank_sum[:, H:2 * H], ones[:], dt_a[:, :, 0], start=True, stop=False)
                    pe.matmul(bank_sum[:, H:2 * H], causal[:], dt_a[:, :, 1], start=False,
                              stop=True).then_inc(summed, 1)
                elif kind == "scores":
                    sum_begins(job)
                    pe.wait_ge(conv_act_ready, CONV_TILES)
                    pe.matmul(bank_sum[:, 0:T], b_state[:, k, 0:P], c_state[:, k, :], start=True, stop=True)
                    pe.matmul(bank_sum[:, T:T + P], b_state[:, k, P:T], c_state[:, k, P:T], start=True,
                              stop=True).then_inc(summed, 1)
                elif kind == "decay":
                    pe.wait_ge(diag_ready, k + 1)
                    at_least(pe, decay_clamped, k)
                    pe.matmul(bank_decay[:], ones[:], diag[:].rearrange("p e t l -> p (e t l)"),
                              start=True, stop=True).then_inc(decay_spread, 1)
                elif kind == "mix":
                    pe.wait_ge(decay_ready, k + 1)
                    pe.wait_ge(x_dt_ready, TT * (k + 1))
                    at_least(pe, ssm_read, k)
                    for e in range(2):
                        rows, head = slice(64 * e, 64 * e + 64), slice(k * P + 64 * e, k * P + 64 * e + 64)
                        pe.matmul(bank_mix[rows, 0:T], x_rows[:, 0, head], decay[:, e, 0:T], start=True,
                                  stop=False)
                        last = pe.matmul(bank_mix[rows, P:T], x_rows[:, 1, head], decay[:, e, T:T + P],
                                         start=False, stop=True)
                    last.then_inc(ssm_out, 1)
                elif kind == "v_norm":
                    sum_begins(job)
                    pe.wait_ge(v_sum_ready, A_HEADS)
                    for t in range(TT):
                        last = pe.matmul(bank_sum[:, t:t + 1], v_sum[:, t * P:(t + 1) * P], ones[:, 0:1],
                                         start=True, stop=True)
                    last.then_inc(summed, 1)
                elif kind == "group_norm":
                    sum_begins(job)
                    pe.wait_ge(y_sum_ready, GROUP_PAIRS * (k + 1))
                    pe.matmul(bank_sum[:, 0:T], ones[:], y_sum[:, k, :], start=True,
                              stop=True).then_inc(summed, 1)
                elif kind == "gating":
                    sum_begins(job)
                    pe.wait_ge(v_rows_ready, TT)
                    for c in range(TT):
                        last = pe.matmul(bank_sum[:, c * P:(c + 1) * P], v_rows[:, c, k * P:(k + 1) * P],
                                         w_cols[:, k, :], start=True, stop=True)
                    last.then_inc(summed, 1)

            n0, s0, t0, p0 = phase("proj")
            for i in range(W_TILES):
                at_least(pe, acc_read, t0 + i - 1)
                chunk(n0 + i, s0 + i, KD, xg, 0, acc[(p0 + i) % 2][:, 0, :], True, True,
                      wait_for=(lambda k: pe.wait_ge(xg_ready, KD + k + 1)) if i == 0 else None)
                if i == 0:
                    pre_sums(1)
                for job in JOBS[i]:
                    mixer_job(*job)

            n0, s0, t0, p0 = phase("wout")
            order = list(range(A_HEADS, KD)) + list(range(A_HEADS))

            def mixed_ready(k):
                if k == order[0]:
                    pe.wait_ge(yb_ready, GROUPS)
                if k == 0:
                    pe.wait_ge(ya_ready, A_HEADS)

            with pe.Fori(0, KD // 4) as i:
                for u in range(4):
                    at_least(pe, acc_read, i * 4 + (t0 + u - 1))
                    chunk(i * 4 + (n0 + u), s0 + u, KD, mixed, 0, acc[(p0 + u) % 2][:, 0, :], True, True,
                          order=order, wait_for=mixed_ready)
            post_sums(1)
            ffn(1, "gate2", "down2")
            for g in range(4):
                pe.wait_ge(x_ready, 12 + g + 1)
                for t in range(TT):
                    n = 2 * g + t
                    if n == 3:
                        pe.wait_ge(variance_ready, 6)
                    if n >= 4:
                        pe.wait_ge((out_copied, out_copied_act)[t], g - 1)
                    for k in range(4):
                        last = transpose(end_banks[n % 4][:, k * P:(k + 1) * P],
                                         x[:, 4 * g + k, t * P:(t + 1) * P])
                    last.then_inc(out_turned, 1)


_INS = ["x", "ffn1_norm_pre", "ffn1_norm_post", "ffn1_w_gate", "ffn1_w_up", "ffn1_w_down",
        "mix_norm_pre", "mix_norm_post", "w_in", "sgu_norm", "w_spatial", "b_spatial", "conv_w",
        "conv_b", "dt_bias", "a_log", "d_skip", "ssm_norm", "w_out", "ffn2_norm_pre",
        "ffn2_norm_post", "ffn2_w_gate", "ffn2_w_up", "ffn2_w_down"]


def kernel(**inputs):
    import numpy as np
    import concourse.bacc as bacc
    from concourse.bass_utils import run_bass_kernel_spmd

    nc = bacc.Bacc("TRN2", target_bir_lowering=False, num_devices=1, dynamic_dma_scratch_size=1024)
    arrays, args = {}, []
    for name in _INS:
        a = np.ascontiguousarray(inputs[name])
        arrays[f"in_{name}"] = a
        args.append(nc.dram_tensor(f"in_{name}", a.shape, mybir.dt.from_np(a.dtype), kind="ExternalInput").ap())
    shape = inputs["x"].shape
    out = nc.dram_tensor("out_x", shape, F32, kind="ExternalOutput").ap()
    hybrid_block(nc, *args, out)
    result = run_bass_kernel_spmd(nc, [arrays], core_ids=[0])
    return result.results[0]["out_x"]
```

```python
import concourse.bass as bass
from concourse import mybir
from contextlib import ExitStack

F32 = mybir.dt.float32
F32R = mybir.dt.float32r
ACT = mybir.ActivationFunctionType
ALU = mybir.AluOpType

P = 128
EPS = 1e-6
RAW_SLOTS = 4
CHUNK = 16


def hybrid_block(nc, x_in, f1_pre, f1_post, f1_gate, f1_up, f1_down, mix_pre, mix_post, w_in,
                 sgu_norm, w_spatial, b_spatial, conv_w, conv_b, dt_bias, a_log, d_skip, ssm_norm,
                 w_out, f2_pre, f2_post, f2_gate, f2_up, f2_down, out):
    T, D = x_in.shape[1], x_in.shape[2]
    TT = T // P
    KD = D // P
    KF = f1_gate.shape[2] // P
    A_HEADS = w_spatial.shape[1]
    A_WIDTH = A_HEADS * P
    SSM_HEADS = dt_bias.shape[1]
    PAIRS = SSM_HEADS // 2
    B_WIDTH = PAIRS * P
    CONV_TILES = conv_b.shape[1] // P
    TAPS = conv_w.shape[1]
    PAD = TAPS - 1
    GROUPS = (CONV_TILES - PAIRS) // 2
    GROUP_PAIRS = PAIRS // GROUPS
    COL_U, COL_V, COL_Z = 0, A_WIDTH, 2 * A_WIDTH
    COL_CONV = COL_Z + B_WIDTH
    DT_ROW = P - SSM_HEADS
    COL_DT_WINDOW = w_in.shape[2] - P
    assert (T, D, TT, KD, A_HEADS, PAIRS, CONV_TILES, GROUPS) == (256, 2048, 2, 16, 8, 8, 12, 2)

    DOWN = [KF // 4 + (1 if c < KF % 4 else 0) for c in range(4)]
    DOWN_AT = [sum(DOWN[:c]) for c in range(4)]

    W_TILES = 1 + CONV_TILES + A_HEADS + PAIRS + A_HEADS
    n, t, first = 0, 0, {}
    for name, tiles, chunks in (("gate1", KF, 2 * KF), ("down1", KD, 4 * KD), ("proj", W_TILES, W_TILES),
                                ("wout", KD, KD), ("gate2", KF, 2 * KF), ("down2", KD, 4 * KD)):
        first[name] = (n, t)
        n, t = n + chunks, t + tiles
    CHUNKS = n

    def blocks_of(n):
        for name in ("down1", "down2"):
            if 0 <= n - first[name][0] < 4 * KD:
                return DOWN[(n - first[name][0]) % 4]
        return CHUNK

    PROJ = [("dt", 0, COL_DT_WINDOW)]
    PROJ += [("conv", c, COL_CONV + c * P) for c in range(CONV_TILES)]
    PROJ += [("v", h, COL_V + h * P) for h in range(A_HEADS)]
    PROJ += [("z", q, COL_Z + q * P) for q in range(PAIRS)]
    PROJ += [("u", h, COL_U + h * P) for h in range(A_HEADS)]
    AT = {(kind, index): i for i, (kind, index, _) in enumerate(PROJ)}

    JOBS = {i: [] for i in range(W_TILES)}
    JOBS[3] += [("dt_rows", 0)]
    JOBS[4] += [("spatial_w", 0), ("dt_log", 0)]
    JOBS[5] += [("spatial_w", 1)]
    JOBS[6] += [("dt", 0)]
    JOBS[7] += [("decay_sum", 0)]
    for c in range(PAIRS):
        JOBS[AT["conv", c] + 5] += [("x_rows", c)]
    for h in range(A_HEADS):
        JOBS[AT["v", h] + 1] += [("v_rows", h)]
        JOBS[AT["u", h]] += [("gating", h)]
    SCORES_AT = AT["conv", CONV_TILES - 1] + 2
    for g in range(GROUPS):
        JOBS[SCORES_AT + g] += [("scores", g)]
        JOBS[AT["z", (g + 1) * GROUP_PAIRS - 1] + 2] += [("group_norm", g)]
    JOBS[AT["v", A_HEADS - 1] + 2] += [("v_norm", 0)]
    for q in range(PAIRS):
        diag_at = 7 + 3 * (q // 2) + q % 2
        JOBS[diag_at] += [("diag", q)]
        JOBS[diag_at + 1] += [("decay", q)]
        if q % 2 == 1:
            JOBS[diag_at + 2] += [("decay_exp", q // 2)]
        JOBS[SCORES_AT + 1 + q] += [("masked", q)]
        JOBS[SCORES_AT + 2 + q] += [("mix", q)]
    JOB_ORDER = [job for i in range(W_TILES) for job in JOBS[i]]
    TURNS = [j for j in JOB_ORDER if j[0] in ("dt_rows", "spatial_w", "x_rows", "v_rows")]
    SUMS = [j for j in JOB_ORDER if j[0] in ("decay_sum", "scores", "v_norm", "group_norm")]

    PARAM_ROWS = [("f1_pre", f1_pre), ("f1_post", f1_post), ("mix_pre", mix_pre), ("mix_post", mix_post),
                  ("f2_pre", f2_pre), ("f2_post", f2_post), ("sgu", sgu_norm), ("ssm", ssm_norm),
                  ("conv_b", conv_b)]
    col, column = 0, {}
    for name, vector in PARAM_ROWS:
        column[name] = col
        col += vector.shape[1] // P
    FIRST_ROWS = col
    column["conv_w"] = col
    PARAMS = col + TAPS * CONV_TILES
    assert FIRST_ROWS <= P and TAPS * CONV_TILES <= P

    ctx = ExitStack()
    with ctx:
        at = [(nc.sbuf_base + 31) // 32 * 32]

        def place(name, shape, dtype=F32, offset=None):
            size = 4
            for s in shape[1:]:
                size *= s
            if offset is None:
                offset = at[0]
                at[0] += (size + 31) // 32 * 32
            return nc.alloc_sbuf_tensor_at(name, shape, dtype, offset=offset)

        raw = place("raw", [P, RAW_SLOTS, CHUNK, P])
        high = place("high", [P, 2, CHUNK, P], F32R)
        low = place("low", [P, 2, CHUNK, P], F32R)
        x = place("x", [P, KD, T])
        xg = place("xg", [P, KD, 2 * T], F32R)
        y_at = at[0]
        y = place("y", [P, KD, T])
        low_half = place("low_half", [P, 2, T])
        gate_up = place("gate_up", [P, 2, T])
        total = place("total", [P, T])
        pre_scale = place("pre_scale", [P, T])
        ident = place("ident", [P, P])
        root_table_scratch = place("root_table_scratch", [P, 1])
        ones = place("ones", [P, P])
        params = place("params", [P, PARAMS])
        h_at = at[0]
        h = place("h", [P, KF, 2 * T], F32R)
        h_end = at[0]
        square_sum = gate_up[:, 0, :]
        squares = gate_up[:, 1, :]

        at[0] = h_at
        mixed = place("mixed", [P, KD, 2 * T], F32R)
        mixed_end = at[0]
        TILE = 2 * T * 4
        at[0] = h_at
        token_inverse = place("token_inverse", [P, TT])
        token_scale = place("token_scale", [P, TT])
        scale_diag = place("scale_diag", [P, TT, P])
        at[0] = h_at + 6 * TILE
        x_squares = place("x_squares", [P, KD, T])
        w_rows = place("w_rows", [P, A_HEADS, P])
        assert at[0] <= mixed_end
        decay_group = [place("decay_group0", [P, GROUP_PAIRS, 2, T + P], offset=h_at + 8 * TILE),
                       place("decay_group1", [P, GROUP_PAIRS, 2, T + P], offset=h_at)]
        at[0] = mixed_end
        causal = place("causal", [P, P])
        x_rows = place("x_rows", [P, TT, B_WIDTH])
        w_cols = place("w_cols", [P, A_HEADS, P])
        b_rows = place("b_rows", [P, A_HEADS, P])
        scores = place("scores", [P, GROUPS, T + P])
        diag = place("diag", [P, 2, TT, P])
        conv_in = place("conv_in", [P, 2, T + 8])
        conv = place("conv", [P, T])
        b_state = place("b_state", [P, GROUPS, T])
        c_state = place("c_state", [P, GROUPS, T])
        proj = place("proj", [P, 2, T])
        z_gate = place("z_gate", [P, 2, T])
        v_act = place("v_act", [P, 2, T])
        v_square = place("v_square", [P, T])
        v_gain = place("v_gain", [P, 2, T])
        u_act = place("u_act", [P, 2, T])
        v_sum = place("v_sum", [P, T])
        y_square = place("y_square", [P, T])
        y_sum = place("y_sum", [P, GROUPS, T])
        group_var = place("group_var", [P, T])
        group_scale = place("group_scale", [P, T])
        gated = place("gated", [P, T])
        HT = [P, SSM_HEADS, TT]
        dt_bias_rows = place("dt_bias_rows", [P, SSM_HEADS])
        a_rows = place("a_rows", [P, SSM_HEADS])
        skip = place("skip", [P, PAIRS])
        dt_raw, dt_abs, dt_exp, dt_one, dt_log, dt_den, dt_zero, dt, dt_a, decay_sum = (
            place(name, HT) for name in ("dt_raw", "dt_abs", "dt_exp", "dt_one", "dt_log", "dt_den",
                                         "dt_zero", "dt", "dt_a", "decay_sum"))
        v_var = place("v_var", [P, TT])
        v_scale = place("v_scale", [P, TT])
        assert at[0] <= h_end, (at[0], h_end)
        x_conv = place("x_conv", [P, PAIRS, T], offset=y_at)
        v_rows = place("v_rows", [P, TT, A_WIDTH], offset=y_at + 4 * PAIRS * T)
        at[0] = mixed_end
        x_nat = place("x_nat", [P, TT, D])
        out_nat = place("out_nat", [P, TT, D])
        params_nat = place("params_nat", [P, 2, P])
        assert at[0] <= h_end

        def psum(name, shape):
            return ctx.enter_context(nc.psum_tensor(name, shape, F32))

        acc = [psum("acc0", [P, 2, 512]), psum("acc1", [P, 2, 512])]
        bank_turn = psum("bank_turn", [P, 512])
        bank_decay = psum("bank_decay", [P, 512])
        bank_mix = psum("bank_mix", [P, 512])
        bank_sum = psum("bank_sum", [P, 512])
        bank_spread = bank_mix
        bank_gate = bank_decay
        end_banks = [bank_turn, bank_decay, bank_mix, bank_sum]

        def sem(name):
            return ctx.enter_context(nc.semaphore(name))

        raw_loaded = [sem(f"raw_loaded{s}") for s in range(RAW_SLOTS)]
        high_ready, low_ready, high_used, low_used = (
            sem(s) for s in ("high_ready", "low_ready", "high_used", "low_used"))
        low_half_ready, acc_read = sem("low_half_ready"), sem("acc_read")
        scaled_ready, silu_ready, product_ready, h_high_ready, h_ready = (
            sem(s) for s in ("scaled_ready", "silu_ready", "product_ready", "h_high_ready", "h_ready"))
        squares_ready, square_sum_ready = sem("squares_ready"), sem("square_sum_ready")
        row_sums, variance_ready, inverse_ready, root_ready, diag_made, scale_spread = (
            sem(s) for s in ("row_sums", "variance_ready", "inverse_ready", "root_ready", "diag_made",
                             "scale_spread"))
        pre_scale_ready = sem("pre_scale_ready")
        y_ready, y_scaled, x_ready = sem("y_ready"), sem("y_scaled"), sem("x_ready")
        xg_high_ready, xg_ready = sem("xg_high_ready"), sem("xg_ready")
        x_squares_ready, last_squares_ready, x_square_sum_ready = (
            sem(s) for s in ("x_squares_ready", "last_squares_ready", "x_square_sum_ready"))
        x_loaded = [sem(f"x_loaded{q}") for q in range(4)]
        consts_ready, params_cleared, params_loaded, params_turned, params_ready = (
            sem(s) for s in ("consts_ready", "params_cleared", "params_loaded",
                             "params_turned", "params_ready"))
        root_table = sem("root_table")
        x_turned, out_turned, out_copied, out_copied_act, stored = (
            sem(s) for s in ("x_turned", "out_turned", "out_copied", "out_copied_act", "stored"))
        mixer_loaded, masks_ready, w_masked = sem("mixer_loaded"), sem("masks_ready"), sem("w_masked")
        proj_ready, conv_started, conv_step, conv_act_ready = (
            sem(s) for s in ("proj_ready", "conv_started", "conv_step", "conv_act_ready"))
        turned, turn_read = sem("turned"), sem("turn_read")
        summed, sum_read = sem("summed"), sem("sum_read")
        gate_summed, gate_read, last_u_ready = sem("gate_summed"), sem("gate_read"), sem("last_u_ready")
        dt_step_dve, dt_step_act, dt_ready, da_ready = (
            sem(s) for s in ("dt_step_dve", "dt_step_act", "dt_ready", "da_ready"))
        diag_ready, decay_spread, decay_clamped, decay_exp, decay_ready, x_dt_ready = (
            sem(s) for s in ("diag_ready", "decay_spread", "decay_clamped", "decay_exp", "decay_ready",
                             "x_dt_ready"))
        ssm_out, ssm_read, z_ready, y_gated, y_square_ready, y_sum_ready = (
            sem(s) for s in ("ssm_out", "ssm_read", "z_ready", "y_gated", "y_square_ready", "y_sum_ready"))
        group_step, group_inverse, group_scale_ready, yb_normed, yb_high_ready, yb_ready = (
            sem(s) for s in ("group_step", "group_inverse", "group_scale_ready", "yb_normed",
                             "yb_high_ready", "yb_ready"))
        v_act_ready, v_square_ready, v_gain_ready, v_sum_ready = (
            sem(s) for s in ("v_act_ready", "v_square_ready", "v_gain_ready", "v_sum_ready"))
        v_step, v_inverse, v_scale_ready, v_rows_ready = (
            sem(s) for s in ("v_step", "v_inverse", "v_scale_ready", "v_rows_ready"))
        u_ready, ya_step, ya_raw_ready, ya_high_ready, ya_ready = (
            sem(s) for s in ("u_ready", "ya_step", "ya_raw_ready", "ya_high_ready", "ya_ready"))

        block = ctx.enter_context(nc.Block())

        def at_least(eng, s, value):
            if not (isinstance(value, int) and value <= 0):
                eng.wait_ge(s, value)

        def f32(ap):
            return ap.bitcast(F32)

        def spread(ap, shape, *axes):
            for a in axes:
                ap = ap.unsqueeze(a)
            return ap.to_broadcast(shape)

        def proj_acc(i):
            last = W_TILES - 1
            return (phase("proj")[3] + last + last // 2 - i // 2) % 2, i % 2

        def param(name, index):
            c = column[name] + index
            return params[:, c:c + 1]

        def phase(name):
            n0, t0 = first[name]
            return n0, n0 % RAW_SLOTS, t0, t0 % 2

        PRE = {"gate1": 0, "proj": 1, "gate2": 2}
        FFNS = [("gate1", "down1", f1_gate, f1_up, f1_down), ("gate2", "down2", f2_gate, f2_up, f2_down)]
        POST = [("down1", "f1_post", 0.25), ("wout", "mix_post", 1.0), ("down2", "f2_post", 0.25)]
        GAIN = ["f1_pre", "mix_pre", "f2_pre"]
        PAIR_ROUNDS = (KF - 2) // 2
        REST = list(range(1 + 2 * PAIR_ROUNDS, KF))
        GROUP = 2
        X_GROUPS = KD // GROUP

        def x_tiles(g):
            return slice(GROUP * g, GROUP * (g + 1))

        @block.sync
        def _(sp):
            def load(n, s, source, blocks):
                s %= RAW_SLOTS
                at_least(sp, low_ready, n - (RAW_SLOTS - 1))
                sp.dma_start(raw[:, s, 0:blocks, :], source).then_inc(raw_loaded[s], 16)

            def rows(w):
                return w[0].rearrange("(k p) f -> p k f", p=P)

            def gate_up_tile(n, s, gate, up, j):
                load(n, s, rows(gate)[:, :, bass.ds(j * P, P)], KD)
                load(n + 1, s + 1, rows(up)[:, :, bass.ds(j * P, P)], KD)

            def ffn(gate_phase, down_phase, gate, up, down):
                n0, s0, _, _ = phase(gate_phase)
                for j in range(3):
                    gate_up_tile(n0 + 2 * j, s0 + 2 * j, gate, up, j)
                with sp.Fori(1, PAIR_ROUNDS) as i:
                    for u in (1, 2):
                        gate_up_tile(i * 4 + (n0 + 2 * u), s0 + 2 * u, gate, up, i * 2 + u)
                for j in REST:
                    gate_up_tile(n0 + 2 * j, s0 + 2 * j, gate, up, j)
                n0, s0, _, _ = phase(down_phase)
                with sp.Fori(0, KD) as d:
                    for c in range(4):
                        load(d * 4 + (n0 + c), s0 + c,
                             rows(down)[:, DOWN_AT[c]:DOWN_AT[c] + DOWN[c], bass.ds(d * P, P)], DOWN[c])

            for q in range(4):
                cols = slice(q * (D // 4), (q + 1) * (D // 4))
                sp.dma_start(x_nat[:, :, cols], x_in[0].rearrange("(t p) d -> p t d", p=P)[:, :, cols]
                             ).then_inc(x_loaded[q], 16)
            ffn(*FFNS[0])
            n0, s0, _, _ = phase("proj")
            for i, (_, _, c) in enumerate(PROJ):
                load(n0 + i, s0 + i, rows(w_in)[:, :, c:c + P], KD)
            n0, s0, _, _ = phase("wout")
            with sp.Fori(0, KD // 4) as i:
                for u in range(4):
                    load(i * 4 + (n0 + u), s0 + u, rows(w_out)[:, :, bass.ds(i * (4 * P) + u * P, P)], KD)
            ffn(*FFNS[1])
            out_rows = out[0].rearrange("(t p) d -> p t d", p=P)
            for g in range(4):
                cols = slice(g * 4 * P, (g + 1) * 4 * P)
                sp.wait_ge(out_copied, g + 1)
                sp.dma_start(out_rows[:, 0, cols], out_nat[:, 0, cols]).then_inc(stored, 16)
                sp.wait_ge(out_copied_act, g + 1)
                sp.dma_start(out_rows[:, 1, cols], out_nat[:, 1, cols]).then_inc(stored, 16)
            sp.wait_ge(stored, 8 * 16)

        @block.scalar
        def _(act):
            def split_high(n, s, blocks):
                s %= RAW_SLOTS
                act.wait_ge(raw_loaded[s], n * 4 + (16 - 4 * s))
                at_least(act, high_used, n - 1)
                at_least(act, low_ready, n - 1)
                act.activation(high[:, s % 2, 0:blocks, :], raw[:, s, 0:blocks, :],
                               ACT.Copy).then_inc(high_ready, 1)

            def take_low_half(n_end, t, parity, banks, first_bank=0):
                act.wait_ge(low_used, n_end + 1)
                at_least(act, acc_read, t)
                act.activation(low_half[:, 0:banks, :],
                               acc[parity % 2][:, first_bank:first_bank + banks, T:2 * T],
                               ACT.Copy).then_inc(low_half_ready, 1)

            def hidden_tile(n, s, t, parity, j, f, blocks, norm=None):
                split_high(n + 2, s + 2, blocks[0])
                take_low_half(n + 1, t, parity, 2)
                split_high(n + 3, s + 3, blocks[1])
                if norm is not None:
                    root(2 * norm, 1.0)
                act.wait_ge(scaled_ready, f + 1)
                act.activation(gate_up[:, 0, :], gate_up[:, 0, :], ACT.Silu).then_inc(silu_ready, 1)
                act.wait_ge(product_ready, f + 1)
                act.activation(h[:, bass.ds(j, 1), 0:T], total[:].unsqueeze(1),
                               ACT.Copy).then_inc(h_high_ready, 1)

            def result_tile(n_end, t, parity, d, r, gain, split, norm=None):
                if norm is not None:
                    b, scale = norm
                    act.activation(root_table_scratch[:], ones[:, 0:1], ACT.Sqrt).then_inc(root_table, 1)
                    act.wait_ge(root_table, b + 1)
                take_low_half(n_end, t, parity, 1)
                if norm is None and split is not None:
                    split_high(*split)
                act.wait_ge(acc_read, t + 1)
                at_least(act, square_sum_ready, r)
                act.activation(squares, total[:], ACT.Square).then_inc(squares_ready, 1)
                if norm is not None:
                    root(2 * b + 1, scale)
                act.activation(y[:, bass.ds(d, 1), :], total[:].unsqueeze(1), ACT.Copy,
                               scale=gain(d)).then_inc(y_ready, 1)
                if norm is not None and split is not None:
                    split_high(*split)

            def root(m, scale):
                act.wait_ge(inverse_ready, m + 1)
                act.activation(token_scale[:], token_inverse[:], ACT.Sqrt, scale=scale).then_inc(root_ready, 1)

            def pre_norm(p):
                for g in range(X_GROUPS):
                    act.wait_ge(x_ready, X_GROUPS * p + g + 1)
                    for k in range(GROUP * g, GROUP * (g + 1)):
                        act.activation(xg[:, k, 0:T], x[:, k, :], ACT.Copy,
                                       scale=param(GAIN[p], k)).then_inc(xg_high_ready, 1)
                    if 0 < g:
                        act.activation(x_squares[:, x_tiles(g - 1), :], x[:, x_tiles(g - 1), :],
                                       ACT.Square).then_inc(x_squares_ready, 1)

            def ffn(which, gate_phase, down_phase, post_name):
                n0, s0, t0, p0 = phase(gate_phase)
                p = PRE[gate_phase]
                pre_norm(p)
                hidden_tile(n0, s0, t0, p0, 0, which * KF, [CHUNK, CHUNK], norm=p)
                with act.Fori(0, PAIR_ROUNDS) as i:
                    for u in (1, 2):
                        hidden_tile(i * 4 + (n0 + 2 * u), s0 + 2 * u, i * 2 + (t0 + u), p0 + u,
                                    i * 2 + u, i * 2 + (which * KF + u), [CHUNK, CHUNK])
                for j in REST:
                    hidden_tile(n0 + 2 * j, s0 + 2 * j, t0 + j, p0 + j, j, which * KF + j,
                                [CHUNK, CHUNK] if j < KF - 1 else DOWN[0:2])
                down(which, down_phase, post_name)

            def down(which, down_phase, post_name):
                n0, s0, t0, p0 = phase(down_phase)
                b = 2 * which
                r0 = b * (KD - 1)

                def tile(n, s, t, parity, d, r, gain, after, norm=None):
                    split_high(n + 2, s + 2, DOWN[2])
                    split_high(n + 3, s + 3, DOWN[3])
                    if after is not None:
                        split_high(n + 4, s + 4, after[0])
                    result_tile(n + 3, t, parity, d, r, gain,
                                None if after is None else (n + 5, s + 5, after[1]), norm)

                def gain_at(d):
                    c = column[post_name]
                    return params[:, bass.ds(d + c, 1)]

                with act.Fori(0, KD // 2 - 1) as i:
                    for u in range(2):
                        tile(i * 8 + (n0 + 4 * u), s0, i * 2 + (t0 + u), p0 + u, i * 2 + u,
                             i * 2 + (r0 + u), gain_at, DOWN[0:2])
                for d in (KD - 2, KD - 1):
                    after = DOWN[0:2] if d < KD - 1 else None if which == 1 else [CHUNK, CHUNK]
                    tile(n0 + 4 * d, s0, t0 + d, p0 + d, d, r0 + d, gain_at, after,
                         (b, POST[b][2]) if d == KD - 1 else None)

            act.wait_ge(params_cleared, 1)
            for name, vector in PARAM_ROWS:
                c, rows = column[name], vector.shape[1] // P
                act.dma_start(params_nat[c:c + rows, 0, :],
                              vector[0].rearrange("(j p) -> j p", p=P)).then_inc(params_loaded, 16)
            act.dma_start(params_nat[0:TAPS * CONV_TILES, 1, :],
                          conv_w[0].rearrange("k (j p) -> (k j) p", p=P)).then_inc(params_loaded, 16)
            split_high(0, 0, CHUNK)
            split_high(1, 1, CHUNK)
            act.wait_ge(params_ready, 1)
            ffn(0, "gate1", "down1", "f1_post")

            pre_norm(1)
            n0, s0, t0, p0 = phase("proj")
            act.dma_start(w_rows[:], w_spatial[0].rearrange("h t s -> t h s")).then_inc(mixer_loaded, 16)
            act.dma_start(b_rows[:].rearrange("p h t -> p (h t)"),
                          b_spatial.rearrange("l h t -> l (h t)").to_broadcast([P, A_HEADS * P])
                          ).then_inc(mixer_loaded, 16)
            act.dma_start(dt_bias_rows[:], dt_bias.to_broadcast([P, SSM_HEADS])).then_inc(mixer_loaded, 16)
            act.dma_start(a_rows[:], a_log.to_broadcast([P, SSM_HEADS])).then_inc(mixer_loaded, 16)
            for e in range(2):
                act.dma_start(skip[64 * e:64 * e + 64, :],
                              d_skip[0:1, e:SSM_HEADS:2].to_broadcast([64, PAIRS]),
                              allow_slow_non_contiguous=True).then_inc(mixer_loaded, 16)

            def activate(i):
                kind, k, _ = PROJ[i]
                if kind == "dt":
                    return
                if i < W_TILES - 1:
                    act.wait_ge(proj_ready, i + 1)
                else:
                    act.wait_ge(last_u_ready, 1)
                if kind == "conv":
                    at_least(act, conv_act_ready, k)
                    act.activation(conv[:], conv_in[:, k % 2, 0:T], ACT.Identity,
                                   scale=param("conv_w", k), bias=param("conv_b", k)
                                   ).then_inc(conv_started, 1)
                elif kind == "z":
                    at_least(act, y_gated, k - 1)
                    act.activation(z_gate[:, k % 2, :], proj[:, i % 2, :], ACT.Silu).then_inc(z_ready, 1)
                elif kind == "v":
                    at_least(act, v_square_ready, k - 1)
                    act.activation(v_act[:, k % 2, :], proj[:, i % 2, :], ACT.Gelu).then_inc(v_act_ready, 1)
                    act.wait_ge(v_act_ready, k + 1)
                    if k >= 2:
                        act.wait_ge(turned, TURNS.index(("v_rows", k - 2)) + 1)
                    act.activation(v_gain[:, k % 2, :], v_act[:, k % 2, :], ACT.Copy,
                                   scale=param("sgu", k)).then_inc(v_gain_ready, 1)
                elif kind == "u":
                    at_least(act, ya_raw_ready, k - 1)
                    act.activation(u_act[:, k % 2, :], proj[:, i % 2, :], ACT.Gelu).then_inc(u_ready, 1)

            def conv_silu(c):
                act.wait_ge(conv_step, PAD * (c + 1))
                to = (x_conv[:, c, :] if c < PAIRS else b_state[:, c - PAIRS, :]
                      if c < PAIRS + GROUPS else c_state[:, c - PAIRS - GROUPS, :])
                act.activation(to, conv[:], ACT.Silu).then_inc(conv_act_ready, 1)

            def mixer_job(kind, k):
                if kind == "dt_rows":
                    act.wait_ge(turn_read, TURNS.index((kind, k)) + 1)
                    act.activation(dt_abs[:], dt_raw[:], ACT.Abs).then_inc(dt_step_act, 1)
                    act.wait_ge(dt_step_act, 1)
                    act.activation(dt_exp[:], dt_abs[:], ACT.Exp, scale=-1.0).then_inc(dt_step_act, 1)
                    act.wait_ge(mixer_loaded, 6 * 16)
                    act.activation(a_rows[:], a_rows[:], ACT.Exp).then_inc(dt_step_act, 1)
                elif kind == "dt":
                    act.wait_ge(dt_step_dve, 1)
                    act.activation(dt_log[:], dt_one[:], ACT.Ln).then_inc(dt_step_act, 1)
                elif kind in ("x_rows", "v_rows"):
                    n = TURNS.index((kind, k))
                    act.wait_ge(turned, n + 1)
                    to = x_rows if kind == "x_rows" else v_rows
                    act.activation(to[:, :, k * P:(k + 1) * P],
                                   bank_turn[:, 0:TT * P].rearrange("p (t d) -> p t d", t=TT),
                                   ACT.Copy).then_inc(turn_read, 1)
                elif kind == "decay_exp":
                    act.wait_ge(decay_clamped, 2 * k + 2)
                    pairs = decay_group[2 * k // GROUP_PAIRS]
                    q = 2 * k % GROUP_PAIRS
                    act.activation(pairs[:, q:q + 2], pairs[:, q:q + 2], ACT.Exp).then_inc(decay_exp, 1)
                elif kind == "v_norm":
                    act.wait_ge(v_inverse, 1)
                    act.activation(v_scale[:], v_var[:], ACT.Sqrt).then_inc(v_scale_ready, 1)
                elif kind == "group_norm":
                    act.wait_ge(group_inverse, k + 1)
                    act.activation(group_scale[:], group_var[:], ACT.Sqrt).then_inc(group_scale_ready, 1)
                    act.wait_ge(yb_normed, GROUP_PAIRS * (k + 1))
                    qs = slice(k * GROUP_PAIRS, (k + 1) * GROUP_PAIRS)
                    act.activation(mixed[:, PAIRS + k * GROUP_PAIRS:PAIRS + (k + 1) * GROUP_PAIRS, 0:T],
                                   x_conv[:, qs, :], ACT.Copy).then_inc(yb_high_ready, 1)
                elif kind == "gating":
                    act.wait_ge(ya_raw_ready, k + 1)
                    act.activation(mixed[:, k, 0:T], gated[:], ACT.Copy).then_inc(ya_high_ready, 1)

            for i in range(W_TILES):
                if i == 0:
                    split_high(n0 + i + 2, s0 + i + 2, CHUNK)
                accumulator, bank = proj_acc(i)
                take_low_half(n0 + i, t0 + i, accumulator, 1, bank)
                if i >= 1 and PROJ[i - 1][0] == "conv":
                    conv_silu(PROJ[i - 1][1])
                if i == 0:
                    root(2, 1.0)
                elif i < W_TILES - 1:
                    split_high(n0 + i + 2, s0 + i + 2, CHUNK)
                activate(i)
                for job in JOBS[i]:
                    mixer_job(*job)
            split_high(n0 + W_TILES + 1, s0 + W_TILES + 1, CHUNK)

            n0, s0, t0, p0 = phase("wout")
            c = column["mix_post"]

            def out_tile(n, s, t, parity, d, r, norm=None):
                result_tile(n, t, parity, d, r, lambda d: params[:, bass.ds(d + c, 1)],
                            (n + 2, s + 2, CHUNK), norm)

            with act.Fori(0, KD // 4 - 1) as i:
                for u in range(4):
                    out_tile(i * 4 + (n0 + u), s0 + u, i * 4 + (t0 + u), p0 + u, i * 4 + u,
                             i * 4 + (KD - 1 + u))
            for d in range(KD - 4, KD):
                out_tile(n0 + d, s0 + d, t0 + d, p0 + d, d, KD - 1 + d,
                         (1, POST[1][2]) if d == KD - 1 else None)
            ffn(1, "gate2", "down2", "f2_post")
            for g in range(4):
                act.wait_ge(out_turned, 2 * g + 2)
                act.activation(out_nat[:, 1, g * 512:(g + 1) * 512], end_banks[(2 * g + 1) % 4][:],
                               ACT.Copy).then_inc(out_copied_act, 1)

        @block.vector
        def _(dve):
            def split_low(n, s, blocks):
                s %= RAW_SLOTS
                dve.wait_ge(high_ready, n + 1)
                at_least(dve, low_used, n - 1)
                dve.tensor_tensor(low[:, s % 2, 0:blocks, :], raw[:, s, 0:blocks, :],
                                  f32(high[:, s % 2, 0:blocks, :]), ALU.subtract).then_inc(low_ready, 1)

            def hidden_tile(n, s, t, parity, j, f, blocks, norm=None):
                split_low(n + 2, s + 2, blocks[0])
                dve.wait_ge(low_half_ready, t + 1)
                dve.tensor_tensor(gate_up[:], acc[parity % 2][:, :, 0:T], low_half[:],
                                  ALU.add).then_inc(acc_read, 1)
                if norm is not None:
                    scale_diagonal(2 * norm)
                    split_low(n + 3, s + 3, blocks[1])
                    take_pre_scale(norm)
                dve.wait_ge(acc_read, t + 1)
                dve.tensor_tensor(gate_up[:], gate_up[:], spread(pre_scale[:], [P, 2, T], 1),
                                  ALU.mult).then_inc(scaled_ready, 1)
                if norm is None:
                    split_low(n + 3, s + 3, blocks[1])
                dve.wait_ge(silu_ready, f + 1)
                dve.tensor_tensor(total[:], gate_up[:, 0, :], gate_up[:, 1, :],
                                  ALU.mult).then_inc(product_ready, 1)
                dve.wait_ge(h_high_ready, f + 1)
                dve.tensor_tensor(h[:, bass.ds(j, 1), T:2 * T], total[:].unsqueeze(1),
                                  f32(h[:, bass.ds(j, 1), 0:T]), ALU.subtract).then_inc(h_ready, 1)

            def result_tile(t, parity, r):
                dve.wait_ge(low_half_ready, t + 1)
                at_least(dve, squares_ready, r)
                dve.tensor_tensor(total[:], acc[parity % 2][:, 0, 0:T], low_half[:, 0, :],
                                  ALU.add).then_inc(acc_read, 1)

            def scale_diagonal(m):
                dve.wait_ge(row_sums, m + 1)
                dve.tensor_scalar(token_inverse[:], bank_sum[:, 0:TT], 1.0 / D, EPS, ALU.mult,
                                  ALU.add).then_inc(variance_ready, 1)
                dve.wait_ge(variance_ready, m + 1)
                dve.reciprocal(token_inverse[:], token_inverse[:]).then_inc(inverse_ready, 1)
                dve.wait_ge(root_ready, m + 1)
                for t in range(TT):
                    last = dve.tensor_scalar(scale_diag[:, t, :], ident[:], token_scale[:, t:t + 1], None,
                                             ALU.mult)
                last.then_inc(diag_made, 1)

            def take_pre_scale(p):
                dve.wait_ge(scale_spread, 2 * p + 1)
                dve.tensor_copy(pre_scale[:], bank_spread[:, 0:T]).then_inc(pre_scale_ready, 1)
                dve.wait_ge(pre_scale_ready, p + 1)

            def scale_y(b, g):
                ys = y[:, x_tiles(g), :]
                dve.tensor_tensor(ys, ys, spread(bank_spread[:, 0:T], [P, GROUP, T], 1),
                                  ALU.mult).then_inc(y_scaled, 1)

            def post_norm(b):
                scale_diagonal(2 * b + 1)
                dve.wait_ge(scale_spread, 2 * b + 2)
                dve.wait_ge(y_ready, KD * (b + 1))

            def x_low(p, g):
                for k in range(GROUP * g, GROUP * (g + 1)):
                    dve.wait_ge(xg_high_ready, KD * p + k + 1)
                    dve.scalar_tensor_tensor(xg[:, k, T:2 * T], x[:, k, :], param(GAIN[p], k),
                                             f32(xg[:, k, 0:T]), ALU.mult,
                                             ALU.subtract).then_inc(xg_ready, 1)

            def add_squares(p):
                for c in range(1, 4):
                    if c < 3:
                        dve.wait_ge(x_squares_ready, (X_GROUPS - 1) * p + 2 * c + 2)
                    else:
                        dve.wait_ge(x_squares_ready, (X_GROUPS - 1) * (p + 1))
                        dve.wait_ge(last_squares_ready, p + 1)
                    if c > 1:
                        dve.wait_ge(x_square_sum_ready, 3 * p + c - 1)
                    dve.tensor_tensor(x_squares[:, 0:4, :], x_squares[:, 0:4, :],
                                      x_squares[:, 4 * c:4 * c + 4, :], ALU.add
                                      ).then_inc(x_square_sum_ready, 1)

            AHEAD = 3

            def update(b):
                post_norm(b)
                for g in range(AHEAD):
                    scale_y(b, g)
                n, s = (first["proj"], first["gate2"])[b][0] + 1, (first["proj"], first["gate2"])[b][0] + 1
                split_low(n, s, CHUNK)
                for g in range(X_GROUPS):
                    x_low(b + 1, g)
                    if g + AHEAD < X_GROUPS:
                        scale_y(b, g + AHEAD)
                add_squares(b + 1)

            def ffn(which, gate_phase, down_phase):
                n0, s0, t0, p0 = phase(gate_phase)
                hidden_tile(n0, s0, t0, p0, 0, which * KF, [CHUNK, CHUNK], norm=PRE[gate_phase])
                with dve.Fori(0, PAIR_ROUNDS) as i:
                    for u in (1, 2):
                        hidden_tile(i * 4 + (n0 + 2 * u), s0 + 2 * u, i * 2 + (t0 + u), p0 + u,
                                    i * 2 + u, i * 2 + (which * KF + u), [CHUNK, CHUNK])
                for j in REST:
                    hidden_tile(n0 + 2 * j, s0 + 2 * j, t0 + j, p0 + j, j, which * KF + j,
                                [CHUNK, CHUNK] if j < KF - 1 else DOWN[0:2])
                n0, s0, t0, p0 = phase(down_phase)
                r0 = 2 * which * KD

                def tile(n, s, t, parity, r, after, last=False):
                    split_low(n + 2, s + 2, DOWN[2])
                    split_low(n + 3, s + 3, DOWN[3])
                    if after is not None:
                        split_low(n + 4, s + 4, after[0])
                    result_tile(t, parity, r)
                    if after is not None and not last:
                        split_low(n + 5, s + 5, after[1])

                with dve.Fori(0, KD // 2 - 1) as i:
                    for u in range(2):
                        tile(i * 8 + (n0 + 4 * u), s0, i * 2 + (t0 + u), p0 + u, i * 2 + (r0 + u),
                             DOWN[0:2])
                for d in (KD - 2, KD - 1):
                    after = DOWN[0:2] if d < KD - 1 else None if which == 1 else [CHUNK, CHUNK]
                    tile(n0 + 4 * d, s0, t0 + d, p0 + d, r0 + d, after, d == KD - 1)

            split_low(0, 0, CHUNK)
            split_low(1, 1, CHUNK)
            dve.wait_ge(params_turned, 1)
            dve.tensor_copy(params[:, 0:FIRST_ROWS], bank_sum[:, 0:FIRST_ROWS])
            dve.tensor_copy(params[:, FIRST_ROWS:PARAMS],
                            bank_sum[:, P:P + PARAMS - FIRST_ROWS]).then_inc(params_ready, 1)
            for g in range(X_GROUPS):
                dve.wait_ge(x_turned, g + 1)
                dve.tensor_copy(x[:, x_tiles(g), :],
                                end_banks[g % 4][:].rearrange("p (k t) -> p k t", k=GROUP)
                                ).then_inc(x_ready, 1)
                if g == 0:
                    dve.wait_ge(params_ready, 1)
                dve.wait_ge(x_ready, g + 1)
                if g > 0:
                    x_low(0, g - 1)
            x_low(0, X_GROUPS - 1)
            add_squares(0)
            ffn(0, "gate1", "down1")
            update(0)

            n0, s0, t0, p0 = phase("proj")

            def conv_taps(c):
                dve.wait_ge(conv_started, c + 1)
                for k in range(1, TAPS):
                    at_least(dve, conv_step, PAD * c + k - 1)
                    dve.scalar_tensor_tensor(conv[:], conv_in[:, c % 2, k:k + T],
                                             param("conv_w", k * CONV_TILES + c), conv[:], ALU.mult,
                                             ALU.add).then_inc(conv_step, 1)

            dt_steps = [0]

            def dt_chain(instruction):
                dt_steps[0] += 1
                instruction.then_inc(dt_step_dve, 1)
                dve.wait_ge(dt_step_dve, dt_steps[0])

            def mixer_job(kind, k):
                if kind == "dt_rows":
                    dve.wait_ge(turned, TURNS.index((kind, k)) + 1)
                    dve.wait_ge(mixer_loaded, 6 * 16)
                    dve.tensor_tensor(
                        dt_raw[:],
                        bank_turn[:, 0:TT * P].rearrange("p (t d) -> p d t", t=TT)[:, DT_ROW:P, :],
                        spread(dt_bias_rows[:], HT, 2), ALU.add).then_inc(turn_read, 1)
                elif kind == "dt_log":
                    dve.wait_ge(dt_step_act, 2)
                    dt_chain(dve.tensor_scalar(dt_one[:], dt_exp[:], 1.0, None, ALU.add))
                    dt_chain(dve.tensor_scalar(dt_den[:], dt_one[:], -1.0, None, ALU.add))
                    dt_chain(dve.tensor_scalar(dt_zero[:], dt_den[:], 0.0, None, ALU.is_equal))
                    dt_chain(dve.tensor_tensor(dt_den[:], dt_den[:], dt_zero[:], ALU.add))
                    dt_chain(dve.reciprocal(dt_den[:], dt_den[:]))
                elif kind == "dt":
                    dve.wait_ge(dt_step_act, 4)
                    dt_chain(dve.tensor_tensor(dt_log[:], dt_log[:], dt_den[:], ALU.mult))
                    dt_chain(dve.tensor_tensor(dt_log[:], dt_log[:], dt_zero[:], ALU.add))
                    dt_chain(dve.tensor_tensor(dt_log[:], dt_log[:], dt_exp[:], ALU.mult))
                    dve.scalar_tensor_tensor(dt[:], dt_raw[:], 0.0, dt_log[:], ALU.max,
                                             ALU.add).then_inc(dt_ready, 1)
                    dve.wait_ge(dt_ready, 1)
                    dve.scalar_tensor_tensor(dt_a[:], dt[:], -1.0, spread(a_rows[:], HT, 2), ALU.mult,
                                             ALU.mult).then_inc(da_ready, 1)
                elif kind == "spatial_w":
                    dve.wait_ge(turned, TURNS.index((kind, k)) + 1)
                    dve.tensor_copy(w_cols[:, 4 * k:4 * k + 4, :],
                                    bank_turn[:].rearrange("p (h t) -> p h t", h=4)).then_inc(turn_read, 1)
                elif kind == "decay_sum":
                    dve.wait_ge(summed, SUMS.index((kind, k)) + 1)
                    sums = bank_sum[:, 0:TT * SSM_HEADS].rearrange("p (t h) -> p h t", t=TT)
                    dve.tensor_copy(decay_sum[:], sums).then_inc(sum_read, 1)
                elif kind == "scores":
                    dve.wait_ge(summed, SUMS.index((kind, k)) + 1)
                    dve.tensor_tensor(scores[:, k, 0:P], bank_sum[:, 0:P], causal[:], ALU.mult)
                    dve.tensor_copy(scores[:, k, P:T], bank_sum[:, P:T])
                    dve.tensor_tensor(scores[:, k, T:T + P], bank_sum[:, T:T + P], causal[:],
                                      ALU.mult).then_inc(sum_read, 1)
                elif kind == "decay":
                    dve.wait_ge(decay_spread, k + 1)
                    decay = decay_group[k // GROUP_PAIRS][:, k % GROUP_PAIRS]
                    for e in range(2):
                        for t, to, source in ((0, slice(0, T), slice(e * T, (e + 1) * T)),
                                              (1, slice(T, T + P), slice(e * T + P, (e + 1) * T))):
                            last = dve.tensor_scalar(decay[:, e, to], bank_decay[:, source],
                                                     decay_sum[:, 2 * k + e, t:t + 1], 0.0,
                                                     ALU.subtract, ALU.min)
                    last.then_inc(decay_clamped, 1)
                elif kind == "masked":
                    decay = decay_group[k // GROUP_PAIRS][:, k % GROUP_PAIRS]
                    dve.wait_ge(decay_exp, k // 2 + 1)
                    dve.tensor_tensor(decay, decay,
                                      spread(scores[:, k // GROUP_PAIRS, :], [P, 2, T + P], 1),
                                      ALU.mult).then_inc(decay_ready, 1)
                elif kind == "mix":
                    dve.wait_ge(ssm_out, k + 1)
                    dve.scalar_tensor_tensor(x_conv[:, k, :], x_conv[:, k, :], skip[:, k:k + 1],
                                             bank_mix[:, 0:T], ALU.mult, ALU.add).then_inc(ssm_read, 1)
                elif kind == "v_norm":
                    dve.wait_ge(summed, SUMS.index((kind, k)) + 1)
                    dve.tensor_scalar(v_var[:], bank_sum[:, 0:TT], 1.0 / A_WIDTH, EPS, ALU.mult,
                                      ALU.add).then_inc(sum_read, 1)
                    dve.wait_ge(sum_read, SUMS.index((kind, k)) + 1)
                    dve.reciprocal(v_var[:], v_var[:]).then_inc(v_inverse, 1)
                    dve.wait_ge(v_scale_ready, 1)
                    for t in range(TT):
                        dve.tensor_scalar(v_rows[:, t, :], v_rows[:, t, :], v_scale[:, t:t + 1], None,
                                          ALU.mult).then_inc(v_rows_ready, 1)
                elif kind == "group_norm":
                    dve.wait_ge(summed, SUMS.index((kind, k)) + 1)
                    dve.tensor_scalar(group_var[:], bank_sum[:, 0:T], 1.0 / (GROUP_PAIRS * P), EPS,
                                      ALU.mult, ALU.add).then_inc(sum_read, 1)
                    dve.wait_ge(sum_read, SUMS.index((kind, k)) + 1)
                    dve.reciprocal(group_var[:], group_var[:]).then_inc(group_inverse, 1)
                    dve.wait_ge(group_scale_ready, k + 1)
                    for q in range(k * GROUP_PAIRS, (k + 1) * GROUP_PAIRS):
                        dve.scalar_tensor_tensor(x_conv[:, q, :], x_conv[:, q, :], param("ssm", q),
                                                 group_scale[:], ALU.mult, ALU.mult).then_inc(yb_normed, 1)
                    dve.wait_ge(yb_high_ready, k + 1)
                    qs = slice(k * GROUP_PAIRS, (k + 1) * GROUP_PAIRS)
                    ks = slice(A_HEADS + k * GROUP_PAIRS, A_HEADS + (k + 1) * GROUP_PAIRS)
                    dve.tensor_tensor(mixed[:, ks, T:2 * T], x_conv[:, qs, :], f32(mixed[:, ks, 0:T]),
                                      ALU.subtract).then_inc(yb_ready, 1)
                elif kind == "gating":
                    dve.wait_ge(gate_summed, k + 1)
                    at_least(dve, ya_ready, k)
                    dve.tensor_tensor(gated[:].rearrange("p (c t) -> p c t", c=TT),
                                      bank_gate[:, 0:T].rearrange("p (c t) -> p c t", c=TT),
                                      spread(b_rows[:, k, :], [P, TT, P], 1), ALU.add).then_inc(gate_read, 1)
                    dve.wait_ge(gate_read, k + 1)
                    dve.wait_ge(u_ready, k + 1)
                    dve.tensor_tensor(gated[:], gated[:], u_act[:, k % 2, :],
                                      ALU.mult).then_inc(ya_raw_ready, 1)
                    dve.wait_ge(ya_high_ready, k + 1)
                    dve.tensor_tensor(mixed[:, k, T:2 * T], gated[:], f32(mixed[:, k, 0:T]),
                                      ALU.subtract).then_inc(ya_ready, 1)

            for i, (kind, k, _) in enumerate(PROJ):
                if i == 0:
                    split_low(n0 + 2, s0 + 2, CHUNK)
                dve.wait_ge(low_half_ready, t0 + i + 1)
                at_least(dve, proj_ready, i - 1)
                accumulator, bank = proj_acc(i)
                dve.tensor_tensor(gate_up[:, i % 2, :], acc[accumulator][:, bank, 0:T], low_half[:, 0, :],
                                  ALU.add).then_inc(acc_read, 1)
                if i == W_TILES - 1:
                    dve.wait_ge(acc_read, t0 + i + 1)
                    dve.wait_ge(u_ready, k - 1)
                    dve.tensor_tensor(proj[:, i % 2, :], gate_up[:, i % 2, :], pre_scale[:],
                                      ALU.mult).then_inc(last_u_ready, 1)
                elif i > 0:
                    split_low(n0 + i + 2, s0 + i + 2, CHUNK)
                else:
                    scale_diagonal(2)
                    take_pre_scale(1)
                if kind == "conv":
                    conv_taps(k)
                for job in JOBS[i]:
                    mixer_job(*job)

            split_low(n0 + W_TILES + 1, s0 + W_TILES + 1, CHUNK)

            n0, s0, t0, p0 = phase("wout")
            with dve.Fori(0, KD // 4 - 1) as i:
                for u in range(4):
                    result_tile(i * 4 + (t0 + u), p0 + u, i * 4 + (KD + u))
                    split_low(i * 4 + (n0 + u + 2), s0 + u + 2, CHUNK)
            for d in range(KD - 4, KD):
                result_tile(t0 + d, p0 + d, KD + d)
                if d < KD - 1:
                    split_low(n0 + d + 2, s0 + d + 2, CHUNK)
            update(1)
            ffn(1, "gate2", "down2")
            post_norm(2)
            for g in range(X_GROUPS):
                scale_y(2, g)
            for g in range(4):
                dve.wait_ge(out_turned, 2 * g + 1)
                dve.tensor_copy(out_nat[:, 0, g * 512:(g + 1) * 512],
                                end_banks[(2 * g) % 4][:]).then_inc(out_copied, 1)

        @block.gpsimd
        def _(pool):
            pool.memset(params_nat[:], 0.0).then_inc(params_cleared, 1)
            pool.memset(ones[:], 1.0).then_inc(consts_ready, 1)
            pool.memset(ident[:], 0.0).then_inc(consts_ready, 1)
            pool.wait_ge(consts_ready, 2)
            pool.affine_select(out=ident[:], in_=ident[:], pattern=[[-1, P]], compare_op=ALU.not_equal,
                               fill=1.0, base=0, channel_multiplier=1).then_inc(consts_ready, 1)

            def sum_squares(b):
                pool.wait_ge(squares_ready, b * KD + 1)
                pool.tensor_copy(square_sum, squares).then_inc(square_sum_ready, 1)
                with pool.Fori(1, KD - 1) as d:
                    pool.wait_ge(squares_ready, d + (b * KD + 1))
                    pool.wait_ge(square_sum_ready, d + b * (KD - 1))
                    pool.tensor_tensor(square_sum, square_sum, squares, ALU.add).then_inc(square_sum_ready, 1)

            def add_residual(b):
                for g in range(X_GROUPS):
                    pool.wait_ge(y_scaled, X_GROUPS * b + g + 1)
                    xs = x[:, x_tiles(g), :]
                    pool.tensor_tensor(xs, xs, y[:, x_tiles(g), :], ALU.add).then_inc(x_ready, 1)

            def last_squares(p):
                pool.wait_ge(x_ready, X_GROUPS * (p + 1))
                xs = x[:, x_tiles(X_GROUPS - 1), :]
                pool.tensor_tensor(x_squares[:, x_tiles(X_GROUPS - 1), :], xs, xs,
                                   ALU.mult).then_inc(last_squares_ready, 1)

            last_squares(0)
            sum_squares(0)
            add_residual(0)
            last_squares(1)

            n0, s0, t0, p0 = phase("proj")
            pool.wait_ge(row_sums, 3)
            pool.memset(conv_in[:, :, 0:PAD], 0.0).then_inc(masks_ready, 1)
            pool.memset(causal[:], 1.0).then_inc(masks_ready, 1)
            pool.wait_ge(masks_ready, 2)
            pool.affine_select(out=causal[:], in_=causal[:], pattern=[[1, P]], compare_op=ALU.is_ge,
                               fill=0.0, base=0, channel_multiplier=-1).then_inc(masks_ready, 1)
            pool.wait_ge(mixer_loaded, 6 * 16)
            pool.affine_select(out=w_rows[:], in_=w_rows[:], pattern=[[0, A_HEADS], [-1, P]],
                               compare_op=ALU.is_ge, fill=0.0, base=0,
                               channel_multiplier=1).then_inc(w_masked, 1)
            pool.wait_ge(pre_scale_ready, 2)

            def gate_y(q):
                pool.wait_ge(z_ready, q + 1)
                pool.wait_ge(ssm_read, q + 1)
                pool.tensor_tensor(x_conv[:, q, :], x_conv[:, q, :], z_gate[:, q % 2, :],
                                   ALU.mult).then_inc(y_gated, 1)
                pool.wait_ge(y_gated, q + 1)
                pool.tensor_tensor(y_square[:], x_conv[:, q, :], x_conv[:, q, :],
                                   ALU.mult).then_inc(y_square_ready, 1)
                pool.wait_ge(y_square_ready, q + 1)
                total_of = y_sum[:, q // GROUP_PAIRS, :]
                if q % GROUP_PAIRS == 0:
                    pool.tensor_copy(total_of, y_square[:]).then_inc(y_sum_ready, 1)
                else:
                    pool.tensor_tensor(total_of, total_of, y_square[:], ALU.add).then_inc(y_sum_ready, 1)
                pool.wait_ge(y_sum_ready, q + 1)

            def square_v(k):
                pool.wait_ge(v_act_ready, k + 1)
                pool.tensor_tensor(v_square[:], v_act[:, k % 2, :], v_act[:, k % 2, :],
                                   ALU.mult).then_inc(v_square_ready, 1)
                pool.wait_ge(v_square_ready, k + 1)
                if k == 0:
                    pool.tensor_copy(v_sum[:], v_square[:]).then_inc(v_sum_ready, 1)
                else:
                    pool.tensor_tensor(v_sum[:], v_sum[:], v_square[:], ALU.add).then_inc(v_sum_ready, 1)
                pool.wait_ge(v_sum_ready, k + 1)

            ACTIVATED = {"v": v_act_ready, "z": z_ready, "u": u_ready}
            for i, (kind, k, _) in enumerate(PROJ):
                if i == W_TILES - 1:
                    break
                pool.wait_ge(acc_read, t0 + i + 1)
                if kind == "conv":
                    at_least(pool, conv_step, PAD * (k - 1))
                    to = conv_in[:, k % 2, PAD:PAD + T]
                else:
                    if i >= 2 and PROJ[i - 2][0] in ACTIVATED:
                        pool.wait_ge(ACTIVATED[PROJ[i - 2][0]], PROJ[i - 2][1] + 1)
                    to = proj[:, i % 2, :]
                pool.tensor_tensor(to, gate_up[:, i % 2, :], pre_scale[:], ALU.mult).then_inc(proj_ready, 1)
                before, kb, _ = PROJ[i - 1]
                if i >= 1 and before == "z":
                    gate_y(kb)
                if i >= 1 and before == "v":
                    square_v(kb)
                for job, q in JOBS[i]:
                    if job == "diag":
                        pool.wait_ge(sum_read, SUMS.index(("decay_sum", 0)) + 1)
                        at_least(pool, decay_spread, q)
                        shape = [P, 2, TT, P]
                        pool.tensor_tensor(diag[:], spread(ident[:], shape, 1, 1),
                                           spread(decay_sum[:, 2 * q:2 * q + 2, :], shape, 3),
                                           ALU.mult).then_inc(diag_ready, 1)
                        pool.wait_ge(turn_read, TURNS.index(("x_rows", q)) + 1)
                        for t in range(TT):
                            rows = x_rows[:, t, q * P:(q + 1) * P].rearrange("p (e d) -> p e d", e=2)
                            pool.tensor_tensor(rows, rows, spread(dt[:, 2 * q:2 * q + 2, t], [P, 2, 64], 2),
                                               ALU.mult).then_inc(x_dt_ready, 1)

            sum_squares(1)
            add_residual(1)
            last_squares(2)
            sum_squares(2)
            add_residual(2)

        @block.tensor
        def _(pe):
            def chunk(n, s, blocks, moving, k0, bank, start, stop, order=None, wait_for=None,
                      between=None):
                order = order or list(range(blocks))
                pe.wait_ge(high_ready, n + 1)
                for b in order:
                    if wait_for is not None:
                        wait_for(k0 + b)
                    last = pe.matmul(bank, high[:, s % 2, b, :], moving[:, k0 + b, :],
                                     start=start and b == order[0], stop=False)
                last.then_inc(high_used, 1)
                if between is not None:
                    between()
                pe.wait_ge(low_ready, n + 1)
                for b in order:
                    last = pe.matmul(bank[:, 0:T], low[:, s % 2, b, :], moving[:, k0 + b, 0:T],
                                     start=False, stop=stop and b == order[-1])
                last.then_inc(low_used, 1)

            def first_chunks(n, s, p, banks):
                pe.wait_ge(high_ready, n + 2)
                pe.wait_ge(low_ready, n + 2)
                for k in range(KD):
                    pe.wait_ge(xg_ready, KD * p + k + 1)
                    ends = k == KD - 1
                    for c in range(2):
                        last = pe.matmul(banks[c], high[:, (s + c) % 2, k, :], xg[:, k, :],
                                         start=(k == 0), stop=False)
                        if ends:
                            last.then_inc(high_used, 1)
                    for c in range(2):
                        last = pe.matmul(banks[c][:, 0:T], low[:, (s + c) % 2, k, :], xg[:, k, 0:T],
                                         start=False, stop=ends)
                        if ends:
                            last.then_inc(low_used, 1)

            def token_sums(sources):
                for t in range(TT):
                    for source in sources:
                        last = pe.matmul(bank_sum[:, t:t + 1], source[:, t * P:(t + 1) * P], ones[:, 0:1],
                                         start=source is sources[0], stop=source is sources[-1])
                last.then_inc(row_sums, 1)

            def spread_scale(m):
                pe.wait_ge(diag_made, m + 1)
                pe.matmul(bank_spread[:, 0:T], ones[:], scale_diag[:].rearrange("p t l -> p (t l)"),
                          start=True, stop=True).then_inc(scale_spread, 1)

            def post_norm(b):
                pe.wait_ge(square_sum_ready, (KD - 1) * (b + 1))
                pe.wait_ge(variance_ready, 2 * b + 1)
                if b == 1:
                    pe.wait_ge(sum_read, len(SUMS))
                pe.wait_ge(squares_ready, KD * (b + 1))
                token_sums([square_sum, squares])
                spread_scale(2 * b + 1)

            def pre_sums(p):
                pe.wait_ge(x_square_sum_ready, 3 * (p + 1))
                at_least(pe, variance_ready, 2 * p)
                token_sums([x_squares[:, k, :] for k in range(4)])

            def hidden_tile(n, s, t, parity, norm=None):
                at_least(pe, acc_read, t - 1)
                bank = acc[parity % 2]
                chunk(n, s, KD, xg, 0, bank[:, 0, :], True, True,
                      between=None if norm is None else lambda: pre_sums(norm))
                if norm is not None:
                    spread_scale(2 * norm)
                chunk(n + 1, s + 1, KD, xg, 0, bank[:, 1, :], True, True)

            def ffn(which, gate_phase, down_phase):
                n0, s0, t0, p0 = phase(gate_phase)
                p = PRE[gate_phase]
                at_least(pe, acc_read, t0 - 1)
                first_chunks(n0, s0, p, [acc[p0][:, 0, :], acc[p0][:, 1, :]])
                hidden_tile(n0 + 2, s0 + 2, t0 + 1, p0 + 1, norm=p)
                hidden_tile(n0 + 4, s0 + 4, t0 + 2, p0 + 2)
                with pe.Fori(1, PAIR_ROUNDS) as i:
                    for u in (1, 2):
                        hidden_tile(i * 4 + (n0 + 2 * u), s0 + 2 * u, i * 2 + (t0 + u), p0 + u)
                for j in REST:
                    hidden_tile(n0 + 2 * j, s0 + 2 * j, t0 + j, p0 + j)
                n0, s0, t0, p0 = phase(down_phase)

                def tile(n, t, parity):
                    at_least(pe, acc_read, t - 1)
                    for c in range(4):
                        pe.wait_ge(h_ready, which * KF + DOWN_AT[c] + DOWN[c])
                        chunk(n + c, s0 + c, DOWN[c], h, DOWN_AT[c], acc[parity % 2][:, 0, :],
                              c == 0, c == 3)

                with pe.Fori(0, KD // 2) as i:
                    for u in range(2):
                        tile(i * 8 + (n0 + 4 * u), i * 2 + (t0 + u), p0 + u)
                post_norm(2 * which)

            def transpose(to, source):
                return pe.transpose(to, source, ident[:])

            pe.wait_ge(consts_ready, 3)
            pe.wait_ge(params_loaded, 16 * (len(PARAM_ROWS) + 1))
            for r in range(2):
                last = transpose(bank_sum[:, r * P:(r + 1) * P], params_nat[:, r, :])
            last.then_inc(params_turned, 1)
            for g in range(X_GROUPS):
                if g % 2 == 0:
                    pe.wait_ge(x_loaded[g // 2], 16)
                if g == 3:
                    pe.wait_ge(params_ready, 1)
                at_least(pe, x_ready, g - 3)
                for k in range(GROUP):
                    for t in range(TT):
                        last = transpose(end_banks[g % 4][:, k * T + t * P:k * T + (t + 1) * P],
                                         x_nat[:, t, (GROUP * g + k) * P:(GROUP * g + k + 1) * P])
                last.then_inc(x_turned, 1)
            ffn(0, "gate1", "down1")

            def turn_begins(job):
                n = TURNS.index(job)
                at_least(pe, turn_read, n)

            def sum_begins(job):
                n = SUMS.index(job)
                if n == 0:
                    pe.wait_ge(variance_ready, 3)
                else:
                    pe.wait_ge(sum_read, n)

            def mixer_job(kind, k):
                job = (kind, k)
                if kind in ("dt_rows", "x_rows", "v_rows"):
                    turn_begins(job)
                    if kind == "dt_rows":
                        pe.wait_ge(proj_ready, 1)
                        source = proj[:, 0, :]
                    elif kind == "x_rows":
                        pe.wait_ge(conv_act_ready, k + 1)
                        source = x_conv[:, k, :]
                    else:
                        pe.wait_ge(v_gain_ready, k + 1)
                        source = v_gain[:, k % 2, :]
                    for t in range(TT):
                        last = transpose(bank_turn[:, t * P:(t + 1) * P], source[:, t * P:(t + 1) * P])
                    last.then_inc(turned, 1)
                elif kind == "spatial_w":
                    turn_begins(job)
                    pe.wait_ge(w_masked, 1)
                    for a in range(4):
                        last = transpose(bank_turn[:, a * P:(a + 1) * P], w_rows[:, 4 * k + a, :])
                    last.then_inc(turned, 1)
                elif kind == "decay_sum":
                    sum_begins(job)
                    pe.wait_ge(da_ready, 1)
                    pe.wait_ge(masks_ready, 3)
                    H = SSM_HEADS
                    pe.matmul(bank_sum[:, 0:H], causal[:], dt_a[:, :, 0], start=True, stop=True)
                    pe.matmul(bank_sum[:, H:2 * H], ones[:], dt_a[:, :, 0], start=True, stop=False)
                    pe.matmul(bank_sum[:, H:2 * H], causal[:], dt_a[:, :, 1], start=False,
                              stop=True).then_inc(summed, 1)
                elif kind == "scores":
                    sum_begins(job)
                    pe.wait_ge(conv_act_ready, CONV_TILES)
                    pe.matmul(bank_sum[:, 0:T], b_state[:, k, 0:P], c_state[:, k, :], start=True, stop=True)
                    pe.matmul(bank_sum[:, T:T + P], b_state[:, k, P:T], c_state[:, k, P:T], start=True,
                              stop=True).then_inc(summed, 1)
                elif kind == "decay":
                    pe.wait_ge(diag_ready, k + 1)
                    at_least(pe, decay_clamped, k)
                    pe.matmul(bank_decay[:], ones[:], diag[:].rearrange("p e t l -> p (e t l)"),
                              start=True, stop=True).then_inc(decay_spread, 1)
                elif kind == "mix":
                    decay = decay_group[k // GROUP_PAIRS][:, k % GROUP_PAIRS]
                    pe.wait_ge(decay_ready, k + 1)
                    pe.wait_ge(x_dt_ready, TT * (k + 1))
                    at_least(pe, ssm_read, k)
                    for e in range(2):
                        rows, head = slice(64 * e, 64 * e + 64), slice(k * P + 64 * e, k * P + 64 * e + 64)
                        pe.matmul(bank_mix[rows, 0:T], x_rows[:, 0, head], decay[:, e, 0:T], start=True,
                                  stop=False)
                        last = pe.matmul(bank_mix[rows, P:T], x_rows[:, 1, head], decay[:, e, T:T + P],
                                         start=False, stop=True)
                    last.then_inc(ssm_out, 1)
                elif kind == "v_norm":
                    sum_begins(job)
                    pe.wait_ge(v_sum_ready, A_HEADS)
                    for t in range(TT):
                        last = pe.matmul(bank_sum[:, t:t + 1], v_sum[:, t * P:(t + 1) * P], ones[:, 0:1],
                                         start=True, stop=True)
                    last.then_inc(summed, 1)
                elif kind == "group_norm":
                    sum_begins(job)
                    pe.wait_ge(y_sum_ready, GROUP_PAIRS * (k + 1))
                    pe.matmul(bank_sum[:, 0:T], ones[:], y_sum[:, k, :], start=True,
                              stop=True).then_inc(summed, 1)
                elif kind == "gating":
                    pe.wait_ge(v_rows_ready, TT)
                    if k == 0:
                        pe.wait_ge(decay_clamped, PAIRS)
                    else:
                        pe.wait_ge(gate_read, k)
                    for c in range(TT):
                        last = pe.matmul(bank_gate[:, c * P:(c + 1) * P], v_rows[:, c, k * P:(k + 1) * P],
                                         w_cols[:, k, :], start=True, stop=True)
                    last.then_inc(gate_summed, 1)

            n0, s0, t0, p0 = phase("proj")
            pe.wait_ge(acc_read, t0)
            def bank_of(i):
                accumulator, bank = proj_acc(i)
                return acc[accumulator][:, bank, :]

            first_chunks(n0, s0, 1, [bank_of(0), bank_of(1)])
            for i in range(W_TILES):
                if i > 1:
                    pe.wait_ge(acc_read, t0 + i - 3)
                    chunk(n0 + i, s0 + i, KD, xg, 0, bank_of(i), True, True,
                          between=(lambda: pre_sums(1)) if i == 2 else None)
                    if i == 2:
                        spread_scale(2)
                for job in JOBS[i]:
                    mixer_job(*job)

            n0, s0, t0, p0 = phase("wout")
            order = list(range(A_HEADS, KD)) + list(range(A_HEADS))

            def mixed_ready(k):
                if k == order[0]:
                    pe.wait_ge(yb_ready, GROUPS)
                if k == 0:
                    pe.wait_ge(ya_ready, A_HEADS - 1)
                if k == A_HEADS - 1:
                    pe.wait_ge(ya_ready, A_HEADS)

            with pe.Fori(0, KD // 4) as i:
                for u in range(4):
                    at_least(pe, acc_read, i * 4 + (t0 + u - 1))
                    chunk(i * 4 + (n0 + u), s0 + u, KD, mixed, 0, acc[(p0 + u) % 2][:, 0, :], True, True,
                          order=order, wait_for=mixed_ready)
            post_norm(1)
            ffn(1, "gate2", "down2")
            for g in range(4):
                pe.wait_ge(x_ready, 3 * X_GROUPS + 2 * (g + 1))
                for t in range(TT):
                    n = 2 * g + t
                    if n == 2:
                        pe.wait_ge(y_scaled, 3 * X_GROUPS)
                    if n == 3:
                        pe.wait_ge(variance_ready, 6)
                    if n >= 4:
                        pe.wait_ge((out_copied, out_copied_act)[t], g - 1)
                    for k in range(4):
                        last = transpose(end_banks[n % 4][:, k * P:(k + 1) * P],
                                         x[:, 4 * g + k, t * P:(t + 1) * P])
                    last.then_inc(out_turned, 1)


_INS = ["x", "ffn1_norm_pre", "ffn1_norm_post", "ffn1_w_gate", "ffn1_w_up", "ffn1_w_down",
        "mix_norm_pre", "mix_norm_post", "w_in", "sgu_norm", "w_spatial", "b_spatial", "conv_w",
        "conv_b", "dt_bias", "a_log", "d_skip", "ssm_norm", "w_out", "ffn2_norm_pre",
        "ffn2_norm_post", "ffn2_w_gate", "ffn2_w_up", "ffn2_w_down"]


def kernel(**inputs):
    import numpy as np
    import concourse.bacc as bacc
    from concourse.bass_utils import run_bass_kernel_spmd

    nc = bacc.Bacc("TRN2", target_bir_lowering=False, num_devices=1, dynamic_dma_scratch_size=1024)
    arrays, args = {}, []
    for name in _INS:
        a = np.ascontiguousarray(inputs[name])
        arrays[f"in_{name}"] = a
        args.append(nc.dram_tensor(f"in_{name}", a.shape, mybir.dt.from_np(a.dtype), kind="ExternalInput").ap())
    shape = inputs["x"].shape
    out = nc.dram_tensor("out_x", shape, F32, kind="ExternalOutput").ap()
    hybrid_block(nc, *args, out)
    result = run_bass_kernel_spmd(nc, [arrays], core_ids=[0])
    return result.results[0]["out_x"]
```

```python
import concourse.bass as bass
from concourse import mybir
from contextlib import ExitStack

F32 = mybir.dt.float32
F32R = mybir.dt.float32r
ACT = mybir.ActivationFunctionType
ALU = mybir.AluOpType

P = 128
EPS = 1e-6
RAW_SLOTS = 4
CHUNK = 16


def hybrid_block(nc, x_in, f1_pre, f1_post, f1_gate, f1_up, f1_down, mix_pre, mix_post, w_in,
                 sgu_norm, w_spatial, b_spatial, conv_w, conv_b, dt_bias, a_log, d_skip, ssm_norm,
                 w_out, f2_pre, f2_post, f2_gate, f2_up, f2_down, out):
    T, D = x_in.shape[1], x_in.shape[2]
    TT = T // P
    KD = D // P
    KF = f1_gate.shape[2] // P
    A_HEADS = w_spatial.shape[1]
    A_WIDTH = A_HEADS * P
    SSM_HEADS = dt_bias.shape[1]
    PAIRS = SSM_HEADS // 2
    B_WIDTH = PAIRS * P
    CONV_TILES = conv_b.shape[1] // P
    TAPS = conv_w.shape[1]
    PAD = TAPS - 1
    GROUPS = (CONV_TILES - PAIRS) // 2
    GROUP_PAIRS = PAIRS // GROUPS
    COL_U, COL_V, COL_Z = 0, A_WIDTH, 2 * A_WIDTH
    COL_CONV = COL_Z + B_WIDTH
    DT_ROW = P - SSM_HEADS
    COL_DT_WINDOW = w_in.shape[2] - P
    assert (T, D, TT, KD, A_HEADS, PAIRS, CONV_TILES, GROUPS) == (256, 2048, 2, 16, 8, 8, 12, 2)

    DOWN = [KF // 4 + (1 if c < KF % 4 else 0) for c in range(4)]
    DOWN_AT = [sum(DOWN[:c]) for c in range(4)]

    W_TILES = 1 + CONV_TILES + A_HEADS + PAIRS + A_HEADS
    n, t, first = 0, 0, {}
    for name, tiles, chunks in (("gate1", KF, 2 * KF), ("down1", KD, 4 * KD), ("proj", W_TILES, W_TILES),
                                ("wout", KD, KD), ("gate2", KF, 2 * KF), ("down2", KD, 4 * KD)):
        first[name] = (n, t)
        n, t = n + chunks, t + tiles
    CHUNKS = n

    def blocks_of(n):
        for name in ("down1", "down2"):
            if 0 <= n - first[name][0] < 4 * KD:
                return DOWN[(n - first[name][0]) % 4]
        return CHUNK

    PROJ = [("dt", 0, COL_DT_WINDOW)]
    PROJ += [("conv", c, COL_CONV + c * P) for c in range(CONV_TILES)]
    PROJ += [("v", h, COL_V + h * P) for h in range(A_HEADS)]
    PROJ += [("z", q, COL_Z + q * P) for q in range(PAIRS)]
    PROJ += [("u", h, COL_U + h * P) for h in range(A_HEADS)]
    AT = {(kind, index): i for i, (kind, index, _) in enumerate(PROJ)}

    JOBS = {i: [] for i in range(W_TILES)}
    JOBS[3] += [("dt_rows", 0)]
    JOBS[4] += [("dt_plus_one", 0)]
    JOBS[5] += [("dt_log", 0)]
    JOBS[6] += [("dt", 0)]
    JOBS[8] += [("decay_sum", 0)]
    for c in range(PAIRS):
        JOBS[AT["conv", c] + 5] += [("x_rows", c)]
    V_NORM_AT = AT["v", A_HEADS - 1] + 2
    for h in range(A_HEADS):
        JOBS[AT["v", h] + 1] += [("v_rows", h)]
        JOBS[AT["u", h]] += [("gate_sum", h)]
        JOBS[min(AT["u", h] + 1, W_TILES - 1)] += [("gating", h)]
        if h % 2 == 1:
            JOBS[V_NORM_AT + h // 2] += [("spatial_w", h // 2)]
    for step in range(3):
        JOBS[V_NORM_AT + step] += [(("v_norm", "v_root", "v_scale")[step], 0)]
    SCORES_AT = AT["conv", CONV_TILES - 1] + 2
    for g in range(GROUPS):
        JOBS[SCORES_AT + g] += [("scores", g)]
        for step in range(3):
            JOBS[AT["z", (g + 1) * GROUP_PAIRS - 1] + 2 + step] += [
                (("group_norm", "group_root", "group_low")[step], g)]
    for q in range(PAIRS):
        diag_at = 8 + 3 * (q // 2) + q % 2
        JOBS[diag_at] += [("diag", q)]
        JOBS[diag_at + 2] += [("decay", q)]
        if q % 2 == 1:
            JOBS[diag_at + 3] += [("decay_exp", q // 2)]
        JOBS[SCORES_AT + 2 + q] += [("masked", q)]
        JOBS[SCORES_AT + 4 + q] += [("mix", q)]
    JOB_ORDER = [job for i in range(W_TILES) for job in JOBS[i]]
    TURNS = [j for j in JOB_ORDER if j[0] in ("dt_rows", "spatial_w", "x_rows", "v_rows")]
    SUMS = [j for j in JOB_ORDER if j[0] in ("decay_sum", "scores", "v_norm", "group_norm")]

    PARAM_ROWS = [("f1_pre", f1_pre), ("f1_post", f1_post), ("mix_pre", mix_pre), ("mix_post", mix_post),
                  ("f2_pre", f2_pre), ("f2_post", f2_post), ("sgu", sgu_norm), ("ssm", ssm_norm),
                  ("conv_b", conv_b)]
    col, column = 0, {}
    for name, vector in PARAM_ROWS:
        column[name] = col
        col += vector.shape[1] // P
    FIRST_ROWS = col
    column["conv_w"] = col
    PARAMS = col + TAPS * CONV_TILES
    assert FIRST_ROWS <= P and TAPS * CONV_TILES <= P

    ctx = ExitStack()
    with ctx:
        at = [(nc.sbuf_base + 31) // 32 * 32]

        def place(name, shape, dtype=F32, offset=None):
            size = 4
            for s in shape[1:]:
                size *= s
            if offset is None:
                offset = at[0]
                at[0] += (size + 31) // 32 * 32
            return nc.alloc_sbuf_tensor_at(name, shape, dtype, offset=offset)

        raw = place("raw", [P, RAW_SLOTS, CHUNK, P])
        high = place("high", [P, 2, CHUNK, P], F32R)
        low = place("low", [P, 2, CHUNK, P], F32R)
        x = place("x", [P, KD, T])
        xg = place("xg", [P, KD, 2 * T], F32R)
        y_at = at[0]
        y = place("y", [P, KD, T])
        low_half = place("low_half", [P, 2, T])
        gate_up = place("gate_up", [P, 2, T])
        total = place("total", [P, T])
        pre_scale = place("pre_scale", [P, T])
        ident = place("ident", [P, P])
        table_scratch = place("table_scratch", [P, 1])
        ones = place("ones", [P, P])
        params = place("params", [P, PARAMS])
        h_at = at[0]
        h = place("h", [P, KF, 2 * T], F32R)
        h_end = at[0]
        square_sum = gate_up[:, 0, :]
        squares = gate_up[:, 1, :]

        at[0] = h_at
        mixed = place("mixed", [P, KD, 2 * T], F32R)
        mixed_end = at[0]
        TILE = 2 * T * 4
        at[0] = h_at
        token_inverse = place("token_inverse", [P, TT])
        token_scale = place("token_scale", [P, TT])
        scale_diag = place("scale_diag", [P, TT, P])
        at[0] = h_at + 6 * TILE
        x_squares = place("x_squares", [P, KD, T])
        w_rows = place("w_rows", [P, A_HEADS, P])
        assert at[0] <= mixed_end
        decay_group = [place("decay_group0", [P, GROUP_PAIRS, 2, T + P], offset=h_at + 8 * TILE),
                       place("decay_group1", [P, GROUP_PAIRS, 2, T + P], offset=h_at)]
        at[0] = mixed_end
        causal = place("causal", [P, P])
        x_rows = place("x_rows", [P, TT, B_WIDTH])
        w_cols = place("w_cols", [P, A_HEADS, P])
        b_rows = place("b_rows", [P, A_HEADS, P])
        scores = place("scores", [P, GROUPS, T + P])
        diag = place("diag", [P, 2, 2, TT, P])
        conv_in = place("conv_in", [P, 2, T + 8])
        conv = place("conv", [P, T])
        b_state = place("b_state", [P, GROUPS, T])
        c_state = place("c_state", [P, GROUPS, T])
        proj = place("proj", [P, 2, T])
        z_gate = place("z_gate", [P, 2, T])
        v_act = place("v_act", [P, 2, T])
        v_square = place("v_square", [P, T])
        v_gain = place("v_gain", [P, 2, T])
        u_act = place("u_act", [P, 2, T])
        v_sum = place("v_sum", [P, T])
        y_square = place("y_square", [P, T])
        y_sum = place("y_sum", [P, GROUPS, T])
        group_var = place("group_var", [P, T])
        group_scale = place("group_scale", [P, T])
        gate = place("gate", [P, 2, T])
        gated = place("gated", [P, T])
        HT = [P, SSM_HEADS, TT]
        dt_bias_rows = place("dt_bias_rows", [P, SSM_HEADS])
        a_rows = place("a_rows", [P, SSM_HEADS])
        skip = place("skip", [P, PAIRS])
        dt_raw, dt_abs, dt_exp, dt_one, dt_log, dt_den, dt_zero, dt, dt_a, decay_sum = (
            place(name, HT) for name in ("dt_raw", "dt_abs", "dt_exp", "dt_one", "dt_log", "dt_den",
                                         "dt_zero", "dt", "dt_a", "decay_sum"))
        v_var = place("v_var", [P, TT])
        v_scale = place("v_scale", [P, TT])
        assert at[0] <= h_end, (at[0], h_end)
        x_conv = place("x_conv", [P, PAIRS, T], offset=y_at)
        v_rows = place("v_rows", [P, TT, A_WIDTH], offset=y_at + 4 * PAIRS * T)
        at[0] = mixed_end
        x_nat = place("x_nat", [P, TT, D])
        out_nat = place("out_nat", [P, TT, D])
        params_nat = place("params_nat", [P, 2, P])
        assert at[0] <= h_end

        def psum(name, shape):
            return ctx.enter_context(nc.psum_tensor(name, shape, F32))

        acc = [psum("acc0", [P, 2, 512]), psum("acc1", [P, 2, 512])]
        bank_turn = psum("bank_turn", [P, 512])
        bank_decay = psum("bank_decay", [P, 512])
        bank_mix = psum("bank_mix", [P, 512])
        bank_sum = psum("bank_sum", [P, 512])
        bank_spread = bank_mix
        bank_gate = bank_decay
        end_banks = [bank_turn, bank_decay, bank_mix, bank_sum]

        def sem(name):
            return ctx.enter_context(nc.semaphore(name))

        raw_loaded = [sem(f"raw_loaded{s}") for s in range(RAW_SLOTS)]
        high_ready, low_ready, high_used, low_used = (
            sem(s) for s in ("high_ready", "low_ready", "high_used", "low_used"))
        low_half_ready, acc_read = sem("low_half_ready"), sem("acc_read")
        scaled_ready, silu_ready, product_ready, h_high_ready, h_ready = (
            sem(s) for s in ("scaled_ready", "silu_ready", "product_ready", "h_high_ready", "h_ready"))
        squares_ready, square_sum_ready = sem("squares_ready"), sem("square_sum_ready")
        row_sums, variance_ready, inverse_ready, root_ready, diag_made, scale_spread = (
            sem(s) for s in ("row_sums", "variance_ready", "inverse_ready", "root_ready", "diag_made",
                             "scale_spread"))
        pre_scale_ready = sem("pre_scale_ready")
        y_ready, y_scaled, x_ready = sem("y_ready"), sem("y_scaled"), sem("x_ready")
        xg_high_ready, xg_ready = sem("xg_high_ready"), sem("xg_ready")
        x_squares_ready, pool_squares_ready, x_square_sum_ready = (
            sem(s) for s in ("x_squares_ready", "pool_squares_ready", "x_square_sum_ready"))
        x_copied_dve, x_copied_act = sem("x_copied_dve"), sem("x_copied_act")
        x_loaded = [sem(f"x_loaded{q}") for q in range(4)]
        consts_ready, first_params_loaded, params_loaded, params_turned, params_ready = (
            sem(s) for s in ("consts_ready", "first_params_loaded", "params_loaded",
                             "params_turned", "params_ready"))
        table_loaded = sem("table_loaded")
        x_turned, out_turned, out_copied, out_copied_act, stored = (
            sem(s) for s in ("x_turned", "out_turned", "out_copied", "out_copied_act", "stored"))
        mixer_loaded, masks_ready, w_masked = sem("mixer_loaded"), sem("masks_ready"), sem("w_masked")
        proj_ready, conv_started, conv_step, conv_act_ready = (
            sem(s) for s in ("proj_ready", "conv_started", "conv_step", "conv_act_ready"))
        turned, turn_read = sem("turned"), sem("turn_read")
        summed, sum_read = sem("summed"), sem("sum_read")
        gate_summed, gate_read, last_u_ready = sem("gate_summed"), sem("gate_read"), sem("last_u_ready")
        dt_step_dve, dt_step_act, dt_ready, da_ready = (
            sem(s) for s in ("dt_step_dve", "dt_step_act", "dt_ready", "da_ready"))
        diag_ready, decay_spread, decay_clamped, decay_exp, decay_ready, x_dt_ready = (
            sem(s) for s in ("diag_ready", "decay_spread", "decay_clamped", "decay_exp", "decay_ready",
                             "x_dt_ready"))
        ssm_out, ssm_read, z_ready, y_gated, y_square_ready, y_sum_ready = (
            sem(s) for s in ("ssm_out", "ssm_read", "z_ready", "y_gated", "y_square_ready", "y_sum_ready"))
        group_step, group_inverse, group_scale_ready, yb_normed, yb_high_ready, yb_ready = (
            sem(s) for s in ("group_step", "group_inverse", "group_scale_ready", "yb_normed",
                             "yb_high_ready", "yb_ready"))
        v_act_ready, v_square_ready, v_gain_ready, v_sum_ready = (
            sem(s) for s in ("v_act_ready", "v_square_ready", "v_gain_ready", "v_sum_ready"))
        v_step, v_inverse, v_scale_ready, v_rows_ready = (
            sem(s) for s in ("v_step", "v_inverse", "v_scale_ready", "v_rows_ready"))
        u_ready, ya_step, ya_raw_ready, ya_high_ready, ya_ready = (
            sem(s) for s in ("u_ready", "ya_step", "ya_raw_ready", "ya_high_ready", "ya_ready"))

        block = ctx.enter_context(nc.Block())

        def at_least(eng, s, value):
            if not (isinstance(value, int) and value <= 0):
                eng.wait_ge(s, value)

        def f32(ap):
            return ap.bitcast(F32)

        def spread(ap, shape, *axes):
            for a in axes:
                ap = ap.unsqueeze(a)
            return ap.to_broadcast(shape)

        def proj_acc(i):
            following = phase("wout")[3]
            return [(1 - following, 0), (following, 1), (following, 0)][(W_TILES - 1 - i) % 3]

        def turn_bank(job):
            spare = acc[1 - phase("wout")[3]][:, 1, :]
            return (bank_turn, spare)[TURNS.index(job) % 2][:, 0:2 * P]

        def param(name, index):
            c = column[name] + index
            return params[:, c:c + 1]

        def phase(name):
            n0, t0 = first[name]
            return n0, n0 % RAW_SLOTS, t0, t0 % 2

        PRE = {"gate1": 0, "proj": 1, "gate2": 2}
        FFNS = [("gate1", "down1", f1_gate, f1_up, f1_down), ("gate2", "down2", f2_gate, f2_up, f2_down)]
        POST = [("down1", "f1_post", 0.25), ("wout", "mix_post", 1.0), ("down2", "f2_post", 0.25)]
        GAIN = ["f1_pre", "mix_pre", "f2_pre"]
        PAIR_ROUNDS = (KF - 2) // 2
        REST = list(range(1 + 2 * PAIR_ROUNDS, KF))
        GROUP = 2
        X_STEPS = ([(0, 1), (1, 2)] + [(k, k + GROUP) for k in range(2, KD - 2, GROUP)]
                   + [(KD - 2, KD - 1), (KD - 1, KD)])
        X_GROUPS = len(X_STEPS)
        IN_GROUPS = KD // GROUP

        def x_tiles(g):
            return slice(*X_STEPS[g])

        def in_tiles(g):
            return slice(GROUP * g, GROUP * (g + 1))

        def steps_within(k):
            return sum(1 for _, end in X_STEPS if end <= k)

        @block.sync
        def _(sp):
            def load(n, s, source, blocks):
                s %= RAW_SLOTS
                at_least(sp, low_ready, n - (RAW_SLOTS - 1))
                sp.dma_start(raw[:, s, 0:blocks, :], source).then_inc(raw_loaded[s], 16)

            def rows(w):
                return w[0].rearrange("(k p) f -> p k f", p=P)

            def gate_up_tile(n, s, gate, up, j):
                load(n, s, rows(gate)[:, :, bass.ds(j * P, P)], KD)
                load(n + 1, s + 1, rows(up)[:, :, bass.ds(j * P, P)], KD)

            def ffn(gate_phase, down_phase, gate, up, down, loaded=0):
                n0, s0, _, _ = phase(gate_phase)
                for j in range(loaded, 3):
                    gate_up_tile(n0 + 2 * j, s0 + 2 * j, gate, up, j)
                with sp.Fori(1, PAIR_ROUNDS) as i:
                    for u in (1, 2):
                        gate_up_tile(i * 4 + (n0 + 2 * u), s0 + 2 * u, gate, up, i * 2 + u)
                for j in REST:
                    gate_up_tile(n0 + 2 * j, s0 + 2 * j, gate, up, j)
                n0, s0, _, _ = phase(down_phase)
                with sp.Fori(0, KD) as d:
                    for c in range(4):
                        load(d * 4 + (n0 + c), s0 + c,
                             rows(down)[:, DOWN_AT[c]:DOWN_AT[c] + DOWN[c], bass.ds(d * P, P)], DOWN[c])

            for q in range(4):
                cols = slice(q * (D // 4), (q + 1) * (D // 4))
                sp.dma_start(x_nat[:, :, cols], x_in[0].rearrange("(t p) d -> p t d", p=P)[:, :, cols]
                             ).then_inc(x_loaded[q], 16)
            n0, s0, _, _ = phase("gate1")
            for u in range(2):
                gate_up_tile(n0 + 2 * u, s0 + 2 * u, f1_gate, f1_up, u)
            for name, vector in PARAM_ROWS[1:]:
                c, count = column[name], vector.shape[1] // P
                sp.dma_start(params_nat[c:c + count, 0, :],
                             vector[0].rearrange("(j p) -> j p", p=P)).then_inc(params_loaded, 16)
            sp.dma_start(params_nat[0:TAPS * CONV_TILES, 1, :],
                         conv_w[0].rearrange("k (j p) -> (k j) p", p=P)).then_inc(params_loaded, 16)
            ffn(*FFNS[0], loaded=2)
            n0, s0, _, _ = phase("proj")
            for i, (_, _, c) in enumerate(PROJ):
                load(n0 + i, s0 + i, rows(w_in)[:, :, c:c + P], KD)
            n0, s0, _, _ = phase("wout")
            with sp.Fori(0, KD // 4) as i:
                for u in range(4):
                    load(i * 4 + (n0 + u), s0 + u, rows(w_out)[:, :, bass.ds(i * (4 * P) + u * P, P)], KD)
            ffn(*FFNS[1])
            out_rows = out[0].rearrange("(t p) d -> p t d", p=P)
            for g in range(4):
                cols = slice(g * 4 * P, (g + 1) * 4 * P)
                sp.wait_ge(out_copied, g + 1)
                sp.dma_start(out_rows[:, 0, cols], out_nat[:, 0, cols]).then_inc(stored, 16)
                sp.wait_ge(out_copied_act, g + 1)
                sp.dma_start(out_rows[:, 1, cols], out_nat[:, 1, cols]).then_inc(stored, 16)
            sp.wait_ge(stored, 8 * 16)

        @block.scalar
        def _(act):
            def split_high(n, s, blocks):
                s %= RAW_SLOTS
                act.wait_ge(raw_loaded[s], n * 4 + (16 - 4 * s))
                at_least(act, high_used, n - 1)
                at_least(act, low_ready, n - 1)
                act.activation(high[:, s % 2, 0:blocks, :], raw[:, s, 0:blocks, :],
                               ACT.Copy).then_inc(high_ready, 1)

            def take_low_half(n_end, t, parity, banks, first_bank=0):
                act.wait_ge(low_used, n_end + 1)
                at_least(act, acc_read, t)
                act.activation(low_half[:, 0:banks, :],
                               acc[parity % 2][:, first_bank:first_bank + banks, T:2 * T],
                               ACT.Copy).then_inc(low_half_ready, 1)

            def hidden_tile(n, s, t, parity, j, f, blocks, norm=None):
                split_high(n + 2, s + 2, blocks[0])
                take_low_half(n + 1, t, parity, 2)
                split_high(n + 3, s + 3, blocks[1])
                if norm is not None:
                    root(2 * norm, 1.0)
                act.wait_ge(scaled_ready, f + 1)
                act.activation(gate_up[:, 0, :], gate_up[:, 0, :], ACT.Silu).then_inc(silu_ready, 1)
                act.wait_ge(product_ready, f + 1)
                act.activation(h[:, bass.ds(j, 1), 0:T], total[:].unsqueeze(1),
                               ACT.Copy).then_inc(h_high_ready, 1)

            def result_tile(n_end, t, parity, d, r, gain, split, norm=None):
                if norm is not None:
                    b, scale = norm
                    act.activation(table_scratch[:], ones[:, 0:1], ACT.Sqrt).then_inc(table_loaded, 1)
                    act.wait_ge(table_loaded, b + 2)
                    if split is not None:
                        split_high(*split)
                take_low_half(n_end, t, parity, 1)
                if norm is None and split is not None:
                    split_high(*split)
                act.wait_ge(acc_read, t + 1)
                at_least(act, square_sum_ready, r)
                act.activation(squares, total[:], ACT.Square).then_inc(squares_ready, 1)
                if norm is not None:
                    root(2 * b + 1, scale)
                act.activation(y[:, bass.ds(d, 1), :], total[:].unsqueeze(1), ACT.Copy,
                               scale=gain(d)).then_inc(y_ready, 1)

            def root(m, scale):
                act.wait_ge(inverse_ready, m + 1)
                act.activation(token_scale[:], token_inverse[:], ACT.Sqrt, scale=scale).then_inc(root_ready, 1)

            def x_high(p, tiles):
                for k in range(tiles.start, tiles.stop):
                    act.activation(xg[:, k, 0:T], x[:, k, :], ACT.Copy,
                                   scale=param(GAIN[p], k)).then_inc(xg_high_ready, 1)

            def pre_norm(p):
                for g in range(X_GROUPS):
                    act.wait_ge(x_ready, X_GROUPS * (p - 1) + g + 1)
                    x_high(p, x_tiles(g))
                    if g > 0:
                        act.activation(x_squares[:, x_tiles(g - 1), :], x[:, x_tiles(g - 1), :],
                                       ACT.Square).then_inc(x_squares_ready, 1)

            def take_input():
                act.wait_ge(params_ready, 1)
                for g in range(0, IN_GROUPS, 2):
                    act.wait_ge(x_turned, g + 2)
                    act.activation(x[:, in_tiles(g + 1), :],
                                   end_banks[(g + 1) % 4][:].rearrange("p (k t) -> p k t", k=GROUP),
                                   ACT.Copy).then_inc(x_copied_act, 1)
                    act.wait_ge(x_copied_dve, g // 2 + 1)
                    x_high(0, in_tiles(g))
                    act.wait_ge(x_copied_act, g // 2 + 1)
                    x_high(0, in_tiles(g + 1))
                    if g >= IN_GROUPS - 4:
                        c = (g - (IN_GROUPS - 4)) // 2
                        split_high(c, c, CHUNK)

            def ffn(which, gate_phase, down_phase, post_name):
                n0, s0, t0, p0 = phase(gate_phase)
                p = PRE[gate_phase]
                if p == 0:
                    take_input()
                else:
                    pre_norm(p)
                hidden_tile(n0, s0, t0, p0, 0, which * KF, [CHUNK, CHUNK], norm=p)
                with act.Fori(0, PAIR_ROUNDS) as i:
                    for u in (1, 2):
                        hidden_tile(i * 4 + (n0 + 2 * u), s0 + 2 * u, i * 2 + (t0 + u), p0 + u,
                                    i * 2 + u, i * 2 + (which * KF + u), [CHUNK, CHUNK])
                for j in REST:
                    hidden_tile(n0 + 2 * j, s0 + 2 * j, t0 + j, p0 + j, j, which * KF + j,
                                [CHUNK, CHUNK] if j < KF - 1 else DOWN[0:2])
                down(which, down_phase, post_name)

            def down(which, down_phase, post_name):
                n0, s0, t0, p0 = phase(down_phase)
                b = 2 * which
                r0 = b * (KD - 1)

                def tile(n, s, t, parity, d, r, gain, after, norm=None):
                    split_high(n + 2, s + 2, DOWN[2])
                    split_high(n + 3, s + 3, DOWN[3])
                    if after is not None:
                        split_high(n + 4, s + 4, after[0])
                    result_tile(n + 3, t, parity, d, r, gain,
                                None if after is None else (n + 5, s + 5, after[1]), norm)

                def gain_at(d):
                    c = column[post_name]
                    return params[:, bass.ds(d + c, 1)]

                with act.Fori(0, KD // 2 - 1) as i:
                    for u in range(2):
                        tile(i * 8 + (n0 + 4 * u), s0, i * 2 + (t0 + u), p0 + u, i * 2 + u,
                             i * 2 + (r0 + u), gain_at, DOWN[0:2])
                for d in (KD - 2, KD - 1):
                    after = DOWN[0:2] if d < KD - 1 else None if which == 1 else [CHUNK, CHUNK]
                    tile(n0 + 4 * d, s0, t0 + d, p0 + d, d, r0 + d, gain_at, after,
                         (b, POST[b][2]) if d == KD - 1 else None)

            act.dma_start(params_nat[0:KD, 0, :], f1_pre[0].rearrange("(j p) -> j p", p=P)
                          ).then_inc(first_params_loaded, 16)
            act.wait_ge(consts_ready, 1)
            act.activation(table_scratch[:], ones[:, 0:1], ACT.Silu).then_inc(table_loaded, 1)
            act.wait_ge(table_loaded, 1)
            ffn(0, "gate1", "down1", "f1_post")

            pre_norm(1)
            n0, s0, t0, p0 = phase("proj")
            act.dma_start(w_rows[:], w_spatial[0].rearrange("h t s -> t h s")).then_inc(mixer_loaded, 16)
            act.dma_start(b_rows[:].rearrange("p h t -> p (h t)"),
                          b_spatial.rearrange("l h t -> l (h t)").to_broadcast([P, A_HEADS * P])
                          ).then_inc(mixer_loaded, 16)
            act.dma_start(dt_bias_rows[:], dt_bias.to_broadcast([P, SSM_HEADS])).then_inc(mixer_loaded, 16)
            act.dma_start(a_rows[:], a_log.to_broadcast([P, SSM_HEADS])).then_inc(mixer_loaded, 16)
            for e in range(2):
                act.dma_start(skip[64 * e:64 * e + 64, :],
                              d_skip[0:1, e:SSM_HEADS:2].to_broadcast([64, PAIRS]),
                              allow_slow_non_contiguous=True).then_inc(mixer_loaded, 16)

            def activate(i):
                kind, k, _ = PROJ[i]
                if kind == "dt":
                    return
                if i < W_TILES - 1:
                    act.wait_ge(proj_ready, i + 1)
                else:
                    act.wait_ge(last_u_ready, 1)
                if kind == "conv":
                    at_least(act, conv_act_ready, k)
                    act.activation(conv[:], conv_in[:, k % 2, 0:T], ACT.Identity,
                                   scale=param("conv_w", k), bias=param("conv_b", k)
                                   ).then_inc(conv_started, 1)
                elif kind == "z":
                    at_least(act, y_gated, k - 1)
                    act.activation(z_gate[:, k % 2, :], proj[:, i % 2, :], ACT.Silu).then_inc(z_ready, 1)
                elif kind == "v":
                    at_least(act, v_square_ready, k - 1)
                    act.activation(v_act[:, k % 2, :], proj[:, i % 2, :], ACT.Gelu).then_inc(v_act_ready, 1)
                    act.wait_ge(v_act_ready, k + 1)
                    if k >= 2:
                        act.wait_ge(turned, TURNS.index(("v_rows", k - 2)) + 1)
                    act.activation(v_gain[:, k % 2, :], v_act[:, k % 2, :], ACT.Copy,
                                   scale=param("sgu", k)).then_inc(v_gain_ready, 1)
                elif kind == "u":
                    at_least(act, ya_raw_ready, k - 1)
                    act.activation(u_act[:, k % 2, :], proj[:, i % 2, :], ACT.Gelu).then_inc(u_ready, 1)

            def conv_silu(c):
                act.wait_ge(conv_step, PAD * (c + 1))
                to = (x_conv[:, c, :] if c < PAIRS else b_state[:, c - PAIRS, :]
                      if c < PAIRS + GROUPS else c_state[:, c - PAIRS - GROUPS, :])
                act.activation(to, conv[:], ACT.Silu).then_inc(conv_act_ready, 1)

            def mixer_job(kind, k):
                if kind == "dt_rows":
                    act.wait_ge(turn_read, TURNS.index((kind, k)) + 1)
                    act.activation(dt_abs[:], dt_raw[:], ACT.Abs).then_inc(dt_step_act, 1)
                    act.wait_ge(dt_step_act, 1)
                    act.activation(dt_exp[:], dt_abs[:], ACT.Exp, scale=-1.0).then_inc(dt_step_act, 1)
                    act.wait_ge(mixer_loaded, 6 * 16)
                    act.activation(a_rows[:], a_rows[:], ACT.Exp).then_inc(dt_step_act, 1)
                elif kind == "dt_log":
                    act.wait_ge(dt_step_dve, 1)
                    act.activation(dt_log[:], dt_one[:], ACT.Ln).then_inc(dt_step_act, 1)
                elif kind in ("x_rows", "v_rows", "spatial_w"):
                    act.wait_ge(turned, TURNS.index((kind, k)) + 1)
                    to = (x_rows[:, :, k * P:(k + 1) * P] if kind == "x_rows" else
                          v_rows[:, :, k * P:(k + 1) * P] if kind == "v_rows" else
                          w_cols[:, 2 * k:2 * k + 2, :])
                    act.activation(to, turn_bank((kind, k)).rearrange("p (t d) -> p t d", t=2),
                                   ACT.Copy).then_inc(turn_read, 1)
                elif kind == "decay_exp":
                    act.wait_ge(decay_clamped, 2 * k + 2)
                    pairs = decay_group[2 * k // GROUP_PAIRS]
                    q = 2 * k % GROUP_PAIRS
                    act.activation(pairs[:, q:q + 2], pairs[:, q:q + 2], ACT.Exp).then_inc(decay_exp, 1)
                elif kind == "v_root":
                    act.wait_ge(v_inverse, 1)
                    act.activation(v_scale[:], v_var[:], ACT.Sqrt).then_inc(v_scale_ready, 1)
                elif kind == "group_root":
                    act.wait_ge(group_inverse, k + 1)
                    act.activation(group_scale[:], group_var[:], ACT.Sqrt).then_inc(group_scale_ready, 1)
                elif kind == "group_low":
                    act.wait_ge(yb_normed, GROUP_PAIRS * (k + 1))
                    qs = slice(k * GROUP_PAIRS, (k + 1) * GROUP_PAIRS)
                    act.activation(mixed[:, PAIRS + k * GROUP_PAIRS:PAIRS + (k + 1) * GROUP_PAIRS, 0:T],
                                   x_conv[:, qs, :], ACT.Copy).then_inc(yb_high_ready, 1)
                elif kind == "gating":
                    act.wait_ge(ya_raw_ready, k + 1)
                    act.activation(mixed[:, k, 0:T], gated[:], ACT.Copy).then_inc(ya_high_ready, 1)

            for i in range(W_TILES):
                split_high(n0 + i + 2, s0 + i + 2, CHUNK)
                accumulator, bank = proj_acc(i)
                take_low_half(n0 + i, t0 + i, accumulator, 1, bank)
                if i >= 1 and PROJ[i - 1][0] == "conv":
                    conv_silu(PROJ[i - 1][1])
                if i == 0:
                    root(2, 1.0)
                activate(i)
                for job in JOBS[i]:
                    mixer_job(*job)
            n0, s0, t0, p0 = phase("wout")
            c = column["mix_post"]

            def out_tile(n, s, t, parity, d, r, norm=None):
                result_tile(n, t, parity, d, r, lambda d: params[:, bass.ds(d + c, 1)],
                            (n + 2, s + 2, CHUNK), norm)

            with act.Fori(0, KD // 4 - 1) as i:
                for u in range(4):
                    out_tile(i * 4 + (n0 + u), s0 + u, i * 4 + (t0 + u), p0 + u, i * 4 + u,
                             i * 4 + (KD - 1 + u))
            for d in range(KD - 4, KD):
                out_tile(n0 + d, s0 + d, t0 + d, p0 + d, d, KD - 1 + d,
                         (1, POST[1][2]) if d == KD - 1 else None)
            ffn(1, "gate2", "down2", "f2_post")
            for g in range(4):
                act.wait_ge(out_turned, 2 * g + 2)
                act.activation(out_nat[:, 1, g * 512:(g + 1) * 512], end_banks[(2 * g + 1) % 4][:],
                               ACT.Copy).then_inc(out_copied_act, 1)

        @block.vector
        def _(dve):
            def split_low(n, s, blocks):
                s %= RAW_SLOTS
                dve.wait_ge(high_ready, n + 1)
                at_least(dve, low_used, n - 1)
                dve.tensor_tensor(low[:, s % 2, 0:blocks, :], raw[:, s, 0:blocks, :],
                                  f32(high[:, s % 2, 0:blocks, :]), ALU.subtract).then_inc(low_ready, 1)

            def hidden_tile(n, s, t, parity, j, f, blocks, norm=None):
                split_low(n + 2, s + 2, blocks[0])
                dve.wait_ge(low_half_ready, t + 1)
                dve.tensor_tensor(gate_up[:], acc[parity % 2][:, :, 0:T], low_half[:],
                                  ALU.add).then_inc(acc_read, 1)
                if norm is not None:
                    scale_diagonal(2 * norm)
                    split_low(n + 3, s + 3, blocks[1])
                    take_pre_scale(norm)
                dve.wait_ge(acc_read, t + 1)
                dve.tensor_tensor(gate_up[:], gate_up[:], spread(pre_scale[:], [P, 2, T], 1),
                                  ALU.mult).then_inc(scaled_ready, 1)
                if norm is None:
                    split_low(n + 3, s + 3, blocks[1])
                dve.wait_ge(silu_ready, f + 1)
                dve.tensor_tensor(total[:], gate_up[:, 0, :], gate_up[:, 1, :],
                                  ALU.mult).then_inc(product_ready, 1)
                dve.wait_ge(h_high_ready, f + 1)
                dve.tensor_tensor(h[:, bass.ds(j, 1), T:2 * T], total[:].unsqueeze(1),
                                  f32(h[:, bass.ds(j, 1), 0:T]), ALU.subtract).then_inc(h_ready, 1)

            def result_tile(t, parity, r):
                dve.wait_ge(low_half_ready, t + 1)
                at_least(dve, squares_ready, r)
                dve.tensor_tensor(total[:], acc[parity % 2][:, 0, 0:T], low_half[:, 0, :],
                                  ALU.add).then_inc(acc_read, 1)

            def scale_diagonal(m):
                dve.wait_ge(row_sums, m + 1)
                dve.tensor_scalar(token_inverse[:], bank_sum[:, 0:TT], 1.0 / D, EPS, ALU.mult,
                                  ALU.add).then_inc(variance_ready, 1)
                dve.wait_ge(variance_ready, m + 1)
                dve.reciprocal(token_inverse[:], token_inverse[:]).then_inc(inverse_ready, 1)
                dve.wait_ge(root_ready, m + 1)
                for t in range(TT):
                    last = dve.tensor_scalar(scale_diag[:, t, :], ident[:], token_scale[:, t:t + 1], None,
                                             ALU.mult)
                last.then_inc(diag_made, 1)

            def take_pre_scale(p):
                dve.wait_ge(scale_spread, 2 * p + 1)
                dve.tensor_copy(pre_scale[:], bank_spread[:, 0:T]).then_inc(pre_scale_ready, 1)
                dve.wait_ge(pre_scale_ready, p + 1)

            def scale_y(b, g):
                ys = y[:, x_tiles(g), :]
                dve.tensor_tensor(ys, ys, spread(bank_spread[:, 0:T], [P, ys.shape[1], T], 1),
                                  ALU.mult).then_inc(y_scaled, 1)

            def post_norm(b):
                scale_diagonal(2 * b + 1)
                dve.wait_ge(scale_spread, 2 * b + 2)
                dve.wait_ge(y_ready, KD * (b + 1))

            def x_low(p, tiles):
                for k in range(tiles.start, tiles.stop):
                    dve.wait_ge(xg_high_ready, KD * p + k + 1)
                    dve.scalar_tensor_tensor(xg[:, k, T:2 * T], x[:, k, :], param(GAIN[p], k),
                                             f32(xg[:, k, 0:T]), ALU.mult,
                                             ALU.subtract).then_inc(xg_ready, 1)

            def add_squares(p):
                for c in range(1, 4):
                    if p == 0:
                        dve.wait_ge(pool_squares_ready, 2 * c + 2)
                    elif c < 3:
                        dve.wait_ge(x_squares_ready, (X_GROUPS - 1) * (p - 1) + steps_within(4 * c + 4))
                    else:
                        dve.wait_ge(x_squares_ready, (X_GROUPS - 1) * p)
                        dve.wait_ge(pool_squares_ready, IN_GROUPS + p)
                    if c > 1:
                        dve.wait_ge(x_square_sum_ready, 3 * p + c - 1)
                    dve.tensor_tensor(x_squares[:, 0:4, :], x_squares[:, 0:4, :],
                                      x_squares[:, 4 * c:4 * c + 4, :], ALU.add
                                      ).then_inc(x_square_sum_ready, 1)

            AHEAD = 3

            def update(b):
                post_norm(b)
                for g in range(AHEAD):
                    scale_y(b, g)
                for g in range(X_GROUPS):
                    x_low(b + 1, x_tiles(g))
                    if g + AHEAD < X_GROUPS:
                        scale_y(b, g + AHEAD)
                add_squares(b + 1)

            def ffn(which, gate_phase, down_phase):
                n0, s0, t0, p0 = phase(gate_phase)
                hidden_tile(n0, s0, t0, p0, 0, which * KF, [CHUNK, CHUNK], norm=PRE[gate_phase])
                with dve.Fori(0, PAIR_ROUNDS) as i:
                    for u in (1, 2):
                        hidden_tile(i * 4 + (n0 + 2 * u), s0 + 2 * u, i * 2 + (t0 + u), p0 + u,
                                    i * 2 + u, i * 2 + (which * KF + u), [CHUNK, CHUNK])
                for j in REST:
                    hidden_tile(n0 + 2 * j, s0 + 2 * j, t0 + j, p0 + j, j, which * KF + j,
                                [CHUNK, CHUNK] if j < KF - 1 else DOWN[0:2])
                n0, s0, t0, p0 = phase(down_phase)
                r0 = 2 * which * KD

                def tile(n, s, t, parity, r, after, last=False):
                    split_low(n + 2, s + 2, DOWN[2])
                    split_low(n + 3, s + 3, DOWN[3])
                    if after is not None:
                        split_low(n + 4, s + 4, after[0])
                    result_tile(t, parity, r)
                    if after is not None and not last:
                        split_low(n + 5, s + 5, after[1])

                with dve.Fori(0, KD // 2 - 1) as i:
                    for u in range(2):
                        tile(i * 8 + (n0 + 4 * u), s0, i * 2 + (t0 + u), p0 + u, i * 2 + (r0 + u),
                             DOWN[0:2])
                for d in (KD - 2, KD - 1):
                    after = DOWN[0:2] if d < KD - 1 else None if which == 1 else [CHUNK, CHUNK]
                    tile(n0 + 4 * d, s0, t0 + d, p0 + d, r0 + d, after, d == KD - 1)

            dve.wait_ge(params_turned, 1)
            dve.tensor_copy(params[:, 0:KD], acc[1][:, 0, 0:KD]).then_inc(params_ready, 1)
            dve.wait_ge(params_ready, 1)
            def take_input(g):
                dve.wait_ge(x_turned, g + 1)
                dve.tensor_copy(x[:, in_tiles(g), :],
                                end_banks[g % 4][:].rearrange("p (k t) -> p k t", k=GROUP)
                                ).then_inc(x_copied_dve, 1)

            take_input(0)
            for g in range(IN_GROUPS):
                if g % 2 == 0 and g + 2 < IN_GROUPS:
                    take_input(g + 2)
                dve.wait_ge((x_copied_dve, x_copied_act)[g % 2], g // 2 + 1)
                x_low(0, in_tiles(g))
            split_low(0, 0, CHUNK)
            split_low(1, 1, CHUNK)
            dve.wait_ge(params_turned, 2)
            dve.tensor_copy(params[:, KD:FIRST_ROWS], acc[1][:, 0, KD:FIRST_ROWS])
            dve.tensor_copy(params[:, FIRST_ROWS:PARAMS],
                            acc[1][:, 0, P:P + PARAMS - FIRST_ROWS]).then_inc(params_ready, 1)
            add_squares(0)
            ffn(0, "gate1", "down1")
            update(0)

            n0, s0, t0, p0 = phase("proj")

            def conv_taps(c):
                dve.wait_ge(conv_started, c + 1)
                for k in range(1, TAPS):
                    at_least(dve, conv_step, PAD * c + k - 1)
                    dve.scalar_tensor_tensor(conv[:], conv_in[:, c % 2, k:k + T],
                                             param("conv_w", k * CONV_TILES + c), conv[:], ALU.mult,
                                             ALU.add).then_inc(conv_step, 1)

            dt_steps = [0]

            def dt_chain(instruction):
                dt_steps[0] += 1
                instruction.then_inc(dt_step_dve, 1)
                dve.wait_ge(dt_step_dve, dt_steps[0])

            def mixer_job(kind, k):
                if kind == "dt_rows":
                    dve.wait_ge(turned, TURNS.index((kind, k)) + 1)
                    dve.wait_ge(mixer_loaded, 6 * 16)
                    dve.tensor_tensor(
                        dt_raw[:],
                        turn_bank((kind, k)).rearrange("p (t d) -> p d t", t=TT)[:, DT_ROW:P, :],
                        spread(dt_bias_rows[:], HT, 2), ALU.add).then_inc(turn_read, 1)
                elif kind == "dt_plus_one":
                    dve.wait_ge(dt_step_act, 2)
                    dt_chain(dve.tensor_scalar(dt_one[:], dt_exp[:], 1.0, None, ALU.add))
                    dt_chain(dve.tensor_scalar(dt_den[:], dt_one[:], -1.0, None, ALU.add))
                    dt_chain(dve.tensor_scalar(dt_zero[:], dt_den[:], 0.0, None, ALU.is_equal))
                    dt_chain(dve.tensor_tensor(dt_den[:], dt_den[:], dt_zero[:], ALU.add))
                    dt_chain(dve.reciprocal(dt_den[:], dt_den[:]))
                elif kind == "dt":
                    dve.wait_ge(dt_step_act, 4)
                    dt_chain(dve.tensor_tensor(dt_log[:], dt_log[:], dt_den[:], ALU.mult))
                    dt_chain(dve.tensor_tensor(dt_log[:], dt_log[:], dt_zero[:], ALU.add))
                    dt_chain(dve.tensor_tensor(dt_log[:], dt_log[:], dt_exp[:], ALU.mult))
                    dve.scalar_tensor_tensor(dt[:], dt_raw[:], 0.0, dt_log[:], ALU.max,
                                             ALU.add).then_inc(dt_ready, 1)
                    dve.wait_ge(dt_ready, 1)
                    dve.scalar_tensor_tensor(dt_a[:], dt[:], -1.0, spread(a_rows[:], HT, 2), ALU.mult,
                                             ALU.mult).then_inc(da_ready, 1)
                elif kind == "decay_sum":
                    dve.wait_ge(summed, SUMS.index((kind, k)) + 1)
                    sums = bank_sum[:, 0:TT * SSM_HEADS].rearrange("p (t h) -> p h t", t=TT)
                    dve.tensor_copy(decay_sum[:], sums).then_inc(sum_read, 1)
                elif kind == "scores":
                    dve.wait_ge(summed, SUMS.index((kind, k)) + 1)
                    dve.tensor_tensor(scores[:, k, 0:P], bank_sum[:, 0:P], causal[:], ALU.mult)
                    dve.tensor_copy(scores[:, k, P:T], bank_sum[:, P:T])
                    dve.tensor_tensor(scores[:, k, T:T + P], bank_sum[:, T:T + P], causal[:],
                                      ALU.mult).then_inc(sum_read, 1)
                elif kind == "decay":
                    dve.wait_ge(decay_spread, k + 1)
                    decay = decay_group[k // GROUP_PAIRS][:, k % GROUP_PAIRS]
                    for e in range(2):
                        for t, to, source in ((0, slice(0, T), slice(e * T, (e + 1) * T)),
                                              (1, slice(T, T + P), slice(e * T + P, (e + 1) * T))):
                            last = dve.tensor_scalar(decay[:, e, to], bank_decay[:, source],
                                                     decay_sum[:, 2 * k + e, t:t + 1], 0.0,
                                                     ALU.subtract, ALU.min)
                    last.then_inc(decay_clamped, 1)
                elif kind == "masked":
                    decay = decay_group[k // GROUP_PAIRS][:, k % GROUP_PAIRS]
                    dve.wait_ge(decay_exp, k // 2 + 1)
                    dve.tensor_tensor(decay, decay,
                                      spread(scores[:, k // GROUP_PAIRS, :], [P, 2, T + P], 1),
                                      ALU.mult).then_inc(decay_ready, 1)
                elif kind == "mix":
                    dve.wait_ge(ssm_out, k + 1)
                    dve.scalar_tensor_tensor(x_conv[:, k, :], x_conv[:, k, :], skip[:, k:k + 1],
                                             bank_mix[:, 0:T], ALU.mult, ALU.add).then_inc(ssm_read, 1)
                elif kind == "v_norm":
                    dve.wait_ge(summed, SUMS.index((kind, k)) + 1)
                    dve.tensor_scalar(v_var[:], bank_sum[:, 0:TT], 1.0 / A_WIDTH, EPS, ALU.mult,
                                      ALU.add).then_inc(sum_read, 1)
                    dve.wait_ge(sum_read, SUMS.index((kind, k)) + 1)
                    dve.reciprocal(v_var[:], v_var[:]).then_inc(v_inverse, 1)
                elif kind == "v_scale":
                    dve.wait_ge(v_scale_ready, 1)
                    for t in range(TT):
                        dve.tensor_scalar(v_rows[:, t, :], v_rows[:, t, :], v_scale[:, t:t + 1], None,
                                          ALU.mult).then_inc(v_rows_ready, 1)
                elif kind == "group_norm":
                    dve.wait_ge(summed, SUMS.index((kind, k)) + 1)
                    dve.tensor_scalar(group_var[:], bank_sum[:, 0:T], 1.0 / (GROUP_PAIRS * P), EPS,
                                      ALU.mult, ALU.add).then_inc(sum_read, 1)
                    dve.wait_ge(sum_read, SUMS.index((kind, k)) + 1)
                    dve.reciprocal(group_var[:], group_var[:]).then_inc(group_inverse, 1)
                elif kind == "group_root":
                    dve.wait_ge(group_scale_ready, k + 1)
                    for q in range(k * GROUP_PAIRS, (k + 1) * GROUP_PAIRS):
                        dve.scalar_tensor_tensor(x_conv[:, q, :], x_conv[:, q, :], param("ssm", q),
                                                 group_scale[:], ALU.mult, ALU.mult).then_inc(yb_normed, 1)
                elif kind == "group_low":
                    dve.wait_ge(yb_high_ready, k + 1)
                    qs = slice(k * GROUP_PAIRS, (k + 1) * GROUP_PAIRS)
                    ks = slice(A_HEADS + k * GROUP_PAIRS, A_HEADS + (k + 1) * GROUP_PAIRS)
                    dve.tensor_tensor(mixed[:, ks, T:2 * T], x_conv[:, qs, :], f32(mixed[:, ks, 0:T]),
                                      ALU.subtract).then_inc(yb_ready, 1)
                elif kind == "gate_sum":
                    dve.wait_ge(gate_summed, k + 1)
                    at_least(dve, ya_raw_ready, k - 1)
                    dve.tensor_tensor(gate[:, k % 2, :].rearrange("p (c t) -> p c t", c=TT),
                                      bank_gate[:, 0:T].rearrange("p (c t) -> p c t", c=TT),
                                      spread(b_rows[:, k, :], [P, TT, P], 1), ALU.add).then_inc(gate_read, 1)
                elif kind == "gating":
                    dve.wait_ge(gate_read, k + 1)
                    dve.wait_ge(u_ready, k + 1)
                    at_least(dve, ya_ready, k)
                    dve.tensor_tensor(gated[:], gate[:, k % 2, :], u_act[:, k % 2, :],
                                      ALU.mult).then_inc(ya_raw_ready, 1)
                    dve.wait_ge(ya_high_ready, k + 1)
                    dve.tensor_tensor(mixed[:, k, T:2 * T], gated[:], f32(mixed[:, k, 0:T]),
                                      ALU.subtract).then_inc(ya_ready, 1)

            for i, (kind, k, _) in enumerate(PROJ):
                if i == 0:
                    split_low(n0 + 2, s0 + 2, CHUNK)
                dve.wait_ge(low_half_ready, t0 + i + 1)
                at_least(dve, proj_ready, i - 1)
                accumulator, bank = proj_acc(i)
                dve.tensor_tensor(gate_up[:, i % 2, :], acc[accumulator][:, bank, 0:T], low_half[:, 0, :],
                                  ALU.add).then_inc(acc_read, 1)
                if i == W_TILES - 1:
                    dve.wait_ge(acc_read, t0 + i + 1)
                    dve.wait_ge(u_ready, k - 1)
                    dve.tensor_tensor(proj[:, i % 2, :], gate_up[:, i % 2, :], pre_scale[:],
                                      ALU.mult).then_inc(last_u_ready, 1)
                elif i > 0:
                    split_low(n0 + i + 2, s0 + i + 2, CHUNK)
                else:
                    scale_diagonal(2)
                    take_pre_scale(1)
                if kind == "conv":
                    conv_taps(k)
                for job in JOBS[i]:
                    mixer_job(*job)

            split_low(n0 + W_TILES + 1, s0 + W_TILES + 1, CHUNK)

            n0, s0, t0, p0 = phase("wout")
            with dve.Fori(0, KD // 4 - 1) as i:
                for u in range(4):
                    result_tile(i * 4 + (t0 + u), p0 + u, i * 4 + (KD + u))
                    split_low(i * 4 + (n0 + u + 2), s0 + u + 2, CHUNK)
            for d in range(KD - 4, KD):
                result_tile(t0 + d, p0 + d, KD + d)
                if d < KD - 1:
                    split_low(n0 + d + 2, s0 + d + 2, CHUNK)
            update(1)
            ffn(1, "gate2", "down2")
            post_norm(2)
            for g in range(X_GROUPS):
                scale_y(2, g)
            for g in range(4):
                dve.wait_ge(out_turned, 2 * g + 1)
                dve.tensor_copy(out_nat[:, 0, g * 512:(g + 1) * 512],
                                end_banks[(2 * g) % 4][:]).then_inc(out_copied, 1)

        @block.gpsimd
        def _(pool):
            pool.memset(ones[:], 1.0).then_inc(consts_ready, 1)
            pool.memset(ident[:], 0.0).then_inc(consts_ready, 1)
            pool.wait_ge(consts_ready, 2)
            pool.affine_select(out=ident[:], in_=ident[:], pattern=[[-1, P]], compare_op=ALU.not_equal,
                               fill=1.0, base=0, channel_multiplier=1).then_inc(consts_ready, 1)

            def sum_squares(b):
                pool.wait_ge(squares_ready, b * KD + 1)
                pool.tensor_copy(square_sum, squares).then_inc(square_sum_ready, 1)
                with pool.Fori(1, KD - 1) as d:
                    pool.wait_ge(squares_ready, d + (b * KD + 1))
                    pool.wait_ge(square_sum_ready, d + b * (KD - 1))
                    pool.tensor_tensor(square_sum, square_sum, squares, ALU.add).then_inc(square_sum_ready, 1)

            def add_residual(b):
                for g in range(X_GROUPS):
                    pool.wait_ge(y_scaled, X_GROUPS * b + g + 1)
                    xs = x[:, x_tiles(g), :]
                    pool.tensor_tensor(xs, xs, y[:, x_tiles(g), :], ALU.add).then_inc(x_ready, 1)

            def squares_of(tiles):
                xs = x[:, tiles, :]
                pool.tensor_tensor(x_squares[:, tiles, :], xs, xs, ALU.mult).then_inc(pool_squares_ready, 1)

            def split_low(n, s):
                s %= RAW_SLOTS
                pool.wait_ge(low_ready, n)
                pool.wait_ge(high_ready, n + 1)
                pool.wait_ge(low_used, n - 1)
                pool.tensor_tensor(low[:, s % 2, :, :], raw[:, s, :, :], f32(high[:, s % 2, :, :]),
                                   ALU.subtract).then_inc(low_ready, 1)

            def last_squares(p):
                pool.wait_ge(x_ready, X_GROUPS * p)
                squares_of(x_tiles(X_GROUPS - 1))

            for g in range(IN_GROUPS):
                pool.wait_ge((x_copied_dve, x_copied_act)[g % 2], g // 2 + 1)
                squares_of(in_tiles(g))
            sum_squares(0)
            split_low(first["proj"][0] + 1, first["proj"][0] + 1)
            add_residual(0)
            last_squares(1)

            n0, s0, t0, p0 = phase("proj")
            pool.wait_ge(row_sums, 3)
            pool.memset(conv_in[:, :, 0:PAD], 0.0).then_inc(masks_ready, 1)
            pool.memset(causal[:], 1.0).then_inc(masks_ready, 1)
            pool.wait_ge(masks_ready, 2)
            pool.affine_select(out=causal[:], in_=causal[:], pattern=[[1, P]], compare_op=ALU.is_ge,
                               fill=0.0, base=0, channel_multiplier=-1).then_inc(masks_ready, 1)
            pool.wait_ge(mixer_loaded, 6 * 16)
            pool.affine_select(out=w_rows[:], in_=w_rows[:], pattern=[[0, A_HEADS], [-1, P]],
                               compare_op=ALU.is_ge, fill=0.0, base=0,
                               channel_multiplier=1).then_inc(w_masked, 1)
            pool.wait_ge(pre_scale_ready, 2)

            def gate_y(q):
                pool.wait_ge(z_ready, q + 1)
                pool.wait_ge(ssm_read, q + 1)
                pool.tensor_tensor(x_conv[:, q, :], x_conv[:, q, :], z_gate[:, q % 2, :],
                                   ALU.mult).then_inc(y_gated, 1)
                pool.wait_ge(y_gated, q + 1)
                pool.tensor_tensor(y_square[:], x_conv[:, q, :], x_conv[:, q, :],
                                   ALU.mult).then_inc(y_square_ready, 1)
                pool.wait_ge(y_square_ready, q + 1)
                total_of = y_sum[:, q // GROUP_PAIRS, :]
                if q % GROUP_PAIRS == 0:
                    pool.tensor_copy(total_of, y_square[:]).then_inc(y_sum_ready, 1)
                else:
                    pool.tensor_tensor(total_of, total_of, y_square[:], ALU.add).then_inc(y_sum_ready, 1)
                pool.wait_ge(y_sum_ready, q + 1)

            def square_v(k):
                pool.wait_ge(v_act_ready, k + 1)
                pool.tensor_tensor(v_square[:], v_act[:, k % 2, :], v_act[:, k % 2, :],
                                   ALU.mult).then_inc(v_square_ready, 1)
                pool.wait_ge(v_square_ready, k + 1)
                if k == 0:
                    pool.tensor_copy(v_sum[:], v_square[:]).then_inc(v_sum_ready, 1)
                else:
                    pool.tensor_tensor(v_sum[:], v_sum[:], v_square[:], ALU.add).then_inc(v_sum_ready, 1)
                pool.wait_ge(v_sum_ready, k + 1)

            ACTIVATED = {"v": v_act_ready, "z": z_ready, "u": u_ready}
            for i, (kind, k, _) in enumerate(PROJ[:-1]):
                pool.wait_ge(acc_read, t0 + i + 1)
                if kind == "conv":
                    at_least(pool, conv_step, PAD * (k - 1))
                    to = conv_in[:, k % 2, PAD:PAD + T]
                else:
                    if i >= 2 and PROJ[i - 2][0] in ACTIVATED:
                        pool.wait_ge(ACTIVATED[PROJ[i - 2][0]], PROJ[i - 2][1] + 1)
                    to = proj[:, i % 2, :]
                pool.tensor_tensor(to, gate_up[:, i % 2, :], pre_scale[:], ALU.mult).then_inc(proj_ready, 1)
                before, kb, _ = PROJ[i - 1]
                if i >= 1 and before == "z":
                    gate_y(kb)
                if i >= 1 and before == "v":
                    square_v(kb)
                for job, q in JOBS[i]:
                    if job == "diag":
                        pool.wait_ge(sum_read, SUMS.index(("decay_sum", 0)) + 1)
                        at_least(pool, decay_spread, q - 1)
                        shape = [P, 2, TT, P]
                        pool.tensor_tensor(diag[:, q % 2], spread(ident[:], shape, 1, 1),
                                           spread(decay_sum[:, 2 * q:2 * q + 2, :], shape, 3),
                                           ALU.mult).then_inc(diag_ready, 1)
                        pool.wait_ge(turn_read, TURNS.index(("x_rows", q)) + 1)
                        for t in range(TT):
                            rows = x_rows[:, t, q * P:(q + 1) * P].rearrange("p (e d) -> p e d", e=2)
                            pool.tensor_tensor(rows, rows, spread(dt[:, 2 * q:2 * q + 2, t], [P, 2, 64], 2),
                                               ALU.mult).then_inc(x_dt_ready, 1)

            sum_squares(1)
            split_low(first["gate2"][0] + 1, first["gate2"][0] + 1)
            add_residual(1)
            last_squares(2)
            sum_squares(2)
            add_residual(2)

        @block.tensor
        def _(pe):
            def chunk(n, s, blocks, moving, k0, bank, start, stop, order=None, wait_for=None,
                      between=None):
                order = order or list(range(blocks))
                pe.wait_ge(high_ready, n + 1)
                for b in order:
                    if wait_for is not None:
                        wait_for(k0 + b)
                    last = pe.matmul(bank, high[:, s % 2, b, :], moving[:, k0 + b, :],
                                     start=start and b == order[0], stop=False)
                last.then_inc(high_used, 1)
                if between is not None:
                    between()
                pe.wait_ge(low_ready, n + 1)
                for b in order:
                    last = pe.matmul(bank[:, 0:T], low[:, s % 2, b, :], moving[:, k0 + b, 0:T],
                                     start=False, stop=stop and b == order[-1])
                last.then_inc(low_used, 1)

            LAG = 5

            def first_chunks(n, s, p, banks):
                pe.wait_ge(high_ready, n + 1)
                pe.wait_ge(low_ready, n + 1)

                def block(c, k):
                    ends = k == KD - 1
                    product = pe.matmul(banks[c], high[:, (s + c) % 2, k, :], xg[:, k, :],
                                        start=(k == 0), stop=False)
                    if ends:
                        product.then_inc(high_used, 1)
                    product = pe.matmul(banks[c][:, 0:T], low[:, (s + c) % 2, k, :], xg[:, k, 0:T],
                                        start=False, stop=ends)
                    if ends:
                        product.then_inc(low_used, 1)

                for k in range(KD + LAG):
                    if k < KD:
                        pe.wait_ge(xg_ready, KD * p + k + 1)
                        block(0, k)
                    if k == LAG:
                        pe.wait_ge(high_ready, n + 2)
                        pe.wait_ge(low_ready, n + 2)
                    if k >= LAG:
                        block(1, k - LAG)

            def keep_warm(count):
                for _ in range(count):
                    pe.matmul(bank_turn[:, 0:P], ones[:], ones[:], start=True, stop=True)

            def token_sums(sources):
                for t in range(TT):
                    for source in sources:
                        last = pe.matmul(bank_sum[:, t:t + 1], source[:, t * P:(t + 1) * P], ones[:, 0:1],
                                         start=source is sources[0], stop=source is sources[-1])
                last.then_inc(row_sums, 1)

            def spread_scale(m):
                pe.wait_ge(diag_made, m + 1)
                pe.matmul(bank_spread[:, 0:T], ones[:], scale_diag[:].rearrange("p t l -> p (t l)"),
                          start=True, stop=True).then_inc(scale_spread, 1)

            def post_norm(b):
                keep_warm(8)
                pe.wait_ge(square_sum_ready, (KD - 1) * (b + 1))
                pe.wait_ge(variance_ready, 2 * b + 1)
                if b == 1:
                    pe.wait_ge(sum_read, len(SUMS))
                pe.wait_ge(squares_ready, KD * (b + 1))
                token_sums([square_sum, squares])
                keep_warm(5)
                spread_scale(2 * b + 1)
                keep_warm(9)

            def pre_sums(p):
                pe.wait_ge(x_square_sum_ready, 3 * (p + 1))
                at_least(pe, variance_ready, 2 * p)
                token_sums([x_squares[:, k, :] for k in range(4)])

            def hidden_tile(n, s, t, parity, norm=None):
                at_least(pe, acc_read, t - 1)
                bank = acc[parity % 2]
                chunk(n, s, KD, xg, 0, bank[:, 0, :], True, True,
                      between=None if norm is None else lambda: pre_sums(norm))
                if norm is not None:
                    spread_scale(2 * norm)
                chunk(n + 1, s + 1, KD, xg, 0, bank[:, 1, :], True, True)

            def ffn(which, gate_phase, down_phase):
                n0, s0, t0, p0 = phase(gate_phase)
                p = PRE[gate_phase]
                at_least(pe, acc_read, t0 - 1)
                if p == 0:
                    pe.wait_ge(x_copied_dve, 3)
                    keep_warm(10)
                    for c in range(2):
                        chunk(n0 + c, s0 + c, KD, xg, 0, acc[p0][:, c, :], True, True,
                              wait_for=lambda k: pe.wait_ge(xg_ready, k + 1))
                        if c == 0:
                            turn_other_params()
                else:
                    first_chunks(n0, s0, p, [acc[p0][:, 0, :], acc[p0][:, 1, :]])
                if p == 0:
                    pe.wait_ge(params_ready, 2)
                hidden_tile(n0 + 2, s0 + 2, t0 + 1, p0 + 1, norm=p)
                hidden_tile(n0 + 4, s0 + 4, t0 + 2, p0 + 2)
                with pe.Fori(1, PAIR_ROUNDS) as i:
                    for u in (1, 2):
                        hidden_tile(i * 4 + (n0 + 2 * u), s0 + 2 * u, i * 2 + (t0 + u), p0 + u)
                for j in REST:
                    hidden_tile(n0 + 2 * j, s0 + 2 * j, t0 + j, p0 + j)
                n0, s0, t0, p0 = phase(down_phase)

                def tile(n, t, parity):
                    at_least(pe, acc_read, t - 1)
                    for c in range(4):
                        pe.wait_ge(h_ready, which * KF + DOWN_AT[c] + DOWN[c])
                        chunk(n + c, s0 + c, DOWN[c], h, DOWN_AT[c], acc[parity % 2][:, 0, :],
                              c == 0, c == 3)

                with pe.Fori(0, KD // 2) as i:
                    for u in range(2):
                        tile(i * 8 + (n0 + 4 * u), i * 2 + (t0 + u), p0 + u)
                post_norm(2 * which)

            params_bank = acc[1][:, 0, :]

            def turn_params(source, rows, c):
                return pe.transpose(params_bank[:, c:c + rows], source[0:rows, :], ident[0:rows, 0:rows])

            def turn_other_params():
                pe.wait_ge(first_params_loaded, 16)
                pe.wait_ge(params_loaded, 16 * len(PARAM_ROWS))
                pe.wait_ge(params_ready, 1)
                turn_params(params_nat[:, 0, :], FIRST_ROWS, 0)
                turn_params(params_nat[:, 1, :], PARAMS - FIRST_ROWS, P).then_inc(params_turned, 1)

            def transpose(to, source):
                return pe.transpose(to, source, ident[:])

            pe.wait_ge(consts_ready, 3)
            pe.wait_ge(first_params_loaded, 16)
            turn_params(params_nat[:, 0, :], KD, 0).then_inc(params_turned, 1)
            for g in range(IN_GROUPS):
                if g % 2 == 0:
                    pe.wait_ge(x_loaded[g // 2], 16)
                if g >= 4:
                    pe.wait_ge((x_copied_dve, x_copied_act)[g % 2], (g - 4) // 2 + 1)
                for k in range(GROUP):
                    for t in range(TT):
                        last = transpose(end_banks[g % 4][:, k * T + t * P:k * T + (t + 1) * P],
                                         x_nat[:, t, (GROUP * g + k) * P:(GROUP * g + k + 1) * P])
                last.then_inc(x_turned, 1)
            ffn(0, "gate1", "down1")

            def turn_begins(job):
                n = TURNS.index(job)
                at_least(pe, turn_read, n - 1)
                return turn_bank(job)

            def sum_begins(job):
                n = SUMS.index(job)
                if n == 0:
                    pe.wait_ge(variance_ready, 3)
                else:
                    pe.wait_ge(sum_read, n)

            def mixer_job(kind, k):
                job = (kind, k)
                if kind in ("dt_rows", "x_rows", "v_rows"):
                    to = turn_begins(job)
                    if kind == "dt_rows":
                        pe.wait_ge(proj_ready, 1)
                        source = proj[:, 0, :]
                    elif kind == "x_rows":
                        pe.wait_ge(conv_act_ready, k + 1)
                        source = x_conv[:, k, :]
                    else:
                        pe.wait_ge(v_gain_ready, k + 1)
                        source = v_gain[:, k % 2, :]
                    for t in range(TT):
                        last = transpose(to[:, t * P:(t + 1) * P], source[:, t * P:(t + 1) * P])
                    last.then_inc(turned, 1)
                elif kind == "spatial_w":
                    to = turn_begins(job)
                    pe.wait_ge(w_masked, 1)
                    for a in range(2):
                        last = transpose(to[:, a * P:(a + 1) * P], w_rows[:, 2 * k + a, :])
                    last.then_inc(turned, 1)
                elif kind == "decay_sum":
                    sum_begins(job)
                    pe.wait_ge(da_ready, 1)
                    pe.wait_ge(masks_ready, 3)
                    H = SSM_HEADS
                    pe.matmul(bank_sum[:, 0:H], causal[:], dt_a[:, :, 0], start=True, stop=True)
                    pe.matmul(bank_sum[:, H:2 * H], ones[:], dt_a[:, :, 0], start=True, stop=False)
                    pe.matmul(bank_sum[:, H:2 * H], causal[:], dt_a[:, :, 1], start=False,
                              stop=True).then_inc(summed, 1)
                elif kind == "scores":
                    sum_begins(job)
                    pe.wait_ge(conv_act_ready, CONV_TILES)
                    pe.matmul(bank_sum[:, 0:T], b_state[:, k, 0:P], c_state[:, k, :], start=True, stop=True)
                    pe.matmul(bank_sum[:, T:T + P], b_state[:, k, P:T], c_state[:, k, P:T], start=True,
                              stop=True).then_inc(summed, 1)
                elif kind == "decay":
                    pe.wait_ge(diag_ready, k + 1)
                    at_least(pe, decay_clamped, k)
                    pe.matmul(bank_decay[:], ones[:], diag[:, k % 2].rearrange("p e t l -> p (e t l)"),
                              start=True, stop=True).then_inc(decay_spread, 1)
                elif kind == "mix":
                    decay = decay_group[k // GROUP_PAIRS][:, k % GROUP_PAIRS]
                    pe.wait_ge(decay_ready, k + 1)
                    pe.wait_ge(x_dt_ready, TT * (k + 1))
                    at_least(pe, ssm_read, k)
                    for e in range(2):
                        rows, head = slice(64 * e, 64 * e + 64), slice(k * P + 64 * e, k * P + 64 * e + 64)
                        pe.matmul(bank_mix[rows, 0:T], x_rows[:, 0, head], decay[:, e, 0:T], start=True,
                                  stop=False)
                        last = pe.matmul(bank_mix[rows, P:T], x_rows[:, 1, head], decay[:, e, T:T + P],
                                         start=False, stop=True)
                    last.then_inc(ssm_out, 1)
                elif kind == "v_norm":
                    sum_begins(job)
                    pe.wait_ge(v_sum_ready, A_HEADS)
                    for t in range(TT):
                        last = pe.matmul(bank_sum[:, t:t + 1], v_sum[:, t * P:(t + 1) * P], ones[:, 0:1],
                                         start=True, stop=True)
                    last.then_inc(summed, 1)
                elif kind == "group_norm":
                    sum_begins(job)
                    pe.wait_ge(y_sum_ready, GROUP_PAIRS * (k + 1))
                    pe.matmul(bank_sum[:, 0:T], ones[:], y_sum[:, k, :], start=True,
                              stop=True).then_inc(summed, 1)
                elif kind == "gate_sum":
                    pe.wait_ge(v_rows_ready, TT)
                    if k == 0:
                        pe.wait_ge(decay_clamped, PAIRS)
                    else:
                        pe.wait_ge(gate_read, k)
                    for c in range(TT):
                        last = pe.matmul(bank_gate[:, c * P:(c + 1) * P], v_rows[:, c, k * P:(k + 1) * P],
                                         w_cols[:, k, :], start=True, stop=True)
                    last.then_inc(gate_summed, 1)

            n0, s0, t0, p0 = phase("proj")
            pe.wait_ge(acc_read, t0)
            def bank_of(i):
                accumulator, bank = proj_acc(i)
                return acc[accumulator][:, bank, :]

            first_chunks(n0, s0, 1, [bank_of(0), bank_of(1)])
            for i in range(W_TILES):
                if i > 1:
                    pe.wait_ge(acc_read, t0 + i - 2)
                    chunk(n0 + i, s0 + i, KD, xg, 0, bank_of(i), True, True,
                          between=(lambda: pre_sums(1)) if i == 2 else None)
                    if i == 2:
                        spread_scale(2)
                for job in JOBS[i]:
                    mixer_job(*job)

            n0, s0, t0, p0 = phase("wout")
            order = list(range(A_HEADS, KD)) + list(range(A_HEADS))

            def mixed_ready(k):
                if k == order[0]:
                    pe.wait_ge(yb_ready, GROUPS)
                if k == 0:
                    pe.wait_ge(ya_ready, A_HEADS - 1)
                if k == A_HEADS - 1:
                    pe.wait_ge(ya_ready, A_HEADS)

            with pe.Fori(0, KD // 4) as i:
                for u in range(4):
                    at_least(pe, acc_read, i * 4 + (t0 + u - 1))
                    chunk(i * 4 + (n0 + u), s0 + u, KD, mixed, 0, acc[(p0 + u) % 2][:, 0, :], True, True,
                          order=order, wait_for=mixed_ready)
            post_norm(1)
            ffn(1, "gate2", "down2")
            for g in range(4):
                pe.wait_ge(x_ready, 2 * X_GROUPS + steps_within(4 * g + 4))
                for t in range(TT):
                    n = 2 * g + t
                    if n == 2:
                        pe.wait_ge(y_scaled, 3 * X_GROUPS)
                    if n == 3:
                        pe.wait_ge(variance_ready, 6)
                    if n >= 4:
                        pe.wait_ge((out_copied, out_copied_act)[t], g - 1)
                    for k in range(4):
                        last = transpose(end_banks[n % 4][:, k * P:(k + 1) * P],
                                         x[:, 4 * g + k, t * P:(t + 1) * P])
                    last.then_inc(out_turned, 1)


_INS = ["x", "ffn1_norm_pre", "ffn1_norm_post", "ffn1_w_gate", "ffn1_w_up", "ffn1_w_down",
        "mix_norm_pre", "mix_norm_post", "w_in", "sgu_norm", "w_spatial", "b_spatial", "conv_w",
        "conv_b", "dt_bias", "a_log", "d_skip", "ssm_norm", "w_out", "ffn2_norm_pre",
        "ffn2_norm_post", "ffn2_w_gate", "ffn2_w_up", "ffn2_w_down"]


def kernel(**inputs):
    import numpy as np
    import concourse.bacc as bacc
    from concourse.bass_utils import run_bass_kernel_spmd

    nc = bacc.Bacc("TRN2", target_bir_lowering=False, num_devices=1, dynamic_dma_scratch_size=1024)
    arrays, args = {}, []
    for name in _INS:
        a = np.ascontiguousarray(inputs[name])
        arrays[f"in_{name}"] = a
        args.append(nc.dram_tensor(f"in_{name}", a.shape, mybir.dt.from_np(a.dtype), kind="ExternalInput").ap())
    shape = inputs["x"].shape
    out = nc.dram_tensor("out_x", shape, F32, kind="ExternalOutput").ap()
    hybrid_block(nc, *args, out)
    result = run_bass_kernel_spmd(nc, [arrays], core_ids=[0])
    return result.results[0]["out_x"]
```
